# Optimizing a Trainium2 kernel written in Bass

```python
import jax, jax.numpy as jnp
from jax import lax
import numpy as np
import math

D_MODEL = 1024
BATCH = 1
SEQ = 512
DEPTH = 1

HEAD_DIM = 64
ATTN_GROUPS = ((128, 1), (512, 4), (2048, 16))
N_GROUPS = len(ATTN_GROUPS)
ATTN_HEADS_PER_GROUP = 4
ATTN_GROUP_WIDTH = ATTN_HEADS_PER_GROUP * HEAD_DIM
Q_BLOCK = 128
ROPE_THETA = 10000.0
RWKV_HEADS = 8
RWKV_WIDTH = RWKV_HEADS * HEAD_DIM
DECAY_LORA = 32
ICLR_LORA = 32
GATE_LORA = 96
RWKV_GN_EPS = 64e-5
D_FF = 4 * D_MODEL
PLE_DIM = 256
NORM_EPS = 1e-6

ATTN_QKV_COLS = 3 * N_GROUPS * ATTN_GROUP_WIDTH
RWKV_SPLITS = (RWKV_WIDTH, 2 * RWKV_WIDTH, 3 * RWKV_WIDTH,
               3 * RWKV_WIDTH + DECAY_LORA, 3 * RWKV_WIDTH + DECAY_LORA + ICLR_LORA)
RWKV_COLS = 3 * RWKV_WIDTH + DECAY_LORA + ICLR_LORA + GATE_LORA
GATE_COLS = 2 * D_MODEL
IN_COLS = ATTN_QKV_COLS + RWKV_COLS + GATE_COLS


def rmsnorm(x, g):
    xf = x.astype(jnp.float32)
    y = xf * lax.rsqrt(jnp.mean(xf * xf, axis=-1, keepdims=True) + NORM_EPS)
    return (y * g.astype(jnp.float32)).astype(x.dtype)

def rope(x, pos):
    half = HEAD_DIM // 2
    inv_freq = ROPE_THETA ** (-jnp.arange(0, HEAD_DIM, 2, dtype=jnp.float32) / HEAD_DIM)
    ang = pos[:, None] * inv_freq[None, :]
    ang = ang.reshape((pos.shape[0],) + (1,) * (x.ndim - 3) + (half,))
    c, s = jnp.cos(ang), jnp.sin(ang)
    xf = x.astype(jnp.float32)
    x1, x2 = xf[..., :half], xf[..., half:]
    return jnp.concatenate([x1 * c - x2 * s, x2 * c + x1 * s], axis=-1).astype(x.dtype)

def token_shift(z):
    return jnp.pad(z[:, :-1], ((0, 0), (1, 0), (0, 0)))

def dilated_attention_branch(z_attn):
    B, S, _ = z_attn.shape
    qkv = z_attn.reshape(B, S, 3, N_GROUPS, ATTN_HEADS_PER_GROUP, HEAD_DIM)
    pos = jnp.arange(S, dtype=jnp.float32)
    q = rope(qkv[:, :, 0], pos)
    k = rope(qkv[:, :, 1], pos)
    v = qkv[:, :, 2]
    qs = [q[:, :, g] for g in range(N_GROUPS)]
    ks = [k[:, :, g] for g in range(N_GROUPS)]
    vs = [v[:, :, g] for g in range(N_GROUPS)]
    scale = HEAD_DIM ** -0.5

    def block(bi):
        start = bi * Q_BLOCK
        t = start + jnp.arange(Q_BLOCK)
        outs, lses = [], []
        for g, (window, dil) in enumerate(ATTN_GROUPS):
            j = jnp.arange(window // dil + 1)
            idx = t[:, None] - dil * j[None, :]
            valid = idx >= 0
            idx_c = jnp.maximum(idx, 0)
            qb = lax.dynamic_slice_in_dim(qs[g], start, Q_BLOCK, axis=1)
            kg = jnp.take(ks[g], idx_c, axis=1)
            vg = jnp.take(vs[g], idx_c, axis=1)
            s = jnp.einsum('bqhd,bqjhd->bqhj', qb, kg, preferred_element_type=jnp.float32) * scale
            s = jnp.where(valid[None, :, None, :], s, -jnp.inf)
            m = jnp.max(s, axis=-1, keepdims=True)
            e = jnp.exp(s - m)
            den = jnp.sum(e, axis=-1)
            o = jnp.einsum('bqhj,bqjhd->bqhd', e, vg.astype(jnp.float32)) / den[..., None]
            outs.append(o)
            lses.append(m[..., 0] + jnp.log(den))
        alpha = jax.nn.softmax(jnp.stack(lses, axis=0), axis=0)
        o = alpha[0][..., None] * outs[0]
        for g in range(1, N_GROUPS):
            o = o + alpha[g][..., None] * outs[g]
        return o.astype(z_attn.dtype)

    out = lax.map(block, jnp.arange(S // Q_BLOCK))
    return out.transpose(1, 0, 2, 3, 4).reshape(B, S, ATTN_GROUP_WIDTH)

def rwkv7_time_mix(z, mu, w0, w2, a0, a2, g2, k_k, k_a, r_k, ln_w, ln_b):
    B, S, _ = z.shape
    f32 = jnp.float32
    z = z + (token_shift(z) - z) * mu
    r, k, v, xw, xa, xg = jnp.split(z, RWKV_SPLITS, axis=-1)
    logw = -jax.nn.softplus(-(w0 + jnp.tanh(xw) @ w2)) - 0.5
    decay = jnp.exp(-jnp.exp(logw.astype(f32)))
    a = jax.nn.sigmoid(a0 + xa @ a2)
    g = jax.nn.sigmoid(xg) @ g2
    heads = lambda t: t.reshape(B, S, RWKV_HEADS, HEAD_DIM).astype(f32)
    kk = heads(k * k_k)
    kk = kk / jnp.maximum(jnp.sqrt(jnp.sum(kk * kk, axis=-1, keepdims=True)), 1e-12)
    k = k * (1.0 + (a - 1.0) * k_a)
    r_h, k_h, v_h, a_h, w_h = heads(r), heads(k), heads(v), heads(a), heads(decay)
    seq = tuple(jnp.moveaxis(t, 1, 0) for t in (r_h, w_h, k_h, v_h, -kk, kk * a_h))

    def step(state, inp):
        r_t, w_t, k_t, v_t, a_t, b_t = inp
        sa = jnp.einsum('bhvk,bhk->bhv', state, a_t)
        state = (state * w_t[:, :, None, :] + sa[..., None] * b_t[:, :, None, :]
                 + v_t[..., None] * k_t[:, :, None, :])
        y = jnp.einsum('bhvk,bhk->bhv', state, r_t)
        return state, y

    state0 = jnp.zeros((B, RWKV_HEADS, HEAD_DIM, HEAD_DIM), f32)
    _, y = lax.scan(step, state0, seq)
    y = jnp.moveaxis(y, 0, 1)
    mean = jnp.mean(y, axis=-1, keepdims=True)
    var = jnp.mean(jnp.square(y - mean), axis=-1, keepdims=True)
    y = (y - mean) * lax.rsqrt(var + RWKV_GN_EPS)
    y = y.reshape(B, S, RWKV_WIDTH) * ln_w.astype(f32) + ln_b.astype(f32)
    bonus = jnp.sum(r_h * k_h * r_k.astype(f32), axis=-1, keepdims=True) * v_h
    y = (y + bonus.reshape(B, S, RWKV_WIDTH)) * g.astype(f32)
    return y.astype(z.dtype)

def first_inputs(seed: int = 0) -> dict:
    key = jax.random.key(seed)
    ks = jax.random.split(key, 32)
    f32 = jnp.float32
    nrm = lambda k, shape, scale: jax.random.normal(k, shape, f32) * scale
    gain = lambda k, n: 1.0 + 0.02 * jax.random.normal(k, (DEPTH, n), f32)
    L = DEPTH
    return {
        'x': jax.random.normal(ks[0], (BATCH, SEQ, D_MODEL), f32),
        'p': jax.random.normal(ks[1], (DEPTH, BATCH, SEQ, PLE_DIM), f32),
        'mix_pre_norm': gain(ks[2], D_MODEL),
        'w_in': nrm(ks[3], (L, D_MODEL, IN_COLS), D_MODEL ** -0.5),
        'rwkv_mu': jax.random.uniform(ks[4], (L, RWKV_COLS), f32, 0.2, 0.8),
        'rwkv_w0': jax.random.uniform(ks[5], (L, RWKV_WIDTH), f32, -4.0, 0.0),
        'rwkv_w2': nrm(ks[6], (L, DECAY_LORA, RWKV_WIDTH), 0.5 * DECAY_LORA ** -0.5),
        'rwkv_a0': nrm(ks[7], (L, RWKV_WIDTH), 0.1),
        'rwkv_a2': nrm(ks[8], (L, ICLR_LORA, RWKV_WIDTH), 0.5 * ICLR_LORA ** -0.5),
        'rwkv_g2': nrm(ks[9], (L, GATE_LORA, RWKV_WIDTH), GATE_LORA ** -0.5),
        'rwkv_k_k': 0.85 + 0.02 * jax.random.normal(ks[10], (L, RWKV_WIDTH), f32),
        'rwkv_k_a': 1.0 + 0.02 * jax.random.normal(ks[11], (L, RWKV_WIDTH), f32),
        'rwkv_r_k': nrm(ks[12], (L, RWKV_HEADS, HEAD_DIM), 0.1),
        'rwkv_ln_w': gain(ks[13], RWKV_WIDTH),
        'rwkv_ln_b': nrm(ks[14], (L, RWKV_WIDTH), 0.02),
        'w_attn_up': nrm(ks[15], (L, ATTN_GROUP_WIDTH, D_MODEL), ATTN_GROUP_WIDTH ** -0.5),
        'w_rwkv_up': nrm(ks[16], (L, RWKV_WIDTH, D_MODEL), RWKV_WIDTH ** -0.5),
        'w_out': nrm(ks[17], (L, D_MODEL, D_MODEL), D_MODEL ** -0.5),
        'mix_post_norm': gain(ks[18], D_MODEL),
        'ffn_pre_norm': gain(ks[19], D_MODEL),
        'w_ff_in': nrm(ks[20], (L, D_MODEL, D_FF), D_MODEL ** -0.5),
        'w_ff_out': nrm(ks[21], (L, D_FF, D_MODEL), D_FF ** -0.5),
        'ffn_post_norm': gain(ks[22], D_MODEL),
        'w_ple': nrm(ks[23], (L, PLE_DIM, D_MODEL), PLE_DIM ** -0.5),
        'w_ple_gate': nrm(ks[24], (L, D_MODEL, D_MODEL), D_MODEL ** -0.5),
        'ple_post_norm': gain(ks[25], D_MODEL),
    }

def first_block(x, p, mix_pre_norm, w_in, rwkv_mu, rwkv_w0, rwkv_w2, rwkv_a0, rwkv_a2, rwkv_g2,
              rwkv_k_k, rwkv_k_a, rwkv_r_k, rwkv_ln_w, rwkv_ln_b, w_attn_up, w_rwkv_up, w_out,
              mix_post_norm, ffn_pre_norm, w_ff_in, w_ff_out, ffn_post_norm, w_ple, w_ple_gate,
              ple_post_norm):
    h = x
    for i in range(DEPTH):
        u = rmsnorm(h, mix_pre_norm[i])
        z = u @ w_in[i]
        z_attn = z[..., :ATTN_QKV_COLS]
        z_rwkv = z[..., ATTN_QKV_COLS:ATTN_QKV_COLS + RWKV_COLS]
        z_gate = z[..., ATTN_QKV_COLS + RWKV_COLS:]
        o_attn = dilated_attention_branch(z_attn)
        o_rwkv = rwkv7_time_mix(z_rwkv, rwkv_mu[i], rwkv_w0[i], rwkv_w2[i], rwkv_a0[i],
                                rwkv_a2[i], rwkv_g2[i], rwkv_k_k[i], rwkv_k_a[i], rwkv_r_k[i],
                                rwkv_ln_w[i], rwkv_ln_b[i])
        gate_attn, gate_rwkv = jnp.split(jax.nn.sigmoid(z_gate), 2, axis=-1)
        merged = gate_attn * (o_attn @ w_attn_up[i]) + gate_rwkv * (o_rwkv @ w_rwkv_up[i])
        h = h + rmsnorm(merged @ w_out[i], mix_post_norm[i])
        f = rmsnorm(h, ffn_pre_norm[i])
        f = jnp.square(jax.nn.relu(f @ w_ff_in[i])) @ w_ff_out[i]
        h = h + rmsnorm(f, ffn_post_norm[i])
        e = (p[i] @ w_ple[i]) * jax.nn.sigmoid(h @ w_ple_gate[i])
        h = h + rmsnorm(e, ple_post_norm[i])
    return h


N_HEADS = 8
HEAD_DIM_2 = D_MODEL // (2 * N_HEADS)
V_DIM = 2 * HEAD_DIM_2
ATT_QK_WIDTH = N_HEADS * 2 * HEAD_DIM_2
ATT_V_WIDTH = N_HEADS * V_DIM
ROPE_DIM = HEAD_DIM_2 // 4
ROPE_THETA_2 = 500000.0
POOL_WINDOWS = (2, 4, 8, 16)
N_POOL_GROUPS = 4
POOL_GROUP_IN = 128
POOL_WIDTH = N_POOL_GROUPS * POOL_GROUP_IN
POOL_GROUP_OUT = D_MODEL // N_POOL_GROUPS
N_BRANCHES = 2
D_FF_2 = 4 * D_MODEL
IN_WIDTH = 2 * ATT_QK_WIDTH + ATT_V_WIDTH + POOL_WIDTH + N_BRANCHES * D_MODEL
RMS_EPS = 1e-6


def lambda_init(layer_idx):
    return 0.8 - 0.6 * math.exp(-0.3 * layer_idx)

def rmsnorm_2(x, g):
    xf = x.astype(jnp.float32)
    y = xf * lax.rsqrt(jnp.mean(xf * xf, axis=-1, keepdims=True) + RMS_EPS)
    return (y * g.astype(jnp.float32)).astype(x.dtype)

def rope_partial(t, cos, sin):
    half = ROPE_DIM // 2
    t1 = t[..., :half]
    t2 = t[..., half:ROPE_DIM]
    rest = t[..., ROPE_DIM:]
    return jnp.concatenate([t1 * cos - t2 * sin, t2 * cos + t1 * sin, rest], axis=-1)

def diff_attention(q, k, v, positions, lam, subln_g, lam_init):
    B, S = q.shape[0], q.shape[1]
    inv_freq = ROPE_THETA_2 ** (-jnp.arange(0, ROPE_DIM, 2, dtype=jnp.float32) / ROPE_DIM)
    ang = positions.astype(jnp.float32)[..., None] * inv_freq
    cos = jnp.cos(ang)[:, :, None, :].astype(q.dtype)
    sin = jnp.sin(ang)[:, :, None, :].astype(q.dtype)
    q = rope_partial(q.reshape(B, S, N_HEADS * 2, HEAD_DIM_2), cos, sin).reshape(B, S, N_HEADS, 2, HEAD_DIM_2)
    k = rope_partial(k.reshape(B, S, N_HEADS * 2, HEAD_DIM_2), cos, sin).reshape(B, S, N_HEADS, 2, HEAD_DIM_2)
    q = q * (HEAD_DIM_2 ** -0.5)
    outs = []
    for i in range(S // Q_BLOCK):
        q0 = i * Q_BLOCK
        kend = q0 + Q_BLOCK
        qb = q[:, q0:kend]
        kb = k[:, :kend]
        vb = v[:, :kend]
        s = jnp.einsum('bqhcd,bkhcd->bhcqk', qb, kb).astype(jnp.float32)
        mask = jnp.arange(kend)[None, :] <= (q0 + jnp.arange(Q_BLOCK))[:, None]
        s = jnp.where(mask, s, -jnp.inf)
        p = jax.nn.softmax(s, axis=-1)
        w = p[:, :, 0] - lam * p[:, :, 1]
        outs.append(jnp.einsum('bhqk,bkhd->bqhd', w.astype(v.dtype), vb))
    o = jnp.concatenate(outs, axis=1)
    o = rmsnorm_2(o, subln_g) * (1.0 - lam_init)
    return o.reshape(B, S, ATT_V_WIDTH)

def multiscale_pool(u, w_pool, pool_scale):
    B, S = u.shape[0], u.shape[1]
    uf = u.astype(jnp.float32).reshape(B, S, N_POOL_GROUPS, POOL_GROUP_IN)
    c = lax.cumsum(uf, axis=1)
    idx = jnp.arange(S)
    parts = []
    for g, w in enumerate(POOL_WINDOWS):
        cg = c[:, :, g]
        c_prev = jnp.pad(cg, ((0, 0), (w, 0), (0, 0)))[:, :S]
        cnt = jnp.minimum(idx + 1, w).astype(jnp.float32)[None, :, None]
        parts.append((cg - c_prev) / cnt - uf[:, :, g])
    d = jnp.stack(parts, axis=2).astype(u.dtype)
    y = jnp.einsum('bsgc,gcd->bsgd', d, w_pool).reshape(B, S, D_MODEL)
    return y * pool_scale

def second_inputs(seed: int = 0) -> dict:
    key = jax.random.key(seed)
    ks = jax.random.split(key, 18)
    f32 = jnp.float32
    x = jax.random.normal(ks[0], (BATCH, SEQ, D_MODEL), f32)
    offs = jax.random.randint(ks[1], (BATCH, 1), 0, 1024, dtype=jnp.int32)
    positions = (offs + jnp.arange(SEQ, dtype=jnp.int32)[None, :]).astype(jnp.int32)
    gain = lambda k, n: 1.0 + 0.02 * jax.random.normal(k, (DEPTH, n), f32)
    return {
        "x": x,
        "positions": positions,
        "norm_attn_g": gain(ks[2], D_MODEL),
        "w_in": jax.random.normal(ks[3], (DEPTH, D_MODEL, IN_WIDTH), f32) * D_MODEL ** -0.5,
        "lam_q1": 0.1 * jax.random.normal(ks[4], (DEPTH, HEAD_DIM_2), f32),
        "lam_k1": 0.1 * jax.random.normal(ks[5], (DEPTH, HEAD_DIM_2), f32),
        "lam_q2": 0.1 * jax.random.normal(ks[6], (DEPTH, HEAD_DIM_2), f32),
        "lam_k2": 0.1 * jax.random.normal(ks[7], (DEPTH, HEAD_DIM_2), f32),
        "subln_g": gain(ks[8], V_DIM),
        "w_pool": jax.random.normal(ks[9], (DEPTH, N_POOL_GROUPS, POOL_GROUP_IN, POOL_GROUP_OUT), f32) * POOL_GROUP_IN ** -0.5,
        "pool_scale": 1.0 + 0.1 * jax.random.normal(ks[10], (DEPTH, D_MODEL), f32),
        "w_out": jax.random.normal(ks[11], (DEPTH, D_MODEL, D_MODEL), f32) * D_MODEL ** -0.5,
        "norm_mlp_g": gain(ks[12], D_MODEL),
        "w_up": jax.random.normal(ks[13], (DEPTH, D_MODEL, D_FF_2), f32) * D_MODEL ** -0.5,
        "w_down": jax.random.normal(ks[14], (DEPTH, D_FF_2, D_MODEL), f32) * D_FF_2 ** -0.5,
        "final_norm_g": 1.0 + 0.02 * jax.random.normal(ks[15], (D_MODEL,), f32),
    }

def second_block(x, positions, norm_attn_g, w_in, lam_q1, lam_k1, lam_q2, lam_k2, subln_g,
              w_pool, pool_scale, w_out, norm_mlp_g, w_up, w_down, final_norm_g):
    B, S = x.shape[0], x.shape[1]
    splits = np.cumsum([ATT_QK_WIDTH, ATT_QK_WIDTH, ATT_V_WIDTH, POOL_WIDTH]).tolist()
    for l in range(DEPTH):
        lam_init = lambda_init(l)
        h = rmsnorm_2(x, norm_attn_g[l])
        u = h @ w_in[l]
        u_q, u_k, u_v, u_pool, u_gate = jnp.split(u, splits, axis=-1)
        q = u_q.reshape(B, S, N_HEADS, 2, HEAD_DIM_2)
        k = u_k.reshape(B, S, N_HEADS, 2, HEAD_DIM_2)
        v = u_v.reshape(B, S, N_HEADS, V_DIM)
        lam = (jnp.exp(jnp.sum(lam_q1[l].astype(jnp.float32) * lam_k1[l].astype(jnp.float32)))
               - jnp.exp(jnp.sum(lam_q2[l].astype(jnp.float32) * lam_k2[l].astype(jnp.float32)))
               + lam_init)
        a = diff_attention(q, k, v, positions, lam, subln_g[l], lam_init)
        p = multiscale_pool(u_pool, w_pool[l], pool_scale[l])
        gates = jax.nn.sigmoid(u_gate.reshape(B, S, N_BRANCHES, D_MODEL))
        merged = gates[:, :, 0] * a + gates[:, :, 1] * p
        x = x + (merged @ w_out[l]).astype(x.dtype)
        h2 = rmsnorm_2(x, norm_mlp_g[l])
        z = jnp.square(jax.nn.relu(h2 @ w_up[l]))
        x = x + (z @ w_down[l]).astype(x.dtype)
    return rmsnorm_2(x, final_norm_g)


def setup_inputs(seed=0):
    out = dict(first_inputs(seed))
    for name, value in second_inputs(seed + 1).items():
        if name != "x":
            out[name + "_2"] = value
    return out


def reference(
    x, p, mix_pre_norm, w_in, rwkv_mu, rwkv_w0, rwkv_w2, rwkv_a0, rwkv_a2, rwkv_g2, rwkv_k_k,
    rwkv_k_a, rwkv_r_k, rwkv_ln_w, rwkv_ln_b, w_attn_up, w_rwkv_up, w_out, mix_post_norm,
    ffn_pre_norm, w_ff_in, w_ff_out, ffn_post_norm, w_ple, w_ple_gate, ple_post_norm,
    positions_2, norm_attn_g_2, w_in_2, lam_q1_2, lam_k1_2, lam_q2_2, lam_k2_2, subln_g_2,
    w_pool_2, pool_scale_2, w_out_2, norm_mlp_g_2, w_up_2, w_down_2, final_norm_g_2,
):
    x = first_block(
        x, p, mix_pre_norm, w_in, rwkv_mu, rwkv_w0, rwkv_w2, rwkv_a0, rwkv_a2, rwkv_g2,
        rwkv_k_k, rwkv_k_a, rwkv_r_k, rwkv_ln_w, rwkv_ln_b, w_attn_up, w_rwkv_up, w_out,
        mix_post_norm, ffn_pre_norm, w_ff_in, w_ff_out, ffn_post_norm, w_ple, w_ple_gate,
        ple_post_norm,
    )
    return second_block(
        x, positions_2, norm_attn_g_2, w_in_2, lam_q1_2, lam_k1_2, lam_q2_2, lam_k2_2,
        subln_g_2, w_pool_2, pool_scale_2, w_out_2, norm_mlp_g_2, w_up_2, w_down_2,
        final_norm_g_2,
    )


_drawn_inputs = setup_inputs


def setup_inputs(seed=0):
    import zlib

    import numpy as np

    out = dict(_drawn_inputs(seed))
    spreads = {}
    factors = {'rwkv_k_k': 6.808,
     'rwkv_k_a': 3.651,
     'rwkv_ln_w': 4.302,
     'rwkv_ln_b': 4.075,
     'mix_post_norm': 4.126,
     'ffn_pre_norm': 4.496,
     'ffn_post_norm': 4.948,
     'ple_post_norm': 5.343,
     'norm_attn_g_2': 7.651,
     'lam_q1_2': 8.0,
     'lam_k1_2': 8.0,
     'lam_q2_2': 7.937,
     'lam_k2_2': 5.943,
     'subln_g_2': 8.0,
     'norm_mlp_g_2': 4.869,
     'final_norm_g_2': 2.877}
    for name, (base, spread) in spreads.items():
        noise = np.random.default_rng([zlib.crc32(name.encode()), seed]).standard_normal(out[name].shape)
        drawn = base * np.exp(spread * noise) if base else spread * noise
        out[name] = __import__('jax').numpy.asarray(drawn.astype(out[name].dtype))
    for name, factor in factors.items():
        out[name] = (out[name] * factor).astype(out[name].dtype)
    return out
```

```python
from contextlib import ExitStack, contextmanager

import numpy as np

import concourse.bass as bass
from concourse import mybir

F32 = mybir.dt.float32
F32R = mybir.dt.float32r
I32 = mybir.dt.int32
ALU = mybir.AluOpType
ACT = mybir.ActivationFunctionType

P = 128
T = 512
D = 1024
KT = D // P
NT = T // P
HD = 64
DFF = 4 * D
EPS = 1e-6
GN_EPS = 64e-5
NEG = -1.0e30

N_QKV = 18
N_RWKV = 14
U_QKV = 0
U_LORA = U_QKV + N_QKV
U_RKV = U_LORA + 2
U_MERGE = U_LORA + N_RWKV
U_OUT = U_MERGE + 3 * KT
U_FFN = U_OUT + KT
U_PLE = U_FFN + 64
U_HEADS = U_PLE + KT
U_POOL = U_HEADS + 3 * 8
U_POOLW = U_POOL + 4
U_GATE2 = U_POOLW + 1
U_OUT2 = U_GATE2 + 2 * KT
U_FFN2 = U_OUT2 + KT
N_UNITS = U_FFN2 + 64
RING = 4

O_QKV = 0
O_RWKV = O_QKV + N_QKV
O_GATE = O_RWKV + N_RWKV
O_OUT = O_GATE + 2 * KT
O_FFN = O_OUT + KT
O_PLE = O_FFN + 48
O_HEADS = O_PLE + KT
O_POOL = O_HEADS + 24
O_GATE2 = O_POOL + 4
O_OUT2 = O_GATE2 + 2 * KT
O_FFN2 = O_OUT2 + KT

PARAM_COLS = {}


def _columns():
    at = 0
    for name, n in (("mix_pre", 8), ("mix_post", 8), ("ffn_pre", 8), ("ffn_post", 8), ("ple_post", 8),
                    ("attn2", 8), ("mlp2", 8), ("final", 8), ("pool_scale", 8), ("mu", 14), ("w0", 4),
                    ("a0", 4), ("k_k", 4), ("k_a", 4), ("r_k", 4), ("ln_w", 4), ("ln_b", 4), ("subln", 1)):
        PARAM_COLS[name] = at
        at += n
    return at


N_PARAMS = _columns()

MATS = ("ident", "ones", "head_ones", "head_mean", "rot1", "rot2")
SCAN_MASKS = ("pair_lower", "pair_upper", "before", "upto", "lvl1", "lvl2", "lvl3", "lvl4", "lvl5")
LAM_INIT = 0.8 - 0.6 * float(np.exp(-0.0))


def shape_constants():
    i = np.arange(P)
    m = {"ident": np.eye(P), "ones": np.ones((P, P))}
    same_head = (i[:, None] // HD == i[None, :] // HD).astype(float)
    m["head_ones"], m["head_mean"] = same_head, same_head / HD
    r1, r2 = np.zeros((P, P)), np.zeros((P, P))
    for b in (0, 64):
        for j in range(32):
            r1[b + j, b + j + 32], r1[b + j + 32, b + j] = -1, 1
        for j in range(8):
            r2[b + j, b + j + 8], r2[b + j + 8, b + j] = -1, 1
    m["rot1"], m["rot2"] = r1.T, r2.T
    row, col = i[:, None], i[None, :]
    m["pair_lower"] = ((row == col + 1) & (col % 2 == 0)).astype(float)
    m["pair_upper"] = m["pair_lower"].T
    chunk = row // 64 == col // 64
    m["before"] = (chunk & (row < col)).astype(float)
    m["upto"] = (chunk & (row <= col)).astype(float)
    for l in range(1, 6):
        b = 2 ** l
        m[f"lvl{l}"] = ((row // (2 * b) == col // (2 * b)) & (row // b % 2 == 1) & (col // b % 2 == 0)).astype(float)
    mats = np.concatenate([m[n] for n in MATS], 1)
    scan_masks = np.concatenate([m[n] for n in SCAN_MASKS], 1)

    q = 4 * i[:, None]
    key = np.arange(T)[None, :]
    by4 = np.where(col <= row, 0.0, NEG)
    by16 = np.where((col <= row) & (col % 4 == row % 4), 0.0, NEG)
    masks = []
    for r in range(4):
        d = q + r - key
        masks += [np.where((d >= 0) & (d <= 128), 0.0, NEG), by4, by16]
    causal = np.where(key <= i[:, None] + 384, 0.0, NEG)
    f = i % HD
    inv1 = (10000.0 ** (-np.arange(0, HD, 2, dtype=np.float32) / np.float32(HD))).astype(np.float32)
    ang = (np.arange(T, dtype=np.float32)[None, :] * inv1[f % 32][:, None]).astype(np.float32).astype(np.float64)
    table1 = np.concatenate([np.cos(ang), np.sin(ang)], 1)
    inv2 = (500000.0 ** (-np.arange(0, 16, 2, dtype=np.float32) / np.float32(16))).astype(np.float32)
    invf2 = np.where(f < 16, inv2[f % 8], 0.0)
    small = np.zeros((P, 68))
    small[:, 0], small[:, 1], small[:, 2] = invf2, EPS, GN_EPS
    for g, w in enumerate((2, 4, 8, 16)):
        small[:, 4 + 16 * g:20 + 16 * g] = 1.0 / np.minimum(np.arange(16) + 1, w)
    c = np.ascontiguousarray
    f32 = np.float32
    return {"mats": c(mats, f32), "scan_masks": c(scan_masks, f32), "masks1": c(np.concatenate(masks, 1), f32),
            "causal": c(causal, f32), "table1": c(table1, f32), "small": c(small, f32)}


class Lane:

    def __init__(self, eng, sem, name):
        self.eng, self.sem, self.eng_name = eng, sem, name
        self.count, self.turn, self.each = {}, None, {}

    def value(self, name):
        n = self.count[name]
        return n + self.turn * self.each[name] if self.turn is not None else n

    def do(self, instruction, name="chain"):
        name = f"{self.eng_name}_{name}" if name == "chain" else name
        self.count[name] = self.count.get(name, 0) + 1
        instruction.then_inc(self.sem(name), 1)
        self.eng.wait_ge(self.sem(name), self.value(name))

    def leaves(self, o):
        name = f"out_evicted{o % 2}"
        self.count[name] = o // 2
        return name

    @contextmanager
    def loop(self, turns, each):
        each = {(f"{self.eng_name}_chain" if k == "chain" else k): v for k, v in each.items()}
        before = dict(self.count)
        with self.eng.Fori(0, turns, 1) as g:
            self.turn, self.each = g, each
            yield g
        self.turn = None
        for k in [k for k in each if not k.startswith("out_evicted")]:
            assert self.count[k] - before.get(k, 0) == each[k], (k, self.count[k], before.get(k), each[k])
            self.count[k] += each[k] * (turns - 1)


def build(nc, a):
    ctx = ExitStack()
    with ctx:
        sems = {}

        def S(name):
            if name not in sems:
                sems[name] = ctx.enter_context(nc.semaphore(name))
            return sems[name]

        def sbuf(stack, name, shape, dt=F32):
            return stack.enter_context(nc.sbuf_tensor(name, shape, dt))

        h = sbuf(ctx, "h", [P, KT, T])
        raw = [sbuf(ctx, f"raw{i}", [P, KT, P]) for i in range(RING)]
        WH = [sbuf(ctx, f"w_high{i}", [P, KT, P], F32R) for i in range(RING)]
        WL = [sbuf(ctx, f"w_low{i}", [P, KT, P], F32R) for i in range(RING)]
        UH = sbuf(ctx, "u_high", [P, KT, T], F32R)
        UL = sbuf(ctx, "u_low", [P, KT, T], F32R)
        par = sbuf(ctx, "params", [P, N_PARAMS])
        mats = sbuf(ctx, "mats", [P, len(MATS) * P])
        small = sbuf(ctx, "small", [P, 68])
        rstd = sbuf(ctx, "rstd", [P, T])
        acc = sbuf(ctx, "acc", [P, T])
        sq = sbuf(ctx, "sq", [P, T])
        tmp = [sbuf(ctx, f"tmp{i}", [P, T]) for i in range(2)]
        PS = ctx.enter_context(nc.psum_tensor("PS", [P, 8, 512], F32))

        M = {n: mats[:, i * P:(i + 1) * P] for i, n in enumerate(MATS)}

        def col(name, j=0):
            return par[:, PARAM_COLS[name] + j:PARAM_COLS[name] + j + 1]

        def over(m, n=NT):
            return m.unsqueeze(1).to_broadcast([P, n, P])

        def blk(x):
            return x.rearrange("p (a b) -> p a b", b=P)

        mix = ExitStack()
        OH = sbuf(mix, "o_high", [P, 2, T], F32R)
        OL = sbuf(mix, "o_low", [P, 2, T], F32R)

        att = ExitStack()
        aq = sbuf(att, "qk1", [P, 12, T])
        av = sbuf(att, "v1", [P, NT, 3, 256])
        table1 = sbuf(att, "table1", [P, 2 * T])
        masks1 = sbuf(att, "masks1", [P, 4 * 768])
        sp1 = [sbuf(att, f"probs1_{i}", [P, 768]) for i in range(2)]
        pt1 = [sbuf(att, f"probsT1_{i}", [P, 768]) for i in range(2)]
        oA = sbuf(att, "o1", [P, 2, T])
        st = sbuf(att, "stats1", [P, 8])
        rt = sbuf(att, "rope_tmp", [P, T])
        att.close()

        YH = sbuf(mix, "y_high", [P, 4, T], F32R)
        YL = sbuf(mix, "y_low", [P, 4, T], F32R)
        rw = ExitStack()
        smask = sbuf(rw, "scan_masks", [P, len(SCAN_MASKS) * P])
        K_ = {n: smask[:, i * P:(i + 1) * P] for i, n in enumerate(SCAN_MASKS)}
        lora_w = sbuf(rw, "lora_w", [P, 512])
        lora_g = sbuf(rw, "lora_g", [P, 512])
        zp = [sbuf(rw, f"z_padded{i}", [P, T + 1]) for i in range(3)]
        la = sbuf(rw, "lora_in", [P, T])
        lg = sbuf(rw, "lora_gate", [P, T])
        wkA = sbuf(rw, "work_a", [P, 2 * T])
        wkB = sbuf(rw, "work_b", [P, 2 * T])
        wkC = sbuf(rw, "work_c", [P, 2 * T])
        vs = sbuf(rw, "v_feature", [P, T])
        gt = sbuf(rw, "gate_feature", [P, T])
        PP = sbuf(rw, "decay_product", [P, 8, 65])
        FR, FA, FB, FK = (sbuf(rw, n, [P, T]) for n in ("r_scaled", "a_scaled", "b_scaled", "k_scaled"))
        bonus = sbuf(rw, "bonus", [P, T])
        RHS = sbuf(rw, "a_and_mv", [P, 2, NT, P])
        Bt, Kt, Vt = (sbuf(rw, n, [P, NT, P]) for n in ("b_token", "k_token", "v_token"))
        Lt, X, Y, Z = (sbuf(rw, n, [P, 2, T]) for n in ("lower_T", "inverse", "inverse_T", "product"))
        omka = sbuf(rw, "one_minus_ka", [P, 4 + 64])
        rw.close()

        late = ExitStack()
        ple = late.enter_context(nc.sbuf_tensor("ple", [P, KT, T], F32, side="right"))
        PH = sbuf(mix, "p_high", [P, 2, T], F32R)
        PL = sbuf(mix, "p_low", [P, 2, T], F32R)
        pf = sbuf(mix, "p_in", [P, 2, T])
        mg = ExitStack()
        MH = sbuf(mg, "merged_high", [P, KT, T], F32R)
        ML = sbuf(mg, "merged_low", [P, KT, T], F32R)
        mg.close()
        mix.close()

        ff = ExitStack()
        t8 = sbuf(ff, "branch_out", [P, KT, T])
        FH = sbuf(ff, "hidden_high", [P, 16, T], F32R)
        FL = sbuf(ff, "hidden_low", [P, 16, T], F32R)
        ff.close()
        late.close()

        b2 = ExitStack()
        aT = sbuf(b2, "attn_out2", [P, KT, T])
        poolT = sbuf(b2, "pool_out2", [P, KT, T])
        b2w = ExitStack()
        table2 = sbuf(b2w, "table2", [P, 2 * T])
        causal = sbuf(b2w, "causal", [P, T])
        pos = sbuf(b2w, "positions", [P, T], I32)
        rt2 = sbuf(b2w, "rope_tmp2", [P, T])
        lam4 = sbuf(b2w, "lam_vectors", [P, 4, HD])
        lamw = sbuf(b2w, "lam_work", [P, 8])
        q2 = [sbuf(b2w, f"q2_{i}", [P, T]) for i in range(2)]
        k2 = [sbuf(b2w, f"k2_{i}", [P, T]) for i in range(2)]
        v2 = [sbuf(b2w, f"v2_{i}", [P, NT, P]) for i in range(2)]
        e2 = [sbuf(b2w, f"exp2_{i}", [P, 2, T]) for i in range(2)]
        pt2 = [sbuf(b2w, f"weightsT2_{i}", [P, T]) for i in range(2)]
        st2 = sbuf(b2w, "stats2", [P, 2, 8])
        DH = sbuf(b2w, "pool_high", [P, 4, T], F32R)
        DL = sbuf(b2w, "pool_low", [P, 4, T], F32R)
        pz, pa, pb = (sbuf(b2w, n, [P, 16 + T]) for n in ("pool_in", "pool_sum_a", "pool_sum_b"))
        b2w.close()
        M2H = sbuf(b2, "merged2_high", [P, KT, T], F32R)
        M2L = sbuf(b2, "merged2_low", [P, KT, T], F32R)
        b2.close()
        f2 = ExitStack()
        F2H = sbuf(f2, "hidden2_high", [P, 16, T], F32R)
        F2L = sbuf(f2, "hidden2_low", [P, 16, T], F32R)
        f2.close()

        def flat(x):
            return x.rearrange("p a b -> p (a b)")

        def evicted(o):
            return S(f"out_evicted{o % 2}"), o // 2 + 1

        block = ctx.enter_context(nc.Block())

        @block.sync
        def _(sp):
            groups = a["w"][0:(N_UNITS // RING) * RING].rearrange("(g s) p k n -> g s p k n", s=RING)
            for s in range(RING):
                sp.dma_start(raw[s][:], a["w"][s]).then_inc(S(f"raw_in{s}"), 16)
            with sp.Fori(1, N_UNITS // RING, 1) as g:
                for s in range(RING):
                    sp.wait_ge(S("split_done"), g * RING + (s + 1 - RING))
                    sp.dma_start(raw[s][:], groups[g, s]).then_inc(S(f"raw_in{s}"), 16)
            for u in range((N_UNITS // RING) * RING, N_UNITS):
                sp.wait_ge(S("split_done"), u + 1 - RING)
                sp.dma_start(raw[u % RING][:], a["w"][u]).then_inc(S(f"raw_in{u % RING}"), 16)
            sp.wait_ge(S("stored"), 16 * KT)

        @block.gpsimd
        def _(pool):
            lane = Lane(pool, S, "pool")

            def split(s, arrived, free):
                pool.wait_ge(S(f"raw_in{s}"), arrived)
                if free is not None:
                    pool.wait_ge(S("units_done"), free)
                    pool.sem_inc(S("slot_taken"), 1)
                lane.do(nc.gpsimd.tensor_scalar(flat(WH[s][:]), flat(raw[s][:]), 1.0, 0.0, ALU.mult, ALU.add),
                        "split_high")
                nc.gpsimd.tensor_tensor(flat(WL[s][:]), flat(raw[s][:]), flat(WH[s][:]).bitcast(F32),
                                        ALU.subtract).then_inc(S("split_done"), 1)

            for s in range(RING):
                split(s, 16, None)
            lane.count["split_high"] = RING
            with pool.Fori(1, N_UNITS // RING, 1) as g:
                lane.turn, lane.each = g - 1, {"split_high": RING}
                for s in range(RING):
                    split(s, g * 16 + 16, g * RING + (s + 1 - RING))
                lane.turn = None
            lane.count["split_high"] = (N_UNITS // RING) * RING
            for u in range((N_UNITS // RING) * RING, N_UNITS):
                split(u % RING, 16 * (u // RING + 1), u + 1 - RING)

        @block.tensor
        def _(pe):
            def mm(out, lhsT, rhs, start=True, stop=True):
                return nc.tensor.matmul(out, lhsT, rhs, start=start, stop=stop)

            def product(out, s, slices, high, low, wait_slice=None, start=True, stop=True):
                for n, (k, r) in enumerate(slices):
                    if wait_slice is not None:
                        wait_slice(r)
                    first, last = start and n == 0, stop and n == len(slices) - 1
                    mm(out, WH[s][:, k, :], high[:, r, :], first, False)
                    mm(out, WH[s][:, k, :], low[:, r, :], False, False)
                    i = mm(out, WL[s][:, k, :], high[:, r, :], False, last)
                return i

            ALL = [(k, k) for k in range(KT)]

            def unit(u, o, high, low, wait_slice=None):
                pe.wait_ge(S("split_done"), u + 1)
                if o >= 2:
                    pe.wait_ge(*evicted(o - 2))
                product(PS[:, o % 2, :], u % RING, ALL, high, low, wait_slice).then_inc(S("units_done"), 1)

            def units_loop(u, o, n, high, low):
                with pe.Fori(0, n // 4, 1) as g:
                    for j in range(4):
                        pe.wait_ge(S("split_done"), g * 4 + (u + j + 1))
                        pe.wait_ge(S(f"out_evicted{(o + j) % 2}"), g * 2 + (o + j) // 2)
                        product(PS[:, (o + j) % 2, :], (u + j) % RING, ALL, high, low)\
                            .then_inc(S("units_done"), 1)

            def norm_sum(n):
                pe.wait_ge(S("squares_summed"), KT * (n + 1))
                mm(PS[:, 7, :], M["ones"], acc[:]).then_inc(S("norm_summed"), 1)

            def input_split(n):
                return lambda k: pe.wait_ge(S("u_low"), KT * n + k + 1)

            def after_qkv(o):
                pe.wait_ge(*evicted(o))
                if o < 12:
                    if o >= 2:
                        pe.wait_ge(S("roped"), o - 1)
                    mm(PS[:, 2 + o % 2, :], M["rot1"], tmp[o % 2][:]).then_inc(S("rotated"), 1)
                else:
                    i = o - 12
                    if i >= 2:
                        pe.wait_ge(S("v_token"), i - 1)
                    for t in range(NT):
                        src = tmp[o % 2][:, t * P:(t + 1) * P] if i < 2 else tmp[o % 2][:, t::4]
                        x = nc.tensor.transpose(PS[:, 4 + o % 2, t * P:(t + 1) * P], src, M["ident"])
                    x.then_inc(S("v_turned"), 1)

            pe.wait_ge(S("consts_in"), 48)
            for o in range(N_QKV):
                unit(U_QKV + o, O_QKV + o, UH, UL, input_split(0) if o == 0 else None)
                if o == 0:
                    norm_sum(0)
                else:
                    after_qkv(o - 1)
            after_qkv(N_QKV - 1)

            def scores(i):
                r, n = i // 4, i % 4
                half, row = n // 2, 64 * (n % 2)
                if i == 0:
                    pe.wait_ge(S("roped"), 12)
                    pe.wait_ge(S("v_token"), 6)
                if i >= 2:
                    pe.wait_ge(S("masked"), i - 1)
                b = 2 + 2 * (i % 2)
                for g in range(3):
                    q = aq[row:row + 64, 2 * g + half, r::4]
                    k = aq[row:row + 64, 6 + 2 * g + half, :] if g == 0 else aq[row:row + 64, 6 + 2 * g + half, r::4]
                    out = PS[:, b, :] if g == 0 else PS[:, b + 1, (g - 1) * P:g * P]
                    x = mm(out, q, k)
                x.then_inc(S("scores"), 1)

            def turn_probs(i):
                pe.wait_ge(S("probs"), i + 1)
                if i >= 1:
                    pe.wait_ge(S("probs_copied"), i)
                for j in range(6):
                    x = nc.tensor.transpose(PS[:, j // 4, (j % 4) * P:(j % 4 + 1) * P],
                                            sp1[i % 2][:, j * P:(j + 1) * P], M["ident"])
                x.then_inc(S("probs_turned"), 1)

            def values(i):
                r, n = i // 4, i % 4
                row = 64 * (n % 2)
                pe.wait_ge(S("probs_copied"), i + 1)
                if i >= 2:
                    pe.wait_ge(S("o_copied"), i - 1)
                out = PS[row:row + 64, 6 + i % 2, 0:P]
                for j in range(6):
                    g, t = (0, j) if j < 4 else (j - 3, r)
                    x = mm(out, av[:, t, g, n * 64:(n + 1) * 64], pt1[i % 2][:, j * P:(j + 1) * P],
                           j == 0, j == 5)
                x.then_inc(S("o_done"), 1)

            for i in range(16 + 2):
                if i < 16:
                    scores(i)
                if 1 <= i < 17:
                    turn_probs(i - 1)
                if i >= 2:
                    values(i - 2)

            def rkv_units(hp):
                for j in range(3):
                    unit(U_RKV + 3 * hp + j, O_RWKV + 2 + 3 * hp + j, UH, UL)

            def tiles4(out, lhsT, rhs):
                for t in range(NT):
                    x = mm(out(t), lhsT(t), rhs(t))
                return x

            pe.wait_ge(S("probs_copied"), 16)
            unit(U_LORA, O_RWKV, UH, UL)
            unit(U_LORA + 1, O_RWKV + 1, UH, UL)
            rkv_units(0)
            for hp in range(4):
                c = slice(hp * P, (hp + 1) * P)
                if hp == 0:
                    pe.wait_ge(S("lora_in"), 2)
                    pe.wait_ge(S("scan_consts_in"), 64)
                    pe.wait_ge(S("o_copied"), 16)
                else:
                    pe.wait_ge(S("rwkv_out"), hp)
                mm(PS[:, 2, :], lora_w[0:32, c], la[0:32, :]).then_inc(S("lora_done"), 1)
                mm(PS[:, 3, :], lora_w[32:64, c], la[32:64, :]).then_inc(S("lora_done"), 1)
                mm(PS[:, 4, :], lora_g[0:96, c], lg[0:96, :]).then_inc(S("lora_done"), 1)
                pe.wait_ge(S("k_squared"), hp + 1)
                mm(PS[:, 5, :], M["head_ones"], sq[:]).then_inc(S("k_summed"), 1)
                pe.wait_ge(S("rk_ready"), hp + 1)
                mm(PS[:, 6, :], M["head_ones"], tmp[1][:]).then_inc(S("rk_summed"), 1)
                if hp < 3:
                    rkv_units(hp + 1)
                pe.wait_ge(S("scaled"), 4 * (hp + 1))
                pe.wait_ge(S("lora_used"), 4 * (hp + 1))
                pe.wait_ge(S("k_root"), hp + 1)
                for n, src in enumerate((FA, FB, FK, vs)):
                    for t in range(NT):
                        x = nc.tensor.transpose(PS[:, 2 + n, t * P:(t + 1) * P], src[:, t * P:(t + 1) * P], M["ident"])
                    x.then_inc(S("turned"), 1)

                def tokens(out_bank, lhsT, rhs, e):
                    r = slice(64 * e, 64 * e + 64)
                    for t in range(NT):
                        b = slice(t * P, (t + 1) * P)
                        x = mm(PS[:, out_bank, b], lhsT[r, b], rhs[r, b])
                    return x

                pe.wait_ge(S("token_a"), 3 * (hp + 1))
                pe.wait_ge(S("token_d"), 2 * (hp + 1))
                for e in range(2):
                    tokens(2 + 2 * e, FA, FB, e)
                    tokens(3 + 2 * e, FB, FA, e).then_inc(S("lower_done"), 1)
                for l in range(1, 6):
                    for e in range(2):
                        pe.wait_ge(S("inverse_ready"), 12 * hp + 2 * (l - 1) + e + 1)
                        for t in range(NT):
                            b = slice(t * P, (t + 1) * P)
                            x = mm(PS[:, 6 + e, b], Lt[:, e, b], X[:, e, b])
                        x.then_inc(S("lx_done"), 1)
                    for e in range(2):
                        pe.wait_ge(S("lx_masked"), 10 * hp + 2 * (l - 1) + e + 1)
                        for t in range(NT):
                            b = slice(t * P, (t + 1) * P)
                            if l < 5:
                                mm(PS[:, 2 + e, b], Y[:, e, b], Z[:, e, b])
                            x = mm(PS[:, 4 + e, b], Z[:, e, b], Y[:, e, b])
                        x.then_inc(S("xlx_done"), 1)
                pe.wait_ge(S("inverse_ready"), 12 * (hp + 1))
                for n, (l, r) in enumerate(((FK, FA), (FB, FR), (FK, FR))):
                    for e in range(2):
                        tokens(2 + 2 * n + e, l, r, e).then_inc(S("pairs_done"), 1)
                for e in range(2):
                    pe.wait_ge(S("pairs_masked"), 6 * hp + 1 + e)
                    for t in range(NT):
                        x = mm(PS[:, 2 + e, t * 64:(t + 1) * 64], Lt[:, e, t * P:(t + 1) * P],
                               Vt[:, t, 64 * e:64 * e + 64])
                    x.then_inc(S("mv_done"), 1)
                for e in range(2):
                    pe.wait_ge(S("mv_copied"), 2 * hp + e + 1)
                    pe.wait_ge(S("pairs_masked"), 6 * hp + 3 + e)
                    for t in range(NT):
                        x = mm(PS[:, 4 + e, t * P:(t + 1) * P], Y[:, e, t * P:(t + 1) * P], RHS[:, e, t, :])
                    x.then_inc(S("wu_done"), 1)
                WU = Z[:].rearrange("p w (t n) -> p w t n", t=NT)
                mrk = (FA, FB)
                for e in range(2):
                    pe.wait_ge(S("wu_copied"), 4 * hp + 2 * e + 2)
                    pe.wait_ge(S("pairs_masked"), 6 * hp + 6)
                    r = slice(64 * e, 64 * e + 64)
                    for t in range(NT):
                        b = slice(t * P, (t + 1) * P)
                        mm(PS[r, 6, b], WU[:, 0, t, r], X[:, e, b])
                        mm(PS[r, 7, b], WU[:, 1, t, r], X[:, e, b], True, False)
                        x = mm(PS[r, 7, b], Vt[:, t, r], mrk[e][:, b], False, True)
                x.then_inc(S("qy_done"), 1)
                for ch in range(7):
                    r, t = slice(64 * (ch % 2), 64 * (ch % 2) + 64), ch // 2
                    b = slice(t * P, (t + 1) * P)
                    if ch:
                        mm(PS[:, 2 + ch % 2, b], WU[r, 0, t, :], Bt[r, t, :])
                    mm(PS[:, 4 + ch % 2, b], Bt[r, t, :], WU[r, 1, t, :], True, False)
                    x = mm(PS[:, 4 + ch % 2, b], Kt[r, t, :], Vt[r, t, :], False, True)
                x.then_inc(S("chunks_done"), 1)
                G = blk(wkA[:])
                H = blk(wkB[:])
                St = blk(wkC[:])
                pe.wait_ge(S("chunks_ready"), hp + 1)
                pe.wait_ge(S("q_ready"), hp + 1)
                pe.wait_ge(S("y0_ready"), hp + 1)
                for ch in range(1, 7):
                    if ch > 1:
                        pe.wait_ge(S("state_ready"), 6 * hp + ch - 1)
                    mm(PS[:, 6 + ch % 2, 0:P], G[:, ch, :], H[:, 0, :] if ch == 1 else St[:, ch, :])\
                        .then_inc(S("state_done"), 1)
                pe.wait_ge(S("state_ready"), 6 * hp + 6)
                for ch in range(1, 8):
                    b = slice(64 * ch, 64 * ch + 64)
                    x = mm(PS[:, 2, b], H[:, 0, :] if ch == 1 else St[:, ch, :], FR[:, b])
                x.then_inc(S("y_done"), 1)
                pe.wait_ge(S("y_ready"), hp + 1)
                mm(PS[:, 3, :], M["head_mean"], FK[:]).then_inc(S("mean_done"), 1)
                pe.wait_ge(S("y_squared"), hp + 1)
                mm(PS[:, 4, :], M["head_mean"], sq[:]).then_inc(S("var_done"), 1)

            for m in range(KT):
                u, o = U_MERGE + 3 * m, O_GATE + 2 * m
                unit(u, o, UH, UL)
                unit(u + 1, o + 1, UH, UL)
                pe.wait_ge(S("split_done"), u + 3)
                b = 2 + 3 * (m % 2)
                if m == 0:
                    pe.wait_ge(S("rwkv_out"), 4)
                    pe.wait_ge(S("p_low"), 2)
                if m >= 2:
                    pe.wait_ge(S("merged"), m - 1)
                    pe.wait_ge(S("ple_copied"), m - 1)
                s = (u + 2) % RING
                product(PS[:, b, :], s, [(0, 0), (1, 1)], OH, OL)
                product(PS[:, b + 1, :], s, [(2 + k, k) for k in range(4)], YH, YL)
                product(PS[:, b + 2, :], s, [(6, 0), (7, 1)], PH, PL).then_inc(S("units_done"), 1)
            for m in range(KT):
                unit(U_OUT + m, O_OUT + m, MH, ML,
                     (lambda k: pe.wait_ge(S("merged_low"), k + 1)) if m == 0 else None)
            norm_sum(1)

            def feed_forward(U, O, n, norm, high, low, hid, done):
                norm_first = True
                for half in range(2):
                    u, o = U + 32 * half, O + 24 * half
                    if half == 0:
                        pe.wait_ge(S("u_low"), KT * (n + 1))
                        norm_sum(norm)
                    units_loop(u, o, 16, UH, UL)
                    pe.wait_ge(S("hidden_low"), hid + 16 * (half + 1))
                    u, o = u + 16, o + 16
                    with pe.Fori(0, 4, 1) as g:
                        for j in range(2):
                            pe.wait_ge(S(f"out_evicted{(o + j) % 2}"), g + (o + j) // 2)
                            for w in range(2):
                                pe.wait_ge(S("split_done"), g * 4 + (u + 2 * j + w + 1))
                                product(PS[:, (o + j) % 2, :], (u + 2 * j + w) % RING,
                                        [(k, 8 * w + k) for k in range(KT)], high, low,
                                        start=w == 0, stop=w == 1).then_inc(S("units_done"), 1)

            feed_forward(U_FFN, O_FFN, 1, 2, FH, FL, 0, 0)
            norm_sum(3)
            pe.wait_ge(S("u_low"), KT * 3)
            units_loop(U_PLE, O_PLE, KT, UH, UL)
            norm_sum(4)

            def after_heads(o):
                pe.wait_ge(*evicted(O_HEADS + o))
                if o >= 1:
                    pe.wait_ge(S("head_input"), o)
                src = tmp[(O_HEADS + o) % 2]
                if o % 3 < 2:
                    x = mm(PS[:, 2, :], M["rot2"], src[:])
                else:
                    for t in range(NT):
                        x = nc.tensor.transpose(PS[:, 2, t * P:(t + 1) * P], src[:, t * P:(t + 1) * P], M["ident"])
                x.then_inc(S("head_turned"), 1)

            def scores2(i):
                n, qt = i // 4, i % 4
                if qt == 0:
                    pe.wait_ge(S("head_input"), 3 * n + 3)
                if i >= 1:
                    pe.wait_ge(S("masked2"), 2 * i)
                for c in range(2):
                    r = slice(64 * c, 64 * c + 64)
                    x = mm(PS[:, 4 + c, 0:P * (qt + 1)], q2[n % 2][r, qt * P:(qt + 1) * P],
                           k2[n % 2][r, 0:P * (qt + 1)])
                x.then_inc(S("scores2"), 1)

            def turn_weights(i):
                qt = i % 4
                pe.wait_ge(S("weights2"), i + 1)
                if i >= 1:
                    pe.wait_ge(S("weights_copied"), i)
                for j in range(qt + 1):
                    x = nc.tensor.transpose(PS[:, 3, j * P:(j + 1) * P], e2[i % 2][:, 0, j * P:(j + 1) * P], M["ident"])
                x.then_inc(S("weights_turned"), 1)

            def values2(i):
                n, qt = i // 4, i % 4
                pe.wait_ge(S("weights_copied"), i + 1)
                if qt == 0 and n >= 1:
                    pe.wait_ge(S("a_copied"), n)
                for j in range(qt + 1):
                    x = mm(PS[:, 6, qt * P:(qt + 1) * P], v2[n % 2][:, j, :], pt2[i % 2][:, j * P:(j + 1) * P],
                           j == 0, j == qt)
                x.then_inc(S("a_done"), 1)

            def head_sum(n):
                pe.wait_ge(S("a_squared"), n + 1)
                mm(PS[:, 7, :], M["ones"], sq[:]).then_inc(S("a_summed"), 1)

            for o in range(3):
                unit(U_HEADS + o, O_HEADS + o, UH, UL, input_split(3) if o == 0 else None)
                if o == 0:
                    norm_sum(5)
                after_heads(o)
            for i in range(32 + 2):
                n, qt = i // 4, i % 4
                if i < 32:
                    scores2(i)
                if n < 7:
                    if qt >= 1:
                        after_heads(3 * (n + 1) + qt - 1)
                    if qt < 3:
                        o = 3 * (n + 1) + qt
                        unit(U_HEADS + o, O_HEADS + o, UH, UL)
                if 1 <= i < 33:
                    turn_weights(i - 1)
                if i >= 2:
                    values2(i - 2)
                    if i % 4 == 1:
                        head_sum((i - 2) // 4)

            for j in range(4):
                unit(U_POOL + j, O_POOL + j, UH, UL)
            pe.wait_ge(S("split_done"), U_POOLW + 1)
            for m in range(KT):
                pe.wait_ge(S("pooled_low"), m // 2 + 1)
                if m >= 4:
                    pe.wait_ge(S("pool_copied"), m - 3)
                product(PS[:, 2 + m % 4, :], U_POOLW % RING, [(m, m // 2)], DH, DL)\
                    .then_inc(S("pool_done") if m < KT - 1 else S("units_done"), 1)
            for m in range(2 * KT):
                unit(U_GATE2 + m, O_GATE2 + m, UH, UL)
            for m in range(KT):
                unit(U_OUT2 + m, O_OUT2 + m, M2H, M2L,
                     (lambda k: pe.wait_ge(S("merged_low"), KT + k + 1)) if m == 0 else None)
            feed_forward(U_FFN2, O_FFN2, 4, 6, F2H, F2L, 32, 0)
            norm_sum(7)

        @block.scalar
        def _(act):
            lane = Lane(act, S, "act")

            def f(out, in_, func, name="chain", **more):
                lane.do(nc.scalar.activation(out, in_, func, **more), name)

            act.dma_start(h[:, 0:4, :], a["x"][:, 0:4, :]).then_inc(S("x_in0"), 16)
            act.dma_start(par[:], a["params"]).then_inc(S("consts_in"), 16)
            act.dma_start(small[:], a["small"]).then_inc(S("consts_in"), 16)
            act.dma_start(h[:, 4:8, :], a["x"][:, 4:8, :]).then_inc(S("x_in1"), 16)
            act.dma_start(mats[:], a["mats"]).then_inc(S("consts_in"), 16)
            act.dma_start(table1[:], a["table1"]).then_inc(S("table1_in"), 16)
            act.dma_start(masks1[:], a["masks1"]).then_inc(S("masks1_in"), 16)

            def split_high(n, m, gain, norm):
                src = h[:, m, :]
                if gain:
                    if m >= 2:
                        act.wait_ge(S("u_low"), KT * n + m - 1)
                    f(tmp[m % 2][:], src, ACT.Identity, scale=col(gain, m))
                    src = tmp[m % 2][:]
                f(UH[:, m, :], src, ACT.Copy, "u_high")
                if norm is not None:
                    square(h[:, m, :], norm, m)

            def square(src, norm, m):
                if norm or m:
                    act.wait_ge(S("squares_summed"), KT * norm + m)
                f(sq[:], src, ACT.Square, "squared")

            def root(n):
                act.wait_ge(S("norm_summed"), n + 1)
                f(acc[:], PS[:, 7, :], ACT.Sqrt, "rooted", scale=1.0 / D, bias=small[:, 1:2])

            act.wait_ge(S("consts_in"), 48)
            for m in range(KT):
                if m % 4 == 0:
                    act.wait_ge(S(f"x_in{m // 4}"), 16)
                split_high(0, m, "mix_pre", 0)
            root(0)

            for i in range(16 + 2):
                if i < 16:
                    p = 4 * (i % 2)
                    act.wait_ge(S("neg_max"), i + 1)
                    f(sp1[i % 2][:], sp1[i % 2][:], ACT.Exp, "exp1", scale=0.125, bias=st[:, p + 1:p + 2],
                      accum_out=st[:, p + 2:p + 3])
                if 1 <= i < 17:
                    act.wait_ge(S("probs_turned"), i)
                    if i >= 3:
                        act.wait_ge(S("o_done"), i - 2)
                    f(pt1[(i - 1) % 2][:], flat(PS[:, 0:2, :])[:, 0:768], ACT.Copy, "probs_copied")
                if i >= 2:
                    r, n = (i - 2) // 4, (i - 2) % 4
                    row = slice(64 * (n % 2), 64 * (n % 2) + 64)
                    act.wait_ge(S("o_done"), i - 1)
                    f(oA[row, n // 2, r::4], PS[row, 6 + i % 2, 0:P], ACT.Copy, "o_copied")
            for m in range(2):
                f(OH[:, m, :], oA[:, m, :], ACT.Copy, "o_high")
            act.wait_ge(S("o_low"), 2)
            act.dma_start(smask[:], a["scan_masks"]).then_inc(S("scan_consts_in"), 16)
            act.dma_start(lora_w[0:32, :], a["w2"]).then_inc(S("scan_consts_in"), 16)
            act.dma_start(lora_w[32:64, :], a["a2"]).then_inc(S("scan_consts_in"), 16)
            act.dma_start(lora_g[0:96, :], a["g2"]).then_inc(S("scan_consts_in"), 16)

            act.wait_ge(S("lora_shifted"), 1)
            f(la[0:32, :], la[0:32, :], ACT.Tanh, "lora_in")
            act.wait_ge(S("lora_shifted"), 2)
            f(lg[0:96, :], lg[0:96, :], ACT.Sigmoid, "lora_in")
            WU = Z[:].rearrange("p w (t n) -> p w t n", t=NT)
            for hp in range(4):
                act.wait_ge(S("lora_done"), 3 * hp + 1)
                f(wkA[:, 0:T], PS[:, 2, :], ACT.Sigmoid, "lora_used", bias=col("w0", hp))
                act.wait_ge(S("lora_done"), 3 * hp + 2)
                f(wkA[:, T:2 * T], PS[:, 3, :], ACT.Sigmoid, "lora_used", bias=col("a0", hp))
                act.wait_ge(S("lora_done"), 3 * hp + 3)
                f(gt[:], PS[:, 4, :], ACT.Copy, "lora_used")
                f(wkA[:, 0:T], wkA[:, 0:T], ACT.Exp, "lora_used", scale=-float(np.exp(-0.5)))
                act.wait_ge(S("kk_raw"), hp + 1)
                f(sq[:], wkB[:, 0:T], ACT.Square, "k_squared")
                act.wait_ge(S("k_summed"), hp + 1)
                f(sq[:], PS[:, 5, :], ACT.Sqrt, "k_root")
                act.wait_ge(S("turned"), 4 * hp + 1)
                for e in range(2):
                    f(RHS[:, e, :, 0:64], blk(PS[:, 2, :])[:, :, 64 * e:64 * e + 64], ACT.Copy, "token_a")
                act.wait_ge(S("turned"), 4 * hp + 2)
                f(Bt[:], blk(PS[:, 3, :]), ACT.Copy, "token_a")
                for e in range(2):
                    act.wait_ge(S("mv_done"), 2 * hp + e + 1)
                    f(RHS[:, e, :, 64:128], PS[:, 2 + e, 0:256].rearrange("p (t n) -> p t n", t=NT), ACT.Copy,
                      "mv_copied")
                for e in range(2):
                    act.wait_ge(S("wu_done"), 2 * hp + e + 1)
                    for w in range(2):
                        f(WU[:, w, :, 64 * e:64 * e + 64], blk(PS[:, 4 + e, :])[:, :, 64 * w:64 * w + 64], ACT.Copy,
                          "wu_copied")
                act.wait_ge(S("qy_done"), hp + 1)
                f(FK[:], PS[:, 7, :], ACT.Copy, "y0_ready")
                act.wait_ge(S("y_centered"), hp + 1)
                f(sq[:], tmp[0][:], ACT.Square, "y_squared")
                act.wait_ge(S("var_done"), hp + 1)
                f(sq[:], PS[:, 4, :], ACT.Sqrt, "y_root", bias=small[:, 2:3])
                act.wait_ge(S("y_final"), hp + 1)
                f(YH[:, hp, :], tmp[1][:], ACT.Copy, "y_high")

            act.wait_ge(S("rwkv_out"), 4)
            act.dma_start(pf[:], a["p"]).then_inc(S("p_in"), 16)
            act.wait_ge(S("p_in"), 16)
            for m in range(2):
                f(PH[:, m, :], pf[:, m, :], ACT.Copy, "p_high")

            def sigmoids(o, m, base):
                for j in range(2):
                    act.wait_ge(*evicted(o + 2 * m + j))
                    f(tmp[j][:], tmp[j][:], ACT.Sigmoid, "gated")

            def merged_high(high, m, base):
                act.wait_ge(S("merged"), base + m + 1)
                f(high[:, m, :], tmp[0][:], ACT.Copy, "merged_high")

            for m in range(KT):
                sigmoids(O_GATE, m, 0)
                act.wait_ge(S("units_done"), U_MERGE + 3 * m + 3)
                f(ple[:, m, :], PS[:, 4 + 3 * (m % 2), :], ACT.Copy, "ple_copied")
                merged_high(MH, m, 0)
            for m in range(KT):
                act.wait_ge(S("units_done"), U_OUT + m + 1)
                f(t8[:, m, :], PS[:, (O_OUT + m) % 2, :], ACT.Copy, lane.leaves(O_OUT + m))
                square(t8[:, m, :], 1, m)
            root(1)

            def feed_forward(U, O, high, hid, dst, norm):
                highs = high[:].rearrange("p (g j) t -> p g j t", j=4)
                outs = dst[:].rearrange("p (g j) t -> p g j t", j=2)
                for half in range(2):
                    o = O + 24 * half
                    with lane.loop(4, {"chain": 4, "hidden_high": 4}) as g:
                        for j in range(4):
                            act.wait_ge(S(f"out_evicted{(o + j) % 2}"), g * 2 + ((o + j) // 2 + 1))
                            f(tmp[j % 2][:], tmp[j % 2][:], ACT.Square)
                            f(highs[:, g, j, :], tmp[j % 2][:], ACT.Copy, "hidden_high")
                o += 16
                with lane.loop(4, {"squared": 2}) as g:
                    for j in range(2):
                        act.wait_ge(S(f"out_evicted{(o + j) % 2}"), g + ((o + j) // 2 + 1))
                        act.wait_ge(S("squares_summed"), g * 2 + (KT * norm + j))
                        f(sq[:], outs[:, g, j, :], ACT.Square, "squared")
                root(norm)

            def updated(n, m):
                act.wait_ge(S("h_new"), KT * n + m + 1)

            for m in range(KT):
                updated(0, m)
                split_high(1, m, "ffn_pre", 2)
            root(2)
            feed_forward(U_FFN, O_FFN, FH, 0, t8, 3)

            act.dma_start(pos[:], a["positions"].to_broadcast([P, T])).then_inc(S("block2_in"), 16)
            act.dma_start(causal[:], a["causal"]).then_inc(S("block2_in"), 16)
            for j in range(4):
                act.dma_start(lam4[:, j, :], a[f"lam{j}"].to_broadcast([P, HD])).then_inc(S("block2_in"), 16)
            for m in range(KT):
                updated(1, m)
                split_high(2, m, None, None)
            plev = ple[:].rearrange("p (g j) t -> p g j t", j=4)
            t8v = t8[:].rearrange("p (g j) t -> p g j t", j=4)
            with lane.loop(2, {"out_evicted0": 2, "out_evicted1": 2, "squared": 4}) as g:
                for j in range(4):
                    act.wait_ge(S("units_done"), g * 4 + (U_PLE + j + 1))
                    f(tmp[j % 2][:], PS[:, j % 2, :], ACT.Sigmoid, lane.leaves(O_PLE + j))
                    act.wait_ge(S("e_new"), g * 4 + (j + 1))
                    act.wait_ge(S("squares_summed"), g * 4 + (KT * 4 + j))
                    f(sq[:], t8v[:, g, j, :], ACT.Square, "squared")
            root(4)
            act.wait_ge(S("lam_dots"), 2)
            f(lamw[:, 2:4], lamw[:, 0:2], ACT.Exp, "lam_exp")
            act.wait_ge(S("angles"), 2)
            f(table2[:, T:2 * T], table2[:, T:2 * T], ACT.Sin, "table2")
            f(table2[:, 0:T], table2[:, 0:T], ACT.Sin, "table2")

            for m in range(KT):
                updated(2, m)
                split_high(3, m, "attn2", 5)
            root(5)
            for i in range(32 + 2):
                if i < 32:
                    p, n = i % 2, P * (i % 4 + 1)
                    act.wait_ge(S("neg_max2"), i + 1)
                    for c in range(2):
                        f(e2[p][:, c, 0:n], e2[p][:, c, 0:n], ACT.Exp, "exp2", scale=0.125,
                          bias=st2[:, p, 2 + c:3 + c], accum_out=st2[:, p, 4 + c:5 + c])
                if 1 <= i < 33:
                    n = P * ((i - 1) % 4 + 1)
                    act.wait_ge(S("weights_turned"), i)
                    if i >= 3:
                        act.wait_ge(S("a_done"), i - 2)
                    f(pt2[(i - 1) % 2][:, 0:n], PS[:, 3, 0:n], ACT.Copy, "weights_copied")
                if i >= 2 and i % 4 == 1:
                    n = (i - 2) // 4
                    act.wait_ge(S("a_done"), 4 * n + 4)
                    f(aT[:, n, :], PS[:, 6, :], ACT.Copy, "a_copied")
                    f(sq[:], aT[:, n, :], ACT.Square, "a_squared")
                    act.wait_ge(S("a_summed"), n + 1)
                    f(sq[:], PS[:, 7, :], ACT.Sqrt, "a_root", scale=1.0 / P, bias=small[:, 1:2])
            for j in range(4):
                act.wait_ge(S("pool_diff"), j + 1)
                f(DH[:, j, :], pz[:, 16:16 + T], ACT.Copy, "pool_high")
            for m in range(KT):
                if m < KT - 1:
                    act.wait_ge(S("pool_done"), m + 1)
                else:
                    act.wait_ge(S("units_done"), U_POOLW + 1)
                f(poolT[:, m, :], PS[:, 2 + m % 4, :], ACT.Identity, "pool_copied", scale=col("pool_scale", m))
            for m in range(KT):
                sigmoids(O_GATE2, m, KT)
                merged_high(M2H, m, KT)
            for m in range(KT):
                act.wait_ge(*evicted(O_OUT2 + m))
                split_high(4, m, "mlp2", 6)
            root(6)
            feed_forward(U_FFN2, O_FFN2, F2H, 32, h, 7)
            for m in range(KT):
                act.wait_ge(S("final"), m + 1)
                act.dma_start(a["out"][:, m, :], h[:, m, :]).then_inc(S("stored"), 16)

        @block.vector
        def _(dve):
            lane = Lane(dve, S, "dve")

            def tt(out, x, y, op, name="chain"):
                lane.do(nc.vector.tensor_tensor(out, x, y, op), name)

            def ts(out, x, s1, op1, name="chain", s2=None, op2=ALU.bypass):
                if s2 is None:
                    lane.do(nc.vector.tensor_scalar(out, x, s1, None, op1), name)
                else:
                    lane.do(nc.vector.tensor_scalar(out, x, s1, s2, op1, op2), name)

            def stt(out, x, s, y, op1, op2, name="chain"):
                lane.do(nc.vector.scalar_tensor_tensor(out=out, in0=x, scalar=s, in1=y, op0=op1, op1=op2), name)

            def copy(out, x, name="chain"):
                lane.do(nc.vector.tensor_copy(out, x), name)

            def recip(out, x):
                lane.do(nc.vector.reciprocal(out, x))

            MUL, ADD, SUB = ALU.mult, ALU.add, ALU.subtract

            def split_low(n, m, gain, norm):
                dve.wait_ge(S("u_high"), KT * n + m + 1)
                tt(UL[:, m, :], tmp[m % 2][:] if gain else h[:, m, :], UH[:, m, :].bitcast(F32), SUB, "u_low")
                if norm is not None:
                    add_squares(norm, m)

            def add_squares(norm, m):
                dve.wait_ge(S("squared"), KT * norm + m + 1)
                if m == 0:
                    copy(acc[:], sq[:], "squares_summed")
                else:
                    tt(acc[:], acc[:], sq[:], ADD, "squares_summed")

            def norm_scale(n):
                dve.wait_ge(S("rooted"), n + 1)
                recip(rstd[:], acc[:])

            def evict(o, u, dst):
                dve.wait_ge(S("units_done"), u + 1)
                tt(dst, PS[:, o % 2, :], rstd[:], MUL, lane.leaves(o))

            for m in range(KT):
                split_low(0, m, True, 0)
            norm_scale(0)

            def finish_qkv(o):
                if o < 12:
                    tt(rt[:], tmp[o % 2][:], table1[:, 0:T], MUL)
                    dve.wait_ge(S("rotated"), o + 1)
                    tt(tmp[o % 2][:], PS[:, 2 + o % 2, :], table1[:, T:2 * T], MUL)
                    tt(aq[:, o, :], rt[:], tmp[o % 2][:], ADD, "roped")
                else:
                    i = o - 12
                    dve.wait_ge(S("v_turned"), i + 1)
                    copy(av[:, :, i // 2, (i % 2) * P:(i % 2 + 1) * P], blk(PS[:, 4 + o % 2, :]), "v_token")

            dve.wait_ge(S("table1_in"), 16)
            for o in range(N_QKV):
                evict(O_QKV + o, U_QKV + o, tmp[o % 2][:])
                if o:
                    finish_qkv(o - 1)
            finish_qkv(N_QKV - 1)

            dve.wait_ge(S("masks1_in"), 16)
            for i in range(16 + 1):
                if i < 16:
                    r, p = i // 4, 4 * (i % 2)
                    dve.wait_ge(S("scores"), i + 1)
                    if i >= 2:
                        dve.wait_ge(S("probs_turned"), i - 1)
                    b = 2 + 2 * (i % 2)
                    lane.do(nc.vector.tensor_tensor_reduce(
                        out=sp1[i % 2][:], in0=flat(PS[:, b:b + 2, :])[:, 0:768],
                        in1=masks1[:, r * 768:(r + 1) * 768], scale=1.0, scalar=NEG, op0=ADD, op1=ALU.max,
                        accum_out=st[:, p:p + 1]), "masked")
                    ts(st[:, p + 1:p + 2], st[:, p:p + 1], -0.125, MUL, "neg_max")
                if i >= 1:
                    p = 4 * ((i - 1) % 2)
                    dve.wait_ge(S("exp1"), i)
                    recip(st[:, p + 3:p + 4], st[:, p + 2:p + 3])
                    ts(sp1[(i - 1) % 2][:], sp1[(i - 1) % 2][:], st[:, p + 3:p + 4], MUL, "probs")
            for m in range(2):
                dve.wait_ge(S("o_high"), m + 1)
                tt(OL[:, m, :], oA[:, m, :], OH[:, m, :].bitcast(F32), SUB, "o_low")

            for z in zp:
                lane.do(nc.vector.memset(z[:, 0:1], 0.0))
            lane.do(nc.vector.memset(PP[:, :, 0:1], 1.0))
            lane.do(nc.vector.memset(omka[:], 0.0))
            ts(omka[:, 0:4], par[:, PARAM_COLS["k_a"]:PARAM_COLS["k_a"] + 4], -1.0, MUL, s2=1.0, op2=ADD)

            def shift(b, j, out, name="chain"):
                tt(tmp[0][:], zp[b][:, 0:T], zp[b][:, 1:T + 1], SUB)
                stt(out, tmp[0][:], col("mu", j), zp[b][:, 1:T + 1], MUL, ADD, name)

            def evict_rkv(hp):
                for b in range(3):
                    evict(O_RWKV + 2 + 3 * hp + b, U_RKV + 3 * hp + b, zp[b][:, 1:T + 1])

            evict(O_RWKV, U_LORA, zp[0][:, 1:T + 1])
            evict(O_RWKV + 1, U_LORA + 1, zp[1][:, 1:T + 1])
            shift(0, 12, la[:], "lora_shifted")
            shift(1, 13, lg[:], "lora_shifted")
            evict_rkv(0)
            rs, ks = wkC[:, 0:T], wkC[:, T:2 * T]
            decay, aa = wkA[:, 0:T], wkA[:, T:2 * T]
            kk, ip = wkB[:, 0:T], wkB[:, T:2 * T]
            G, H, St = blk(wkA[:]), blk(wkB[:]), blk(wkC[:])

            def ch(x):
                return x.rearrange("p (c t) -> p c t", c=8)

            dve.wait_ge(S("scan_consts_in"), 64)
            for hp in range(4):
                shift(0, hp, rs)
                shift(1, 4 + hp, ks)
                shift(2, 8 + hp, vs[:])
                ts(kk, ks, col("k_k", hp), MUL, "kk_raw")
                dve.wait_ge(S("lora_used"), 4 * hp + 2)
                ts(tmp[0][:], aa, col("k_a", hp), MUL, s2=omka[:, hp:hp + 1], op2=ADD)
                tt(ks, ks, tmp[0][:], MUL)
                stt(tmp[1][:], rs, col("r_k", hp), ks, MUL, MUL, "rk_ready")
                dve.wait_ge(S("k_root"), hp + 1)
                ts(sq[:], sq[:], 1e-12, ALU.max)
                recip(sq[:], sq[:])
                tt(kk, kk, sq[:], MUL)
                dve.wait_ge(S("rk_summed"), hp + 1)
                tt(bonus[:], PS[:, 6, :], vs[:], MUL)
                dve.wait_ge(S("lora_used"), 4 * hp + 4)
                for c in range(8):
                    lane.do(nc.vector.tensor_tensor_scan(
                        PP[:, c, 1:65], decay[:, 64 * c:64 * c + 64], omka[:, 4:68], 1.0, MUL, ADD))
                tt(ch(FR[:]), ch(rs), PP[:, :, 1:65], MUL, "scaled")
                lane.do(nc.vector.reciprocal(ch(ip), PP[:, :, 1:65]))
                stt(ch(FA[:]), ch(kk), -1.0, PP[:, :, 0:64], MUL, MUL, "scaled")
                tt(tmp[0][:], kk, aa, MUL)
                tt(FB[:], tmp[0][:], ip, MUL, "scaled")
                tt(FK[:], ks, ip, MUL, "scaled")
                if hp < 3:
                    evict_rkv(hp + 1)
                dve.wait_ge(S("turned"), 4 * hp + 3)
                copy(Kt[:], blk(PS[:, 4, :]), "token_d")
                dve.wait_ge(S("turned"), 4 * hp + 4)
                copy(Vt[:], blk(PS[:, 5, :]), "token_d")
                for e in range(2):
                    dve.wait_ge(S("lower_done"), 2 * hp + e + 1)
                    tt(blk(X[:, e, :]), blk(PS[:, 2 + 2 * e, :]), over(K_["pair_lower"]), MUL)
                    tt(blk(X[:, e, :]), blk(X[:, e, :]), over(M["ident"]), ADD)
                    tt(blk(Lt[:, e, :]), blk(PS[:, 3 + 2 * e, :]), over(K_["before"]), MUL)
                    tt(blk(Y[:, e, :]), blk(Lt[:, e, :]), over(K_["pair_upper"]), MUL)
                    tt(blk(Y[:, e, :]), blk(Y[:, e, :]), over(M["ident"]), ADD, "inverse_ready")
                for l in range(1, 6):
                    for e in range(2):
                        dve.wait_ge(S("lx_done"), 10 * hp + 2 * (l - 1) + e + 1)
                        tt(blk(Z[:, e, :]), blk(PS[:, 6 + e, :]), over(K_[f"lvl{l}"]), MUL, "lx_masked")
                    for e in range(2):
                        dve.wait_ge(S("xlx_done"), 10 * hp + 2 * (l - 1) + e + 1)
                        if l < 5:
                            tt(X[:, e, :], X[:, e, :], PS[:, 2 + e, :], ADD)
                        tt(Y[:, e, :], Y[:, e, :], PS[:, 4 + e, :], ADD, "inverse_ready")
                for n, (dst, mask) in enumerate((((Lt[:, 0, :], Lt[:, 1, :]), "before"),
                                                 ((X[:, 0, :], X[:, 1, :]), "upto"), ((FA[:], FB[:]), "upto"))):
                    for e in range(2):
                        dve.wait_ge(S("pairs_done"), 6 * hp + 2 * n + e + 1)
                        tt(blk(dst[e]), blk(PS[:, 2 + 2 * n + e, :]), over(K_[mask]), MUL, "pairs_masked")
                dve.wait_ge(S("qy_done"), hp + 1)
                tt(FR[:], FR[:], PS[:, 6, :], ADD, "q_ready")
                dve.wait_ge(S("chunks_done"), hp + 1)
                for lo, src in ((2, blk(PS[:, 2, :])[:, 1:4, :]), (1, blk(PS[:, 3, :])[:, 0:3, :])):
                    tt(G[:, lo:lo + 5:2, :], src, over(M["head_ones"], 3), MUL)
                    tt(G[:, lo:lo + 5:2, :], G[:, lo:lo + 5:2, :], over(M["ident"], 3), ADD)
                for c in range(7):
                    stt(H[:, c, :], PS[:, 4 + c % 2, (c // 2) * P:(c // 2 + 1) * P], PP[:, c, 64:65], M["head_ones"],
                        MUL, MUL, "chunks_ready" if c == 6 else "chain")
                for c in range(1, 7):
                    dve.wait_ge(S("state_done"), 6 * hp + c)
                    stt(St[:, c + 1, :], PS[:, 6 + c % 2, 0:P], PP[:, c, 64:65], H[:, c, :], MUL, ADD, "state_ready")
                dve.wait_ge(S("y_done"), hp + 1)
                dve.wait_ge(S("y0_ready"), hp + 1)
                tt(FK[:, 64:T], FK[:, 64:T], PS[:, 2, 64:T], ADD, "y_ready")
                dve.wait_ge(S("mean_done"), hp + 1)
                tt(tmp[0][:], FK[:], PS[:, 3, :], SUB, "y_centered")
                dve.wait_ge(S("y_root"), hp + 1)
                recip(sq[:], sq[:])
                tt(tmp[0][:], tmp[0][:], sq[:], MUL)
                ts(tmp[0][:], tmp[0][:], col("ln_w", hp), MUL, s2=col("ln_b", hp), op2=ADD)
                tt(tmp[0][:], tmp[0][:], bonus[:], ADD)
                tt(tmp[1][:], tmp[0][:], gt[:], MUL, "y_final")
                dve.wait_ge(S("y_high"), hp + 1)
                tt(YL[:, hp, :], tmp[1][:], YH[:, hp, :].bitcast(F32), SUB, "rwkv_out")

            for m in range(2):
                dve.wait_ge(S("p_high"), m + 1)
                tt(PL[:, m, :], pf[:, m, :], PH[:, m, :].bitcast(F32), SUB, "p_low")

            def merge(o, u, m, base, step, first, second, high, low):
                evict(o, u, tmp[0][:])
                evict(o + 1, u + 1, tmp[1][:])
                if step == 3:
                    dve.wait_ge(S("units_done"), u + 3)
                dve.wait_ge(S("gated"), 2 * (base + m) + 1)
                tt(tmp[0][:], tmp[0][:], first, MUL)
                dve.wait_ge(S("gated"), 2 * (base + m) + 2)
                tt(tmp[1][:], tmp[1][:], second, MUL)
                tt(tmp[0][:], tmp[0][:], tmp[1][:], ADD, "merged")
                dve.wait_ge(S("merged_high"), base + m + 1)
                tt(low[:, m, :], tmp[0][:], high[:, m, :].bitcast(F32), SUB, "merged_low")

            for m in range(KT):
                b = 2 + 3 * (m % 2)
                merge(O_GATE + 2 * m, U_MERGE + 3 * m, m, 0, 3, PS[:, b, :], PS[:, b + 1, :], MH, ML)
            for m in range(KT):
                add_squares(1, m)
            norm_scale(1)

            def update(m, gain):
                stt(t8[:, m, :], t8[:, m, :], col(gain, m), rstd[:], MUL, MUL)
                tt(h[:, m, :], h[:, m, :], t8[:, m, :], ADD, "h_new")

            def update_all(post, n, gain, norm):
                for m in range(KT):
                    update(m, post)
                    if m:
                        split_low(n, m - 1, gain, norm)
                split_low(n, KT - 1, gain, norm)

            def feed_forward(U, O, low, high, dst, hid, norm, add_first):
                lows = low[:].rearrange("p (g j) t -> p g j t", j=4)
                highs = high[:].rearrange("p (g j) t -> p g j t", j=4)
                outs = dst[:].rearrange("p (g j) t -> p g j t", j=2)
                for half in range(2):
                    u, o = U + 32 * half, O + 24 * half
                    with lane.loop(4, {"out_evicted0": 2, "out_evicted1": 2, "hidden_low": 4}) as g:
                        for j in range(4):
                            dve.wait_ge(S("units_done"), g * 4 + (u + j + 1))
                            stt(tmp[j % 2][:], PS[:, (o + j) % 2, :], 0.0, rstd[:], ALU.max, MUL,
                                lane.leaves(o + j))
                            dve.wait_ge(S("hidden_high"), g * 4 + (hid + 16 * half + j + 1))
                            tt(lows[:, g, j, :], tmp[j % 2][:], highs[:, g, j, :].bitcast(F32), SUB, "hidden_low")
                    u, o = u + 16, o + 16
                    if half:
                        lane.do(nc.vector.memset(acc[:], 0.0))
                    with lane.loop(4, {"out_evicted0": 1, "out_evicted1": 1} | ({"squares_summed": 2} if half else {})) as g:
                        for j in range(2):
                            dve.wait_ge(S("units_done"), g * 4 + (u + 2 * j + 2))
                            d = outs[:, g, j, :]
                            if half or add_first:
                                tt(d, d, PS[:, (o + j) % 2, :], ADD, lane.leaves(o + j))
                            else:
                                copy(d, PS[:, (o + j) % 2, :], lane.leaves(o + j))
                            if half:
                                dve.wait_ge(S("squared"), g * 2 + (KT * norm + j + 1))
                                tt(acc[:], acc[:], sq[:], ADD, "squares_summed")
                norm_scale(norm)

            update_all("mix_post", 1, True, 2)
            norm_scale(2)
            feed_forward(U_FFN, O_FFN, FL, FH, t8, 0, 3, False)
            update_all("ffn_post", 2, False, None)

            dve.wait_ge(S("block2_in"), 96)
            cosv, sinv = table2[:, 0:T], table2[:, T:2 * T]
            two_pi = 2 * np.pi
            c1 = 6.28125
            c2 = float(np.float32(np.floor((two_pi - c1) * 2 ** 20) / 2 ** 20))
            c3 = float(two_pi - c1 - c2)
            magic = 1.5 * 2 ** 23
            copy(cosv, pos[:])
            ts(cosv, cosv, small[:, 0:1], MUL)
            ts(rt2[:], cosv, float(1 / two_pi), MUL, s2=magic, op2=ADD)
            ts(rt2[:], rt2[:], -magic, ADD)
            for c in (c1, c2, c3):
                stt(cosv, rt2[:], -c, cosv, MUL, ADD)
            ts(sinv, cosv, 3.1415925, ALU.min, s2=-3.1415925, op2=ALU.max, name="angles")
            stt(cosv, sinv, -1.0, sinv, MUL, ALU.max)
            ts(cosv, cosv, -1.0, MUL, s2=float(np.pi / 2), op2=ADD, name="angles")
            for j in range(2):
                lane.do(nc.vector.tensor_tensor_reduce(
                    out=lam4[:, 2 * j, :], in0=lam4[:, 2 * j, :], in1=lam4[:, 2 * j + 1, :], scale=1.0, scalar=0.0,
                    op0=MUL, op1=ADD, accum_out=lamw[:, j:j + 1]), "lam_dots")

            plev = ple[:].rearrange("p (g j) t -> p g j t", j=4)
            t8v = t8[:].rearrange("p (g j) t -> p g j t", j=4)
            lane.do(nc.vector.memset(acc[:], 0.0))
            with lane.loop(2, {"e_new": 4, "squares_summed": 4}) as g:
                for j in range(4):
                    dve.wait_ge(S(f"out_evicted{j % 2}"), g * 2 + ((O_PLE + j) // 2 + 1))
                    tt(t8v[:, g, j, :], tmp[j % 2][:], plev[:, g, j, :], MUL, "e_new")
                    dve.wait_ge(S("squared"), g * 4 + (KT * 4 + j + 1))
                    tt(acc[:], acc[:], sq[:], ADD, "squares_summed")
            norm_scale(4)
            dve.wait_ge(S("lam_exp"), 1)
            tt(lamw[:, 4:5], lamw[:, 2:3], lamw[:, 3:4], SUB)
            ts(lamw[:, 5:6], lamw[:, 4:5], LAM_INIT, ADD, s2=-1.0, op2=MUL)
            ts(lamw[:, 6:7], col("subln"), 1.0 - LAM_INIT, MUL)

            update_all("ple_post", 3, True, 5)
            norm_scale(5)

            def finish_head(o):
                n = o // 3
                dve.wait_ge(S("head_turned"), o + 1)
                if o % 3 == 2:
                    copy(v2[n % 2][:], blk(PS[:, 2, :]), "head_input")
                else:
                    tt(rt2[:], tmp[o % 2][:], cosv, MUL)
                    tt(tmp[o % 2][:], PS[:, 2, :], sinv, MUL)
                    tt((q2, k2)[o % 3][n % 2][:], rt2[:], tmp[o % 2][:], ADD, "head_input")

            dve.wait_ge(S("table2"), 2)
            for o in range(3):
                evict(O_HEADS + o, U_HEADS + o, tmp[o % 2][:])
                finish_head(o)
            for i in range(32 + 2):
                n, qt = i // 4, i % 4
                if i < 32:
                    p, w = i % 2, P * (qt + 1)
                    dve.wait_ge(S("scores2"), i + 1)
                    if i >= 2:
                        dve.wait_ge(S("weights_turned"), i - 1)
                    for c in range(2):
                        lane.do(nc.vector.tensor_tensor_reduce(
                            out=e2[p][:, c, 0:w], in0=PS[:, 4 + c, 0:w], in1=causal[:, T - w:T], scale=1.0,
                            scalar=NEG, op0=ADD, op1=ALU.max, accum_out=st2[:, p, c:c + 1]), "masked2")
                    ts(st2[:, p, 2:4], st2[:, p, 0:2], -0.125, MUL, "neg_max2")
                if n < 7 and qt >= 1:
                    finish_head(3 * (n + 1) + qt - 1)
                if 1 <= i < 33:
                    p, w = (i - 1) % 2, P * ((i - 1) % 4 + 1)
                    dve.wait_ge(S("exp2"), 2 * i)
                    recip(st2[:, p, 6:8], st2[:, p, 4:6])
                    tt(st2[:, p, 7:8], st2[:, p, 7:8], lamw[:, 5:6], MUL)
                    ts(e2[p][:, 1, 0:w], e2[p][:, 1, 0:w], st2[:, p, 7:8], MUL)
                    stt(e2[p][:, 0, 0:w], e2[p][:, 0, 0:w], st2[:, p, 6:7], e2[p][:, 1, 0:w], MUL, ADD, "weights2")
                if n < 7 and qt < 3:
                    o = 3 * (n + 1) + qt
                    evict(O_HEADS + o, U_HEADS + o, tmp[o % 2][:])
                if i >= 2 and i % 4 == 1:
                    n = (i - 2) // 4
                    dve.wait_ge(S("a_root"), n + 1)
                    recip(sq[:], sq[:])
                    stt(aT[:, n, :], aT[:, n, :], lamw[:, 6:7], sq[:], MUL, MUL)

            for z in (pz, pa, pb):
                lane.do(nc.vector.memset(z[:, 0:16], 0.0))
            for j, w in enumerate((2, 4, 8, 16)):
                if j:
                    dve.wait_ge(S("pool_high"), j)
                evict(O_POOL + j, U_POOL + j, pz[:, 16:16 + T])
                cur = pz
                for l in range(j + 1):
                    nxt = (pa, pb)[l % 2]
                    tt(nxt[:, 16:16 + T], cur[:, 16:16 + T], cur[:, 16 - 2 ** l:16 - 2 ** l + T], ADD)
                    cur = nxt
                tt(cur[:, 16:32], cur[:, 16:32], small[:, 4 + 16 * j:20 + 16 * j], MUL)
                ts(cur[:, 32:16 + T], cur[:, 32:16 + T], 1.0 / w, MUL)
                tt(pz[:, 16:16 + T], cur[:, 16:16 + T], pz[:, 16:16 + T], SUB, "pool_diff")
                dve.wait_ge(S("pool_high"), j + 1)
                tt(DL[:, j, :], pz[:, 16:16 + T], DH[:, j, :].bitcast(F32), SUB, "pooled_low")

            for m in range(KT):
                dve.wait_ge(S("pool_copied"), m + 1)
                merge(O_GATE2 + 2 * m, U_GATE2 + 2 * m, m, KT, 2, aT[:, m, :], poolT[:, m, :], M2H, M2L)
            for m in range(KT):
                o = O_OUT2 + m
                dve.wait_ge(S("units_done"), U_OUT2 + m + 1)
                tt(h[:, m, :], h[:, m, :], PS[:, o % 2, :], ADD, lane.leaves(o))
                if m:
                    split_low(4, m - 1, True, 6)
            split_low(4, KT - 1, True, 6)
            norm_scale(6)
            feed_forward(U_FFN2, O_FFN2, F2L, F2H, h, 32, 7, True)
            for m in range(KT):
                stt(h[:, m, :], h[:, m, :], col("final", m), rstd[:], MUL, MUL, "final")


def kernel(**inputs):
    import concourse.bacc as bacc
    from concourse.bass_utils import run_bass_kernel_spmd

    x = {k: np.asarray(v) for k, v in inputs.items()}
    w_in, w_in2 = x["w_in"][0], x["w_in_2"][0]

    def unit(w, c, n=P):
        w = w[:, c:c + n]
        if n < P:
            w = np.concatenate([w, np.zeros((D, P - n), w.dtype)], 1)
        return w.reshape(KT, P, P).transpose(1, 0, 2)

    units = [unit(w_in, P * j) for j in range(N_QKV)]
    rw = 9 * 256
    units += [unit(w_in, rw + 1536, 64), unit(w_in, rw + 1600, 96)]
    units += [unit(w_in, rw + 512 * j + P * hp) for hp in range(4) for j in range(3)]
    gate = rw + 1696
    for m in range(KT):
        c = slice(P * m, P * (m + 1))
        up = np.concatenate([x["w_attn_up"][0][:, c], x["w_rwkv_up"][0][:, c], x["w_ple"][0][:, c]], 0)
        units += [unit(w_in, gate + P * m), unit(w_in, gate + D + P * m), unit(up, 0)]

    def feed_forward(w_up, w_down):
        for half in range(2):
            for j in range(16):
                yield unit(w_up, P * (16 * half + j))
            for m in range(KT):
                for w in range(2):
                    yield unit(w_down[2048 * half + 1024 * w:2048 * half + 1024 * (w + 1)], P * m)

    units += [unit(x["w_out"][0], P * m) for m in range(KT)]
    units += list(feed_forward(x["w_ff_in"][0], x["w_ff_out"][0]))
    units += [unit(x["w_ple_gate"][0], P * m) for m in range(KT)]
    units += [unit(w_in2, D * j + P * n) for n in range(8) for j in range(3)]
    units += [unit(w_in2, 3 * D + P * j) for j in range(4)]
    units += [x["w_pool_2"][0].reshape(4, P, 2, P).transpose(1, 0, 2, 3).reshape(P, KT, P)]
    units += [unit(w_in2, 3584 + D * j + P * m) for m in range(KT) for j in range(2)]
    units += [unit(x["w_out_2"][0], P * m) for m in range(KT)]
    units += list(feed_forward(x["w_up_2"][0], x["w_down_2"][0]))
    assert len(units) == N_UNITS

    mu = x["rwkv_mu"][0]
    mu = np.concatenate([mu[:1600], np.zeros(64, mu.dtype), mu[1600:], np.zeros(32, mu.dtype)])
    cols = {"mix_pre": "mix_pre_norm", "mix_post": "mix_post_norm", "ffn_pre": "ffn_pre_norm",
            "ffn_post": "ffn_post_norm", "ple_post": "ple_post_norm", "attn2": "norm_attn_g_2",
            "mlp2": "norm_mlp_g_2", "final": "final_norm_g_2", "pool_scale": "pool_scale_2", "w0": "rwkv_w0",
            "a0": "rwkv_a0", "k_k": "rwkv_k_k", "k_a": "rwkv_k_a", "r_k": "rwkv_r_k", "ln_w": "rwkv_ln_w",
            "ln_b": "rwkv_ln_b", "subln": "subln_g_2"}
    params = np.concatenate([(mu if n == "mu" else x[cols[n]]).reshape(-1, P).T for n in PARAM_COLS], 1)
    arrays = {
        "w": np.stack(units), "params": params,
        "x": x["x"][0].T.reshape(KT, P, T).transpose(1, 0, 2), "p": x["p"][0, 0].T.reshape(2, P, T).transpose(1, 0, 2),
        "w2": x["rwkv_w2"][0], "a2": x["rwkv_a2"][0], "g2": x["rwkv_g2"][0], "positions": x["positions_2"],
        "lam0": x["lam_q1_2"], "lam1": x["lam_k1_2"], "lam2": x["lam_q2_2"], "lam3": x["lam_k2_2"],
        **shape_constants(),
    }
    arrays = {k: np.ascontiguousarray(v) for k, v in arrays.items()}
    nc = bacc.Bacc("TRN2", target_bir_lowering=False, num_devices=1)
    aps = {k: nc.dram_tensor(f"in_{k}", v.shape, mybir.dt.from_np(v.dtype), kind="ExternalInput").ap()
           for k, v in arrays.items()}
    aps["out"] = nc.dram_tensor("out_0", (P, KT, T), F32, kind="ExternalOutput").ap()
    build(nc, aps)
    result = run_bass_kernel_spmd(nc, [{f"in_{k}": v for k, v in arrays.items()}], core_ids=[0])
    out = result.results[0]["out_0"]
    return out.transpose(1, 0, 2).reshape(D, T).T.reshape(1, T, D)
```

```python
from contextlib import ExitStack, contextmanager

import numpy as np

import concourse.bass as bass
from concourse import mybir

F32 = mybir.dt.float32
F32R = mybir.dt.float32r
I32 = mybir.dt.int32
ALU = mybir.AluOpType
ACT = mybir.ActivationFunctionType

P = 128
T = 512
D = 1024
KT = D // P
NT = T // P
HD = 64
DFF = 4 * D
EPS = 1e-6
GN_EPS = 64e-5
NEG = -1.0e30

N_QKV = 18
N_RWKV = 14
U_QKV = 0
U_LORA = U_QKV + N_QKV
U_RKV = U_LORA + 2
U_GATE = U_LORA + N_RWKV
U_UP = U_GATE + 2 * KT
U_OUT = U_UP + KT
U_FFN = U_OUT + KT
U_PLE = U_FFN + 64
U_HEADS = U_PLE + KT
U_STEP = U_HEADS + 3
U_GATE2 = U_STEP + 32
N_EARLY = 6
U_OUT2 = U_GATE2 + 2 * KT - N_EARLY
U_FFN2 = U_OUT2 + KT
N_UNITS = U_FFN2 + 64
RING = 4

O_QKV = 0
O_RWKV = O_QKV + N_QKV
O_GATE = O_RWKV + N_RWKV
O_OUT = O_GATE + 2 * KT
O_FFN = O_OUT + KT
O_PLE = O_FFN + 48
O_HEADS = O_PLE + KT
O_GATE2 = O_HEADS + 3 + 31
O_OUT2 = O_GATE2 + 2 * KT - N_EARLY
O_FFN2 = O_OUT2 + KT

POOLW_STEP = 19


def step_unit(i):
    n, qt = i // 4, i % 4
    if n == 7:
        kind = ("gate", 2 + qt)
    elif qt < 3:
        kind = ("head", 3 * (n + 1) + qt)
    elif n < 4:
        kind = ("pool", n)
    else:
        kind = ("pool_weights", 0) if n == 4 else ("gate", n - 5)
    return kind, O_HEADS + 3 + i - (i > POOLW_STEP)


PARAM_COLS = {}


def _columns():
    at = 0
    for name, n in (("mix_pre", 8), ("mix_post", 8), ("ffn_pre", 8), ("ffn_post", 8), ("ple_post", 8),
                    ("attn2", 8), ("mlp2", 8), ("final", 8), ("pool_scale", 8), ("mu", 14), ("w0", 4),
                    ("a0", 4), ("k_k", 4), ("k_a", 4), ("r_k", 4), ("ln_w", 4), ("ln_b", 4), ("subln", 1)):
        PARAM_COLS[name] = at
        at += n
    return at


N_PARAMS = _columns()

MATS = ("ident", "ones", "head_ones", "head_mean")
SCAN_MASKS = ("pair_lower", "pair_upper", "before", "upto", "lvl1", "lvl2", "lvl3", "lvl4", "lvl5")
LAM_INIT = 0.8 - 0.6 * float(np.exp(-0.0))


def shape_constants():
    i = np.arange(P)
    m = {"ident": np.eye(P), "ones": np.ones((P, P))}
    same_head = (i[:, None] // HD == i[None, :] // HD).astype(float)
    m["head_ones"], m["head_mean"] = same_head, same_head / HD
    r1, r2 = np.zeros((P, P)), np.zeros((P, P))
    for b in (0, 64):
        for j in range(32):
            r1[b + j, b + j + 32], r1[b + j + 32, b + j] = -1, 1
        for j in range(8):
            r2[b + j, b + j + 8], r2[b + j + 8, b + j] = -1, 1
    m["rot1"], m["rot2"] = r1.T, r2.T
    row, col = i[:, None], i[None, :]
    m["pair_lower"] = ((row == col + 1) & (col % 2 == 0)).astype(float)
    m["pair_upper"] = m["pair_lower"].T
    chunk = row // 64 == col // 64
    m["before"] = (chunk & (row < col)).astype(float)
    m["upto"] = (chunk & (row <= col)).astype(float)
    for l in range(1, 6):
        b = 2 ** l
        m[f"lvl{l}"] = ((row // (2 * b) == col // (2 * b)) & (row // b % 2 == 1) & (col // b % 2 == 0)).astype(float)
    mats = np.concatenate([m[n] for n in MATS], 1)
    scan_masks = np.concatenate([m[n] for n in SCAN_MASKS], 1)

    q = 4 * i[:, None]
    key = np.arange(T)[None, :]
    by4 = np.where(col <= row, 0.0, NEG)
    by16 = np.where((col <= row) & (col % 4 == row % 4), 0.0, NEG)
    masks = []
    for r in range(4):
        d = q + r - key
        masks += [np.where((d >= 0) & (d <= 128), 0.0, NEG), by4, by16]
    causal = np.where(key <= i[:, None] + 384, 0.0, NEG)
    f = i % HD
    inv1 = (10000.0 ** (-np.arange(0, HD, 2, dtype=np.float32) / np.float32(HD))).astype(np.float32)
    ang = (np.arange(T, dtype=np.float32)[None, :] * inv1[f % 32][:, None]).astype(np.float32).astype(np.float64)
    table1 = np.concatenate([np.cos(ang), np.sin(ang)], 1)
    inv2 = (500000.0 ** (-np.arange(0, 16, 2, dtype=np.float32) / np.float32(16))).astype(np.float32)
    invf2 = np.where(f < 16, inv2[f % 8], 0.0)
    small = np.zeros((P, 68))
    small[:, 0], small[:, 1], small[:, 2] = invf2, EPS, GN_EPS
    for g, w in enumerate((2, 4, 8, 16)):
        small[:, 4 + 16 * g:20 + 16 * g] = 1.0 / np.minimum(np.arange(16) + 1, w)
    c = np.ascontiguousarray
    f32 = np.float32
    return {"mats": c(mats, f32), "scan_masks": c(scan_masks, f32), "masks1": c(np.concatenate(masks, 1), f32),
            "causal": c(causal, f32), "table1": c(table1, f32), "rot1": c(m["rot1"], f32), "rot2": c(m["rot2"], f32), "small": c(small, f32)}


class Lane:

    def __init__(self, eng, sem, name):
        self.eng, self.sem, self.eng_name = eng, sem, name
        self.count, self.turn, self.each = {}, None, {}

    def value(self, name):
        n = self.count[name]
        return n + self.turn * self.each[name] if self.turn is not None else n

    def do(self, instruction, name="chain"):
        name = f"{self.eng_name}_{name}" if name == "chain" else name
        self.count[name] = self.count.get(name, 0) + 1
        instruction.then_inc(self.sem(name), 1)
        self.eng.wait_ge(self.sem(name), self.value(name))

    def leaves(self, o):
        name = f"out_evicted{o % 2}"
        self.count[name] = o // 2
        return name

    @contextmanager
    def loop(self, turns, each):
        each = {(f"{self.eng_name}_chain" if k == "chain" else k): v for k, v in each.items()}
        before = dict(self.count)
        with self.eng.Fori(0, turns, 1) as g:
            self.turn, self.each = g, each
            yield g
        self.turn = None
        for k in [k for k in each if not k.startswith("out_evicted")]:
            assert self.count[k] - before.get(k, 0) == each[k], (k, self.count[k], before.get(k), each[k])
            self.count[k] += each[k] * (turns - 1)


def build(nc, a):
    ctx = ExitStack()
    with ctx:
        sems = {}

        def S(name):
            if name not in sems:
                sems[name] = ctx.enter_context(nc.semaphore(name))
            return sems[name]

        def sbuf(stack, name, shape, dt=F32):
            return stack.enter_context(nc.sbuf_tensor(name, shape, dt))

        h = sbuf(ctx, "h", [P, KT, T])
        raw = [sbuf(ctx, f"raw{i}", [P, KT, P]) for i in range(RING)]
        WH = [sbuf(ctx, f"w_high{i}", [P, KT, P], F32R) for i in range(RING)]
        WL = [sbuf(ctx, f"w_low{i}", [P, KT, P], F32R) for i in range(RING)]
        UH = sbuf(ctx, "u_high", [P, KT, T], F32R)
        UL = sbuf(ctx, "u_low", [P, KT, T], F32R)
        par = sbuf(ctx, "params", [P, N_PARAMS])
        mats = sbuf(ctx, "mats", [P, len(MATS) * P])
        small = sbuf(ctx, "small", [P, 68])
        rstd = sbuf(ctx, "rstd", [P, T])
        acc = sbuf(ctx, "acc", [P, T])
        sq = sbuf(ctx, "sq", [P, T])
        tmp = [sbuf(ctx, f"tmp{i}", [P, T]) for i in range(2)]
        PS = ctx.enter_context(nc.psum_tensor("PS", [P, 8, 512], F32))

        M = {n: mats[:, i * P:(i + 1) * P] for i, n in enumerate(MATS)}

        def col(name, j=0):
            return par[:, PARAM_COLS[name] + j:PARAM_COLS[name] + j + 1]

        def over(m, n=NT):
            return m.unsqueeze(1).to_broadcast([P, n, P])

        def blk(x):
            return x.rearrange("p (a b) -> p a b", b=P)

        mix = ExitStack()
        OH = sbuf(mix, "o_high", [P, 2, T], F32R)
        OL = sbuf(mix, "o_low", [P, 2, T], F32R)

        att = ExitStack()
        aq = sbuf(att, "qk1", [P, 12, T])
        av = sbuf(att, "v1", [P, NT, 3, 256])
        table1 = sbuf(att, "table1", [P, 2 * T])
        rot1 = sbuf(att, "rotation1", [P, P])
        masks1 = sbuf(att, "masks1", [P, 4 * 768])
        sp1 = [sbuf(att, f"probs1_{i}", [P, 768]) for i in range(2)]
        pt1 = [sbuf(att, f"probsT1_{i}", [P, 768]) for i in range(2)]
        oA = sbuf(att, "o1", [P, 2, T])
        st = sbuf(att, "stats1", [P, 8])
        rt = sbuf(att, "rope_tmp", [P, T])
        zs = [sbuf(att, f"z_out{i}", [P, T]) for i in range(2)]
        att.close()

        YH = sbuf(mix, "y_high", [P, 4, T], F32R)
        YL = sbuf(mix, "y_low", [P, 4, T], F32R)
        rw = ExitStack()
        smask = sbuf(rw, "scan_masks", [P, len(SCAN_MASKS) * P])
        K_ = {n: smask[:, i * P:(i + 1) * P] for i, n in enumerate(SCAN_MASKS)}
        lora_w = sbuf(rw, "lora_w", [P, 512])
        lora_g = sbuf(rw, "lora_g", [P, 512])
        zp = [sbuf(rw, f"z_padded{i}", [P, T + 1]) for i in range(3)]
        la = sbuf(rw, "lora_in", [P, T])
        lg = sbuf(rw, "lora_gate", [P, T])
        wkA = sbuf(rw, "work_a", [P, 2 * T])
        wkB = sbuf(rw, "work_b", [P, 2 * T])
        wkC = sbuf(rw, "work_c", [P, 2 * T])
        vs = sbuf(rw, "v_feature", [P, T])
        gt = sbuf(rw, "gate_feature", [P, T])
        PP = sbuf(rw, "decay_product", [P, 8, 65])
        FR, FA, FB, FK = (sbuf(rw, n, [P, T]) for n in ("r_scaled", "a_scaled", "b_scaled", "k_scaled"))
        bonus = acc
        RHS = sbuf(rw, "a_and_mv", [P, 2, NT, P])
        Bt, Kt, Vt = (sbuf(rw, n, [P, NT, P]) for n in ("b_token", "k_token", "v_token"))
        Lt, X, Y, Z = (sbuf(rw, n, [P, 2, T]) for n in ("lower_T", "inverse", "inverse_T", "product"))
        gs = [sbuf(rw, f"gate_out{i}", [P, T]) for i in range(2)]
        omka = sbuf(rw, "one_minus_ka", [P, 4 + 64])
        rw.close()

        late = ExitStack()
        ple = late.enter_context(nc.sbuf_tensor("ple", [P, KT, T], F32, side="right"))
        PH = sbuf(mix, "p_high", [P, 2, T], F32R)
        PL = sbuf(mix, "p_low", [P, 2, T], F32R)
        pf = sbuf(mix, "p_in", [P, 2, T])
        mg = ExitStack()
        MH = sbuf(mg, "merged_high", [P, KT, T], F32R)
        ML = sbuf(mg, "merged_low", [P, KT, T], F32R)
        gin = [sbuf(mg, f"gate_in{i}", [P, T]) for i in range(4)]
        mg.close()
        mix.close()

        ff = ExitStack()
        t8 = sbuf(ff, "branch_out", [P, KT, T])
        FH = sbuf(ff, "hidden_high", [P, 16, T], F32R)
        FL = sbuf(ff, "hidden_low", [P, 16, T], F32R)
        ff.close()
        late.close()

        b2 = ExitStack()
        aT = sbuf(b2, "attn_out2", [P, KT, T])
        poolT = sbuf(b2, "pool_out2", [P, KT, T])
        b2w = ExitStack()
        rot2 = sbuf(b2w, "rotation2", [P, P])
        table2 = sbuf(b2w, "table2", [P, 2 * T])
        causal = sbuf(b2w, "causal", [P, T])
        pos = sbuf(b2w, "positions", [P, T], I32)
        rt2 = sbuf(b2w, "rope_tmp2", [P, T])
        lam4 = sbuf(b2w, "lam_vectors", [P, 4, HD])
        lamw = sbuf(b2w, "lam_work", [P, 8])
        q2 = [sbuf(b2w, f"q2_{i}", [P, T]) for i in range(2)]
        k2 = [sbuf(b2w, f"k2_{i}", [P, T]) for i in range(2)]
        v2 = [sbuf(b2w, f"v2_{i}", [P, NT, P]) for i in range(2)]
        e2 = [sbuf(b2w, f"exp2_{i}", [P, 2, T]) for i in range(2)]
        pt2 = [sbuf(b2w, f"weightsT2_{i}", [P, T]) for i in range(2)]
        st2 = sbuf(b2w, "stats2", [P, 2, 8])
        pz, pa, pb = (sbuf(b2w, n, [P, 16 + T]) for n in ("pool_in", "pool_sum_a", "pool_sum_b"))
        b2p = ExitStack()
        DH = sbuf(b2p, "pool_high", [P, 4, T], F32R)
        DL = sbuf(b2p, "pool_low", [P, 4, T], F32R)
        b2p.close()
        gates2 = sbuf(b2w, "early_gates", [P, N_EARLY, T])
        b2w.close()
        M2H = sbuf(b2, "merged2_high", [P, KT, T], F32R)
        M2L = sbuf(b2, "merged2_low", [P, KT, T], F32R)
        b2.close()
        f2 = ExitStack()
        F2H = sbuf(f2, "hidden2_high", [P, 16, T], F32R)
        F2L = sbuf(f2, "hidden2_low", [P, 16, T], F32R)
        f2.close()

        z_dram = nc.dram_tensor("z_spill", (N_RWKV, P, T), F32, kind="Internal").ap()
        gate_dram = nc.dram_tensor("gate_spill", (2 * KT, P, T), F32, kind="Internal").ap()

        def flat(x):
            return x.rearrange("p a b -> p (a b)")

        def evicted(o):
            return S(f"out_evicted{o % 2}"), o // 2 + 1

        block = ctx.enter_context(nc.Block())

        @block.sync
        def _(sp):
            groups = a["w"][0:(N_UNITS // RING) * RING].rearrange("(g s) p k n -> g s p k n", s=RING)
            for s in range(RING):
                sp.dma_start(raw[s][:], a["w"][s]).then_inc(S(f"raw_in{s}"), 16)
            with sp.Fori(1, N_UNITS // RING, 1) as g:
                for s in range(RING):
                    sp.wait_ge(S("split_done"), g * RING + (s + 1 - RING))
                    sp.dma_start(raw[s][:], groups[g, s]).then_inc(S(f"raw_in{s}"), 16)
            for u in range((N_UNITS // RING) * RING, N_UNITS):
                sp.wait_ge(S("split_done"), u + 1 - RING)
                sp.dma_start(raw[u % RING][:], a["w"][u]).then_inc(S(f"raw_in{u % RING}"), 16)
            sp.wait_ge(S("stored"), 16 * KT)

        @block.gpsimd
        def _(pool):
            lane = Lane(pool, S, "pool")

            def split(s, arrived, free):
                pool.wait_ge(S(f"raw_in{s}"), arrived)
                if free is not None:
                    pool.wait_ge(S("units_done"), free)
                    pool.sem_inc(S("slot_taken"), 1)
                lane.do(nc.gpsimd.tensor_scalar(flat(WH[s][:]), flat(raw[s][:]), 1.0, 0.0, ALU.mult, ALU.add),
                        "split_high")
                nc.gpsimd.tensor_tensor(flat(WL[s][:]), flat(raw[s][:]), flat(WH[s][:]).bitcast(F32),
                                        ALU.subtract).then_inc(S("split_done"), 1)

            for s in range(RING):
                split(s, 16, None)
            lane.count["split_high"] = RING
            with pool.Fori(1, N_UNITS // RING, 1) as g:
                lane.turn, lane.each = g - 1, {"split_high": RING}
                for s in range(RING):
                    split(s, g * 16 + 16, g * RING + (s + 1 - RING))
                lane.turn = None
            lane.count["split_high"] = (N_UNITS // RING) * RING
            for u in range((N_UNITS // RING) * RING, N_UNITS):
                split(u % RING, 16 * (u // RING + 1), u + 1 - RING)

        @block.tensor
        def _(pe):
            def mm(out, lhsT, rhs, start=True, stop=True):
                return nc.tensor.matmul(out, lhsT, rhs, start=start, stop=stop)

            def product(out, s, slices, high, low, wait_slice=None, start=True, stop=True):
                for n, (k, r) in enumerate(slices):
                    if wait_slice is not None:
                        wait_slice(r)
                    first, last = start and n == 0, stop and n == len(slices) - 1
                    mm(out, WH[s][:, k, :], high[:, r, :], first, False)
                    mm(out, WH[s][:, k, :], low[:, r, :], False, False)
                    i = mm(out, WL[s][:, k, :], high[:, r, :], False, last)
                return i

            ALL = [(k, k) for k in range(KT)]

            def unit(u, o, high, low, wait_slice=None):
                pe.wait_ge(S("split_done"), u + 1)
                if u == U_STEP + POOLW_STEP + 1:
                    pe.wait_ge(S("pool_copied"), KT)
                if o >= 2:
                    pe.wait_ge(*evicted(o - 2))
                product(PS[:, o % 2, :], u % RING, ALL, high, low, wait_slice).then_inc(S("units_done"), 1)

            class Filler:

                def __init__(self, u, o, n):
                    self.u, self.o, self.left, self.k = u, o, n * KT, 0

                def slices(self, n):
                    for _ in range(min(n, self.left)):
                        if self.k == 0:
                            pe.wait_ge(S("split_done"), self.u + 1)
                            pe.wait_ge(*evicted(self.o - 2))
                        x = product(PS[:, self.o % 2, :], self.u % RING, [(self.k, self.k)], UH, UL,
                                    start=self.k == 0, stop=self.k == KT - 1)
                        self.k, self.left = self.k + 1, self.left - 1
                        if self.k == KT:
                            x.then_inc(S("units_done"), 1)
                            self.k, self.u, self.o = 0, self.u + 1, self.o + 1

            def units_loop(u, o, n, high, low):
                with pe.Fori(0, n // 4, 1) as g:
                    for j in range(4):
                        pe.wait_ge(S("split_done"), g * 4 + (u + j + 1))
                        pe.wait_ge(S(f"out_evicted{(o + j) % 2}"), g * 2 + (o + j) // 2)
                        product(PS[:, (o + j) % 2, :], (u + j) % RING, ALL, high, low)\
                            .then_inc(S("units_done"), 1)

            def norm_sum(n):
                pe.wait_ge(S("squares_summed"), KT * (n + 1))
                mm(PS[:, 7, :], M["ones"], acc[:]).then_inc(S("norm_summed"), 1)

            def input_split(n):
                return lambda k: pe.wait_ge(S("u_low"), KT * n + k + 1)

            def after_qkv(o):
                pe.wait_ge(*evicted(o))
                if o < 12:
                    if o >= 2:
                        pe.wait_ge(S("roped"), o - 1)
                    mm(PS[:, 2 + o % 2, :], rot1[:], tmp[o % 2][:]).then_inc(S("rotated"), 1)
                else:
                    i = o - 12
                    if i >= 2:
                        pe.wait_ge(S("v_token"), i - 1)
                    for t in range(NT):
                        src = tmp[o % 2][:, t * P:(t + 1) * P] if i < 2 else tmp[o % 2][:, t::4]
                        x = nc.tensor.transpose(PS[:, 4 + o % 2, t * P:(t + 1) * P], src, M["ident"])
                    x.then_inc(S("v_turned"), 1)

            pe.wait_ge(S("consts_in"), 48)
            for o in range(N_QKV):
                unit(U_QKV + o, O_QKV + o, UH, UL, input_split(0) if o == 0 else None)
                if o == 0:
                    norm_sum(0)
                else:
                    after_qkv(o - 1)
            after_qkv(N_QKV - 1)

            def scores(i):
                r, n = i // 4, i % 4
                half, row = n // 2, 64 * (n % 2)
                if i == 0:
                    pe.wait_ge(S("roped"), 12)
                    pe.wait_ge(S("v_token"), 6)
                if i >= 1:
                    pe.wait_ge(S("masked"), i)
                b = 2
                for g in range(3):
                    q = aq[row:row + 64, 2 * g + half, r::4]
                    k = aq[row:row + 64, 6 + 2 * g + half, :] if g == 0 else aq[row:row + 64, 6 + 2 * g + half, r::4]
                    out = PS[:, b, :] if g == 0 else PS[:, b + 1, (g - 1) * P:g * P]
                    x = mm(out, q, k)
                x.then_inc(S("scores"), 1)

            def turn_probs(i):
                pe.wait_ge(S("probs"), i + 1)
                if i >= 1:
                    pe.wait_ge(S("probs_copied"), i)
                for j in range(6):
                    x = nc.tensor.transpose(PS[:, 4 + j // 4, (j % 4) * P:(j % 4 + 1) * P],
                                            sp1[i % 2][:, j * P:(j + 1) * P], M["ident"])
                x.then_inc(S("probs_turned"), 1)

            def values(i):
                r, n = i // 4, i % 4
                row = 64 * (n % 2)
                pe.wait_ge(S("probs_copied"), i + 1)
                if i >= 2:
                    pe.wait_ge(S("o_copied"), i - 1)
                out = PS[row:row + 64, 6 + i % 2, 0:P]
                for j in range(6):
                    g, t = (0, j) if j < 4 else (j - 3, r)
                    x = mm(out, av[:, t, g, n * 64:(n + 1) * 64], pt1[i % 2][:, j * P:(j + 1) * P],
                           j == 0, j == 5)
                x.then_inc(S("o_done"), 1)

            for i in range(16 + 2):
                if i < 16:
                    scores(i)
                if i < N_RWKV:
                    unit(U_LORA + i, O_RWKV + i, UH, UL)
                if 1 <= i < 17:
                    turn_probs(i - 1)
                if i >= 2:
                    values(i - 2)

            gates = Filler(U_GATE, O_GATE, 2 * KT)
            for hp in range(4):
                c = slice(hp * P, (hp + 1) * P)
                if hp == 0:
                    pe.wait_ge(S("lora_in"), 2)
                    pe.wait_ge(S("scan_consts_in"), 64)
                    pe.wait_ge(S("o_copied"), 16)
                else:
                    pe.wait_ge(S("y_root"), hp)
                mm(PS[:, 2, :], lora_w[0:32, c], la[0:32, :]).then_inc(S("lora_done"), 1)
                mm(PS[:, 3, :], lora_w[32:64, c], la[32:64, :]).then_inc(S("lora_done"), 1)
                mm(PS[:, 4, :], lora_g[0:96, c], lg[0:96, :]).then_inc(S("lora_done"), 1)
                gates.slices(6)
                pe.wait_ge(S("k_squared"), hp + 1)
                mm(PS[:, 5, :], M["head_ones"], sq[:]).then_inc(S("k_summed"), 1)
                pe.wait_ge(S("rk_ready"), hp + 1)
                mm(PS[:, 6, :], M["head_ones"], tmp[1][:]).then_inc(S("rk_summed"), 1)
                gates.slices(10)
                pe.wait_ge(S("scaled"), 4 * (hp + 1))
                pe.wait_ge(S("lora_used"), 4 * (hp + 1))
                pe.wait_ge(S("k_root"), hp + 1)
                for n, src in enumerate((FA, FB, FK, vs)):
                    for t in range(NT):
                        x = nc.tensor.transpose(PS[:, 2 + n, t * P:(t + 1) * P], src[:, t * P:(t + 1) * P], M["ident"])
                    x.then_inc(S("turned"), 1)

                def tokens(banks, lhsT, rhs, signal):
                    for t in range(NT):
                        b = slice(t * P, (t + 1) * P)
                        for e in range(2):
                            r = slice(64 * e, 64 * e + 64)
                            x = mm(PS[:, banks[e], b], lhsT[r, b], rhs[r, b])
                            if signal and t == NT - 1:
                                x.then_inc(S(signal), 1)

                pe.wait_ge(S("token_a"), 3 * (hp + 1))
                pe.wait_ge(S("token_d"), 2 * (hp + 1))
                tokens((2, 4), FA, FB, None)
                tokens((3, 5), FB, FA, "lower_done")
                for l in range(1, 6):
                    for e in range(2):
                        pe.wait_ge(S("inverse_ready"), 12 * hp + 2 * (l - 1) + e + 1)
                        for t in range(NT):
                            b = slice(t * P, (t + 1) * P)
                            x = mm(PS[:, 6 + e, b], Lt[:, e, b], X[:, e, b])
                        x.then_inc(S("lx_done"), 1)
                    for e in range(2):
                        pe.wait_ge(S("lx_masked"), 10 * hp + 2 * (l - 1) + e + 1)
                        for t in range(NT):
                            b = slice(t * P, (t + 1) * P)
                            if l < 5:
                                mm(PS[:, 2 + e, b], Y[:, e, b], Z[:, e, b])
                            x = mm(PS[:, 4 + e, b], Z[:, e, b], Y[:, e, b])
                        x.then_inc(S("xlx_done"), 1)
                pe.wait_ge(S("inverse_ready"), 12 * (hp + 1))
                for n, (l, r) in enumerate(((FK, FA), (FB, FR), (FK, FR))):
                    tokens((2 + 2 * n, 3 + 2 * n), l, r, "pairs_done")
                for e in range(2):
                    pe.wait_ge(S("pairs_masked"), 6 * hp + 1 + e)
                    for t in range(NT):
                        x = mm(PS[:, 2 + e, t * 64:(t + 1) * 64], Lt[:, e, t * P:(t + 1) * P],
                               Vt[:, t, 64 * e:64 * e + 64])
                    x.then_inc(S("mv_done"), 1)
                gates.slices(1)
                for e in range(2):
                    pe.wait_ge(S("mv_copied"), 2 * hp + e + 1)
                    pe.wait_ge(S("pairs_masked"), 6 * hp + 3 + e)
                    for t in range(NT):
                        x = mm(PS[:, 4 + e, t * P:(t + 1) * P], Y[:, e, t * P:(t + 1) * P], RHS[:, e, t, :])
                    x.then_inc(S("wu_done"), 1)
                gates.slices(1)
                WU = Z[:].rearrange("p w (t n) -> p w t n", t=NT)
                mrk = (FA, FB)
                pe.wait_ge(S("wu_copied"), 4 * hp + 4)
                pe.wait_ge(S("pairs_masked"), 6 * hp + 6)
                for t in range(NT):
                    b = slice(t * P, (t + 1) * P)
                    for src, right, first, last, bank in ((0, X, True, True, 6), (1, X, True, False, 7),
                                                          (None, mrk, False, True, 7)):
                        for e in range(2):
                            r = slice(64 * e, 64 * e + 64)
                            left = Vt[:, t, r] if src is None else WU[:, src, t, r]
                            x = mm(PS[r, bank, b], left, mrk[e][:, b] if src is None else X[:, e, b], first, last)
                x.then_inc(S("qy_done"), 1)
                for ch in range(7):
                    r, t = slice(64 * (ch % 2), 64 * (ch % 2) + 64), ch // 2
                    b = slice(t * P, (t + 1) * P)
                    if ch:
                        mm(PS[:, 2 + ch % 2, b], WU[r, 0, t, :], Bt[r, t, :])
                    mm(PS[:, 4 + ch % 2, b], Bt[r, t, :], WU[r, 1, t, :], True, False)
                    x = mm(PS[:, 4 + ch % 2, b], Kt[r, t, :], Vt[r, t, :], False, True)
                x.then_inc(S("chunks_done"), 1)
                gates.slices(4)
                G = blk(wkA[:])
                H = blk(wkB[:])
                St = blk(wkC[:])
                pe.wait_ge(S("chunks_ready"), hp + 1)
                pe.wait_ge(S("q_ready"), hp + 1)
                pe.wait_ge(S("y0_ready"), hp + 1)
                for ch in range(1, 7):
                    if ch > 1:
                        pe.wait_ge(S("state_ready"), 6 * hp + ch - 1)
                    mm(PS[:, 6 + ch % 2, 0:P], G[:, ch, :], H[:, 0, :] if ch == 1 else St[:, ch, :])\
                        .then_inc(S("state_done"), 1)
                    gates.slices(1)
                pe.wait_ge(S("state_ready"), 6 * hp + 6)
                for ch in range(1, 8):
                    b = slice(64 * ch, 64 * ch + 64)
                    x = mm(PS[:, 2, b], H[:, 0, :] if ch == 1 else St[:, ch, :], FR[:, b])
                x.then_inc(S("y_done"), 1)
                gates.slices(1)
                pe.wait_ge(S("y_ready"), hp + 1)
                mm(PS[:, 3, :], M["head_mean"], FK[:]).then_inc(S("mean_done"), 1)
                gates.slices(1)
                pe.wait_ge(S("y_squared"), hp + 1)
                mm(PS[:, 4, :], M["head_mean"], sq[:]).then_inc(S("var_done"), 1)
                gates.slices(2)

            for m in range(KT):
                u, b = U_UP + m, 2 + 3 * (m % 2)
                s = u % RING
                pe.wait_ge(S("split_done"), u + 1)
                if m == 0:
                    pe.wait_ge(S("rwkv_out"), 4)
                if m >= 2:
                    pe.wait_ge(S("merged"), m - 1)
                    pe.wait_ge(S("ple_copied"), m - 1)
                product(PS[:, b, :], s, [(0, 0), (1, 1)], OH, OL)
                product(PS[:, b + 1, :], s, [(2 + k, k) for k in range(4)], YH, YL)
                if m == 0:
                    pe.wait_ge(S("p_low"), 2)
                product(PS[:, b + 2, :], s, [(6, 0), (7, 1)], PH, PL).then_inc(S("units_done"), 1)
            for m in range(KT):
                unit(U_OUT + m, O_OUT + m, MH, ML,
                     (lambda k: pe.wait_ge(S("merged_low"), k + 1)) if m == 0 else None)
            norm_sum(1)

            def feed_forward(U, O, n, norm, high, low, hid):
                for half in range(2):
                    u, o = U + 32 * half, O + 24 * half
                    if half == 0:
                        for j in range(4):
                            unit(u + j, o + j, UH, UL, input_split(n) if j == 0 else None)
                            if j == 0:
                                norm_sum(norm)
                        units_loop(u + 4, o + 4, 12, UH, UL)
                    else:
                        units_loop(u, o, 16, UH, UL)
                    pe.wait_ge(S("hidden_low"), hid + 16 * (half + 1))
                    u, o = u + 16, o + 16
                    with pe.Fori(0, 4, 1) as g:
                        for j in range(2):
                            pe.wait_ge(S(f"out_evicted{(o + j) % 2}"), g + (o + j) // 2)
                            for w in range(2):
                                pe.wait_ge(S("split_done"), g * 4 + (u + 2 * j + w + 1))
                                product(PS[:, (o + j) % 2, :], (u + 2 * j + w) % RING,
                                        [(k, 8 * w + k) for k in range(KT)], high, low,
                                        start=w == 0, stop=w == 1).then_inc(S("units_done"), 1)

            feed_forward(U_FFN, O_FFN, 1, 2, FH, FL, 0)
            norm_sum(3)
            for m in range(KT):
                unit(U_PLE + m, O_PLE + m, UH, UL, input_split(2) if m == 0 else None)
            norm_sum(4)

            def after_heads(c, o):
                pe.wait_ge(*evicted(o))
                if c >= 1:
                    pe.wait_ge(S("head_input"), c)
                src = tmp[o % 2]
                if c % 3 < 2:
                    x = mm(PS[:, 2, :], rot2[:], src[:])
                else:
                    for t in range(NT):
                        x = nc.tensor.transpose(PS[:, 2, t * P:(t + 1) * P], src[:, t * P:(t + 1) * P], M["ident"])
                x.then_inc(S("head_turned"), 1)

            def scores2(i):
                n, qt = i // 4, i % 4
                if qt == 0:
                    pe.wait_ge(S("head_input"), 3 * n + 3)
                if i >= 1:
                    pe.wait_ge(S("masked2"), 2 * i)
                for c in range(2):
                    r = slice(64 * c, 64 * c + 64)
                    x = mm(PS[:, 4 + c, 0:P * (qt + 1)], q2[n % 2][r, qt * P:(qt + 1) * P],
                           k2[n % 2][r, 0:P * (qt + 1)])
                x.then_inc(S("scores2"), 1)

            def turn_weights(i):
                qt = i % 4
                pe.wait_ge(S("weights2"), i + 1)
                if i >= 1:
                    pe.wait_ge(S("weights_copied"), i)
                for j in range(qt + 1):
                    x = nc.tensor.transpose(PS[:, 3, j * P:(j + 1) * P], e2[i % 2][:, 0, j * P:(j + 1) * P], M["ident"])
                x.then_inc(S("weights_turned"), 1)

            def values2(i):
                n, qt = i // 4, i % 4
                pe.wait_ge(S("weights_copied"), i + 1)
                if qt == 0 and n >= 1:
                    pe.wait_ge(S("a_copied"), n)
                for j in range(qt + 1):
                    x = mm(PS[:, 6, qt * P:(qt + 1) * P], v2[n % 2][:, j, :], pt2[i % 2][:, j * P:(j + 1) * P],
                           j == 0, j == qt)
                x.then_inc(S("a_done"), 1)

            def head_sum(n):
                pe.wait_ge(S("a_squared"), n + 1)
                mm(PS[:, 7, :], M["ones"], sq[:]).then_inc(S("a_summed"), 1)

            def pool_products():
                u = U_STEP + POOLW_STEP
                pe.wait_ge(S("split_done"), u + 1)
                for m in range(KT):
                    pe.wait_ge(S("pooled_low"), m // 2 + 1)
                    if m == 0:
                        pe.wait_ge(*evicted(step_unit(POOLW_STEP - 1)[1]))
                        pe.wait_ge(*evicted(step_unit(POOLW_STEP - 2)[1]))
                    if m >= 2:
                        pe.wait_ge(S("pool_copied"), m - 1)
                    product(PS[:, m % 2, :], u % RING, [(m, m // 2)], DH, DL)\
                        .then_inc(S("pool_done") if m < KT - 1 else S("units_done"), 1)

            for o in range(3):
                unit(U_HEADS + o, O_HEADS + o, UH, UL, input_split(3) if o == 0 else None)
                if o == 0:
                    norm_sum(5)
                after_heads(o, O_HEADS + o)
            for i in range(32 + 2):
                n, qt = i // 4, i % 4
                if i < 32:
                    scores2(i)
                if 1 <= i < 33:
                    (kind, c), o = step_unit(i - 1)
                    if kind == "head":
                        after_heads(c, o)
                if i < 32:
                    (kind, c), o = step_unit(i)
                    if kind == "pool_weights":
                        pool_products()
                    else:
                        unit(U_STEP + i, o, UH, UL)
                if 1 <= i < 33:
                    turn_weights(i - 1)
                if i >= 2:
                    values2(i - 2)
                    if i % 4 == 1:
                        head_sum((i - 2) // 4)

            for g in range(N_EARLY, 2 * KT):
                unit(U_GATE2 + g - N_EARLY, O_GATE2 + g - N_EARLY, UH, UL)
            for m in range(KT):
                unit(U_OUT2 + m, O_OUT2 + m, M2H, M2L,
                     (lambda k: pe.wait_ge(S("merged_low"), KT + k + 1)) if m == 0 else None)
            feed_forward(U_FFN2, O_FFN2, 4, 6, F2H, F2L, 32)
            norm_sum(7)

        @block.scalar
        def _(act):
            lane = Lane(act, S, "act")

            def f(out, in_, func, name="chain", **more):
                lane.do(nc.scalar.activation(out, in_, func, **more), name)

            act.dma_start(h[:, 0:4, :], a["x"][:, 0:4, :]).then_inc(S("x_in0"), 16)
            act.dma_start(par[:], a["params"]).then_inc(S("consts_in"), 16)
            act.dma_start(small[:], a["small"]).then_inc(S("consts_in"), 16)
            act.dma_start(h[:, 4:8, :], a["x"][:, 4:8, :]).then_inc(S("x_in1"), 16)
            act.dma_start(mats[:], a["mats"]).then_inc(S("consts_in"), 16)
            act.dma_start(table1[:], a["table1"]).then_inc(S("table1_in"), 16)
            act.dma_start(rot1[:], a["rot1"]).then_inc(S("table1_in"), 16)
            act.dma_start(masks1[:], a["masks1"]).then_inc(S("masks1_in"), 16)

            def split_high(n, m, gain, norm, squares=None):
                if gain:
                    f(UH[:, m, :], h[:, m, :], ACT.Identity, "u_high", scale=col(gain, m))
                else:
                    f(UH[:, m, :], h[:, m, :], ACT.Copy, "u_high")
                if norm is not None:
                    f(squares[:, m, :], h[:, m, :], ACT.Square, "squared")

            def square(src, norm, m):
                if norm or m:
                    act.wait_ge(S("squares_summed"), KT * norm + m)
                f(sq[:], src, ACT.Square, "squared")

            def root(n):
                act.wait_ge(S("norm_summed"), n + 1)
                f(acc[:], PS[:, 7, :], ACT.Sqrt, "rooted", scale=1.0 / D, bias=small[:, 1:2])

            act.wait_ge(S("consts_in"), 48)
            for m in range(KT):
                if m % 4 == 0:
                    act.wait_ge(S(f"x_in{m // 4}"), 16)
                split_high(0, m, "mix_pre", 0, aq)
            root(0)

            for i in range(16 + 2):
                if i < 16:
                    p = 4 * (i % 2)
                    act.wait_ge(S("neg_max"), i + 1)
                    f(sp1[i % 2][:], sp1[i % 2][:], ACT.Exp, "exp1", scale=0.125, bias=st[:, p + 1:p + 2],
                      accum_out=st[:, p + 2:p + 3])
                if 1 <= i < 17:
                    act.wait_ge(S("probs_turned"), i)
                    if i >= 3:
                        act.wait_ge(S("o_done"), i - 2)
                    f(pt1[(i - 1) % 2][:], flat(PS[:, 4:6, :])[:, 0:768], ACT.Copy, "probs_copied")
                if i >= 2:
                    r, n = (i - 2) // 4, (i - 2) % 4
                    row = slice(64 * (n % 2), 64 * (n % 2) + 64)
                    act.wait_ge(S("o_done"), i - 1)
                    f(oA[row, n // 2, r::4], PS[row, 6 + i % 2, 0:P], ACT.Copy, "o_copied")
                if i < N_RWKV:
                    act.wait_ge(*evicted(O_RWKV + i))
                    act.dma_start(z_dram[i], zs[i % 2][:]).then_inc(S(f"z_stored{i % 2}"), 16)
            for m in range(2):
                f(OH[:, m, :], oA[:, m, :], ACT.Copy, "o_high")
            act.wait_ge(S("o_low"), 2)
            act.dma_start(smask[:], a["scan_masks"]).then_inc(S("scan_consts_in"), 16)
            act.dma_start(lora_w[0:32, :], a["w2"]).then_inc(S("scan_consts_in"), 16)
            act.dma_start(lora_w[32:64, :], a["a2"]).then_inc(S("scan_consts_in"), 16)
            act.dma_start(lora_g[0:96, :], a["g2"]).then_inc(S("scan_consts_in"), 16)

            for i in range(2):
                act.wait_ge(S(f"z_stored{i}"), 16 * (N_RWKV // 2))

            def load_z(j, b):
                act.dma_start(zp[b][:, 1:T + 1], z_dram[j]).then_inc(S(f"z_in{b}"), 16)

            def load_rkv(hp):
                for b in range(3):
                    if hp or b < 2:
                        act.wait_ge(S("shifted"), b + 1 if hp == 0 else 3 * hp + b)
                    load_z(2 + 3 * hp + b, b)

            load_z(0, 0)
            load_z(1, 1)
            load_rkv(0)

            def gate(j):
                act.wait_ge(*evicted(O_GATE + j))
                f(gs[j % 2][:], gs[j % 2][:], ACT.Sigmoid, "gate_ready")
                act.dma_start(gate_dram[j], gs[j % 2][:]).then_inc(S(f"gate_stored{j % 2}"), 16)

            act.wait_ge(S("shifted"), 1)
            f(la[0:32, :], la[0:32, :], ACT.Tanh, "lora_in")
            act.wait_ge(S("shifted"), 2)
            f(lg[0:96, :], lg[0:96, :], ACT.Sigmoid, "lora_in")
            WU = Z[:].rearrange("p w (t n) -> p w t n", t=NT)
            for hp in range(4):
                act.wait_ge(S("lora_done"), 3 * hp + 1)
                f(wkA[:, 0:T], PS[:, 2, :], ACT.Sigmoid, "lora_used", bias=col("w0", hp))
                act.wait_ge(S("lora_done"), 3 * hp + 2)
                f(wkA[:, T:2 * T], PS[:, 3, :], ACT.Sigmoid, "lora_used", bias=col("a0", hp))
                act.wait_ge(S("lora_done"), 3 * hp + 3)
                f(gt[:], PS[:, 4, :], ACT.Copy, "lora_used")
                f(wkA[:, 0:T], wkA[:, 0:T], ACT.Exp, "lora_used", scale=-float(np.exp(-0.5)))
                act.wait_ge(S("kk_raw"), hp + 1)
                f(sq[:], wkB[:, 0:T], ACT.Square, "k_squared")
                act.wait_ge(S("k_summed"), hp + 1)
                f(sq[:], PS[:, 5, :], ACT.Sqrt, "k_root")
                if hp < 3:
                    load_rkv(hp + 1)
                gate(4 * hp)
                act.wait_ge(S("turned"), 4 * hp + 1)
                for e in range(2):
                    f(RHS[:, e, :, 0:64], blk(PS[:, 2, :])[:, :, 64 * e:64 * e + 64], ACT.Copy, "token_a")
                act.wait_ge(S("turned"), 4 * hp + 2)
                f(Bt[:], blk(PS[:, 3, :]), ACT.Copy, "token_a")
                gate(4 * hp + 1)
                for e in range(2):
                    act.wait_ge(S("mv_done"), 2 * hp + e + 1)
                    f(RHS[:, e, :, 64:128], PS[:, 2 + e, 0:256].rearrange("p (t n) -> p t n", t=NT), ACT.Copy,
                      "mv_copied")
                for e in range(2):
                    act.wait_ge(S("wu_done"), 2 * hp + e + 1)
                    for w in range(2):
                        f(WU[:, w, :, 64 * e:64 * e + 64], blk(PS[:, 4 + e, :])[:, :, 64 * w:64 * w + 64], ACT.Copy,
                          "wu_copied")
                act.wait_ge(S("qy_done"), hp + 1)
                f(FK[:], PS[:, 7, :], ACT.Copy, "y0_ready")
                gate(4 * hp + 2)
                act.wait_ge(S("y_centered"), hp + 1)
                f(sq[:], tmp[0][:], ACT.Square, "y_squared")
                act.wait_ge(S("var_done"), hp + 1)
                f(sq[:], PS[:, 4, :], ACT.Sqrt, "y_root", bias=small[:, 2:3])
                act.wait_ge(S("y_final"), hp + 1)
                f(YH[:, hp, :], tmp[1][:], ACT.Copy, "y_high")
                gate(4 * hp + 3)

            act.wait_ge(S("rwkv_out"), 4)
            act.dma_start(pf[:], a["p"]).then_inc(S("p_in"), 16)
            act.wait_ge(S("p_in"), 16)
            for m in range(2):
                f(PH[:, m, :], pf[:, m, :], ACT.Copy, "p_high")

            for i in range(2):
                act.wait_ge(S(f"gate_stored{i}"), 16 * KT)

            def load_gates(m):
                if m >= 2:
                    act.wait_ge(S("merged_low"), m - 1)
                for j in range(2):
                    b = 2 * (m % 2) + j
                    act.dma_start(gin[b][:], gate_dram[2 * m + j]).then_inc(S(f"gate_in{b}"), 16)

            load_gates(0)
            load_gates(1)
            for m in range(KT):
                act.wait_ge(S("units_done"), U_UP + m + 1)
                f(ple[:, m, :], PS[:, 4 + 3 * (m % 2), :], ACT.Copy, "ple_copied")
                act.wait_ge(S("merged"), m + 1)
                f(MH[:, m, :], gin[2 * (m % 2)][:], ACT.Copy, "merged_high")
                if m + 2 < KT:
                    load_gates(m + 2)
            for m in range(KT):
                act.wait_ge(S("units_done"), U_OUT + m + 1)
                f(t8[:, m, :], PS[:, (O_OUT + m) % 2, :], ACT.Copy, lane.leaves(O_OUT + m))
                square(t8[:, m, :], 1, m)
            root(1)

            def feed_forward(U, O, high, hid, dst, norm):
                highs = high[:].rearrange("p (g j) t -> p g j t", j=4)
                outs = dst[:].rearrange("p (g j) t -> p g j t", j=2)
                for half in range(2):
                    o = O + 24 * half
                    with lane.loop(4, {"chain": 4, "hidden_high": 4}) as g:
                        for j in range(4):
                            act.wait_ge(S(f"out_evicted{(o + j) % 2}"), g * 2 + ((o + j) // 2 + 1))
                            f(tmp[j % 2][:], tmp[j % 2][:], ACT.Square)
                            f(highs[:, g, j, :], tmp[j % 2][:], ACT.Copy, "hidden_high")
                o += 16
                with lane.loop(4, {"squared": 2}) as g:
                    for j in range(2):
                        act.wait_ge(S(f"out_evicted{(o + j) % 2}"), g + ((o + j) // 2 + 1))
                        act.wait_ge(S("squares_summed"), g * 2 + (KT * norm + j))
                        f(sq[:], outs[:, g, j, :], ACT.Square, "squared")
                root(norm)

            def updated(n, m):
                act.wait_ge(S("h_new"), KT * n + m + 1)

            for m in range(KT):
                updated(0, m)
                split_high(1, m, "ffn_pre", 2, t8)
            root(2)
            feed_forward(U_FFN, O_FFN, FH, 0, t8, 3)

            act.dma_start(pos[:], a["positions"].to_broadcast([P, T])).then_inc(S("block2_in"), 16)
            act.dma_start(rot2[:], a["rot2"]).then_inc(S("block2_in"), 16)
            act.dma_start(causal[:], a["causal"]).then_inc(S("block2_in"), 16)
            for j in range(4):
                act.dma_start(lam4[:, j, :], a[f"lam{j}"].to_broadcast([P, HD])).then_inc(S("block2_in"), 16)
            for m in range(KT):
                updated(1, m)
                split_high(2, m, None, None)
            plev = ple[:].rearrange("p (g j) t -> p g j t", j=4)
            t8v = t8[:].rearrange("p (g j) t -> p g j t", j=4)
            with lane.loop(2, {"out_evicted0": 2, "out_evicted1": 2, "squared": 4}) as g:
                for j in range(4):
                    act.wait_ge(S("units_done"), g * 4 + (U_PLE + j + 1))
                    f(tmp[j % 2][:], PS[:, j % 2, :], ACT.Sigmoid, lane.leaves(O_PLE + j))
                    act.wait_ge(S("e_new"), g * 4 + (j + 1))
                    act.wait_ge(S("squares_summed"), g * 4 + (KT * 4 + j))
                    f(sq[:], t8v[:, g, j, :], ACT.Square, "squared")
            root(4)
            act.wait_ge(S("lam_dots"), 2)
            f(lamw[:, 2:4], lamw[:, 0:2], ACT.Exp, "lam_exp")
            act.wait_ge(S("angles"), 2)
            f(table2[:, T:2 * T], table2[:, T:2 * T], ACT.Sin, "table2")
            f(table2[:, 0:T], table2[:, 0:T], ACT.Sin, "table2")

            for m in range(KT):
                updated(2, m)
                split_high(3, m, "attn2", 5, t8)
            root(5)
            for i in range(32 + 2):
                if i < 32:
                    p, n = i % 2, P * (i % 4 + 1)
                    act.wait_ge(S("neg_max2"), i + 1)
                    for c in range(2):
                        f(e2[p][:, c, 0:n], e2[p][:, c, 0:n], ACT.Exp, "exp2", scale=0.125,
                          bias=st2[:, p, 2 + c:3 + c], accum_out=st2[:, p, 4 + c:5 + c])
                if i == POOLW_STEP:
                    for m in range(KT):
                        if m < KT - 1:
                            act.wait_ge(S("pool_done"), m + 1)
                        else:
                            act.wait_ge(S("units_done"), U_STEP + POOLW_STEP + 1)
                        f(poolT[:, m, :], PS[:, m % 2, :], ACT.Identity, "pool_copied", scale=col("pool_scale", m))
                if 1 <= i < 33 and step_unit(i - 1)[0][0] == "pool":
                    j = step_unit(i - 1)[0][1]
                    act.wait_ge(S("pool_diff"), j + 1)
                    f(DH[:, j, :], pz[:, 16:16 + T], ACT.Copy, "pool_high")
                if 1 <= i < 33 and step_unit(i - 1)[0][0] == "gate":
                    (_, g), o = step_unit(i - 1)
                    act.wait_ge(*evicted(o))
                    f(gates2[:, g, :], gates2[:, g, :], ACT.Sigmoid, "gated")
                if 1 <= i < 33:
                    n = P * ((i - 1) % 4 + 1)
                    act.wait_ge(S("weights_turned"), i)
                    if i >= 3:
                        act.wait_ge(S("a_done"), i - 2)
                    f(pt2[(i - 1) % 2][:, 0:n], PS[:, 3, 0:n], ACT.Copy, "weights_copied")
                if i >= 2 and i % 4 == 1:
                    n = (i - 2) // 4
                    act.wait_ge(S("a_done"), 4 * n + 4)
                    f(aT[:, n, :], PS[:, 6, :], ACT.Copy, "a_copied")
                    f(sq[:], aT[:, n, :], ACT.Square, "a_squared")
                    act.wait_ge(S("a_summed"), n + 1)
                    f(sq[:], PS[:, 7, :], ACT.Sqrt, "a_root", scale=1.0 / P, bias=small[:, 1:2])
            for m in range(KT):
                for j in range(2):
                    if 2 * m + j >= N_EARLY:
                        act.wait_ge(*evicted(O_GATE2 + 2 * m + j - N_EARLY))
                        f(tmp[j][:], tmp[j][:], ACT.Sigmoid, "gated")
                act.wait_ge(S("merged"), KT + m + 1)
                f(M2H[:, m, :], gates2[:, 2 * m, :] if 2 * m < N_EARLY else tmp[0][:], ACT.Copy, "merged_high")
            for m in range(KT):
                act.wait_ge(*evicted(O_OUT2 + m))
                split_high(4, m, "mlp2", 6, aT)
            root(6)
            feed_forward(U_FFN2, O_FFN2, F2H, 32, h, 7)
            for m in range(KT):
                act.wait_ge(S("final"), m + 1)
                act.dma_start(a["out"][:, m, :], h[:, m, :]).then_inc(S("stored"), 16)

        @block.vector
        def _(dve):
            lane = Lane(dve, S, "dve")

            def tt(out, x, y, op, name="chain"):
                lane.do(nc.vector.tensor_tensor(out, x, y, op), name)

            def ts(out, x, s1, op1, name="chain", s2=None, op2=ALU.bypass):
                if s2 is None:
                    lane.do(nc.vector.tensor_scalar(out, x, s1, None, op1), name)
                else:
                    lane.do(nc.vector.tensor_scalar(out, x, s1, s2, op1, op2), name)

            def stt(out, x, s, y, op1, op2, name="chain"):
                lane.do(nc.vector.scalar_tensor_tensor(out=out, in0=x, scalar=s, in1=y, op0=op1, op1=op2), name)

            def copy(out, x, name="chain"):
                lane.do(nc.vector.tensor_copy(out, x), name)

            def recip(out, x):
                lane.do(nc.vector.reciprocal(out, x))

            MUL, ADD, SUB = ALU.mult, ALU.add, ALU.subtract

            def split_low(n, m, gain):
                dve.wait_ge(S("u_high"), KT * n + m + 1)
                if gain:
                    stt(UL[:, m, :], h[:, m, :], col(gain, m), UH[:, m, :].bitcast(F32), MUL, SUB, "u_low")
                else:
                    tt(UL[:, m, :], h[:, m, :], UH[:, m, :].bitcast(F32), SUB, "u_low")

            def add_squares(norm, m, src):
                dve.wait_ge(S("squared"), KT * norm + m + 1)
                if m == 0:
                    copy(acc[:], src, "squares_summed")
                else:
                    tt(acc[:], acc[:], src, ADD, "squares_summed")

            def norm_scale(n):
                dve.wait_ge(S("rooted"), n + 1)
                recip(rstd[:], acc[:])

            def evict(o, u, dst):
                dve.wait_ge(S("units_done"), u + 1)
                tt(dst, PS[:, o % 2, :], rstd[:], MUL, lane.leaves(o))

            for m in range(KT):
                split_low(0, m, "mix_pre")
                add_squares(0, m, aq[:, m, :])
            norm_scale(0)

            def finish_qkv(o):
                if o < 12:
                    tt(rt[:], tmp[o % 2][:], table1[:, 0:T], MUL)
                    dve.wait_ge(S("rotated"), o + 1)
                    tt(tmp[o % 2][:], PS[:, 2 + o % 2, :], table1[:, T:2 * T], MUL)
                    tt(aq[:, o, :], rt[:], tmp[o % 2][:], ADD, "roped")
                else:
                    i = o - 12
                    dve.wait_ge(S("v_turned"), i + 1)
                    copy(av[:, :, i // 2, (i % 2) * P:(i % 2 + 1) * P], blk(PS[:, 4 + o % 2, :]), "v_token")

            dve.wait_ge(S("table1_in"), 32)
            for o in range(N_QKV):
                evict(O_QKV + o, U_QKV + o, tmp[o % 2][:])
                if o:
                    finish_qkv(o - 1)
            finish_qkv(N_QKV - 1)

            dve.wait_ge(S("masks1_in"), 16)
            for i in range(16 + 1):
                if i < 16:
                    r, p = i // 4, 4 * (i % 2)
                    dve.wait_ge(S("scores"), i + 1)
                    if i >= 2:
                        dve.wait_ge(S("probs_turned"), i - 1)
                    b = 2
                    lane.do(nc.vector.tensor_tensor_reduce(
                        out=sp1[i % 2][:], in0=flat(PS[:, b:b + 2, :])[:, 0:768],
                        in1=masks1[:, r * 768:(r + 1) * 768], scale=1.0, scalar=NEG, op0=ADD, op1=ALU.max,
                        accum_out=st[:, p:p + 1]), "masked")
                    ts(st[:, p + 1:p + 2], st[:, p:p + 1], -0.125, MUL, "neg_max")
                if i >= 1:
                    p = 4 * ((i - 1) % 2)
                    dve.wait_ge(S("exp1"), i)
                    recip(st[:, p + 3:p + 4], st[:, p + 2:p + 3])
                    ts(sp1[(i - 1) % 2][:], sp1[(i - 1) % 2][:], st[:, p + 3:p + 4], MUL, "probs")
                if i < N_RWKV:
                    if i >= 2:
                        dve.wait_ge(S(f"z_stored{i % 2}"), 16 * (i // 2))
                    evict(O_RWKV + i, U_LORA + i, zs[i % 2][:])
            for m in range(2):
                dve.wait_ge(S("o_high"), m + 1)
                tt(OL[:, m, :], oA[:, m, :], OH[:, m, :].bitcast(F32), SUB, "o_low")

            for z in zp:
                lane.do(nc.vector.memset(z[:, 0:1], 0.0))
            lane.do(nc.vector.memset(PP[:, :, 0:1], 1.0))
            lane.do(nc.vector.memset(omka[:], 0.0))
            ts(omka[:, 0:4], par[:, PARAM_COLS["k_a"]:PARAM_COLS["k_a"] + 4], -1.0, MUL, s2=1.0, op2=ADD)

            def shift(b, j, out, n):
                dve.wait_ge(S(f"z_in{b}"), 16 * n)
                tt(wkB[:, T:2 * T], zp[b][:, 0:T], zp[b][:, 1:T + 1], SUB)
                stt(out, wkB[:, T:2 * T], col("mu", j), zp[b][:, 1:T + 1], MUL, ADD, "shifted")

            def gate(j):
                if j >= 2:
                    dve.wait_ge(S(f"gate_stored{j % 2}"), 16 * (j // 2))
                evict(O_GATE + j, U_GATE + j, gs[j % 2][:])

            shift(0, 12, la[:], 1)
            shift(1, 13, lg[:], 1)
            rs, ks = wkC[:, 0:T], wkC[:, T:2 * T]
            decay, aa = wkA[:, 0:T], wkA[:, T:2 * T]
            kk, ip = wkB[:, 0:T], wkB[:, T:2 * T]
            G, H, St = blk(wkA[:]), blk(wkB[:]), blk(wkC[:])

            def ch(x):
                return x.rearrange("p (c t) -> p c t", c=8)

            dve.wait_ge(S("scan_consts_in"), 64)

            def rkv(hp):
                shift(0, hp, rs, hp + 2)
                shift(1, 4 + hp, ks, hp + 2)
                ts(kk, ks, col("k_k", hp), MUL, "kk_raw")
                shift(2, 8 + hp, vs[:], hp + 1)

            rkv(0)
            for hp in range(4):
                dve.wait_ge(S("lora_used"), 4 * hp + 2)
                ts(tmp[0][:], aa, col("k_a", hp), MUL, s2=omka[:, hp:hp + 1], op2=ADD)
                tt(ks, ks, tmp[0][:], MUL)
                stt(tmp[1][:], rs, col("r_k", hp), ks, MUL, MUL, "rk_ready")
                dve.wait_ge(S("k_root"), hp + 1)
                ts(sq[:], sq[:], 1e-12, ALU.max)
                recip(sq[:], sq[:])
                tt(kk, kk, sq[:], MUL)
                dve.wait_ge(S("rk_summed"), hp + 1)
                tt(bonus[:], PS[:, 6, :], vs[:], MUL)
                dve.wait_ge(S("lora_used"), 4 * hp + 4)
                for c in range(8):
                    lane.do(nc.vector.tensor_tensor_scan(
                        PP[:, c, 1:65], decay[:, 64 * c:64 * c + 64], omka[:, 4:68], 1.0, MUL, ADD))
                gate(4 * hp)
                tt(ch(FR[:]), ch(rs), PP[:, :, 1:65], MUL, "scaled")
                lane.do(nc.vector.reciprocal(ch(ip), PP[:, :, 1:65]))
                stt(ch(FA[:]), ch(kk), -1.0, PP[:, :, 0:64], MUL, MUL, "scaled")
                tt(tmp[0][:], kk, aa, MUL)
                tt(FB[:], tmp[0][:], ip, MUL, "scaled")
                tt(FK[:], ks, ip, MUL, "scaled")
                gate(4 * hp + 1)
                dve.wait_ge(S("turned"), 4 * hp + 3)
                copy(Kt[:], blk(PS[:, 4, :]), "token_d")
                dve.wait_ge(S("turned"), 4 * hp + 4)
                copy(Vt[:], blk(PS[:, 5, :]), "token_d")
                for e in range(2):
                    dve.wait_ge(S("lower_done"), 2 * hp + e + 1)
                    tt(blk(X[:, e, :]), blk(PS[:, 2 + 2 * e, :]), over(K_["pair_lower"]), MUL)
                    tt(blk(X[:, e, :]), blk(X[:, e, :]), over(M["ident"]), ADD)
                    tt(blk(Lt[:, e, :]), blk(PS[:, 3 + 2 * e, :]), over(K_["before"]), MUL)
                    tt(blk(Y[:, e, :]), blk(Lt[:, e, :]), over(K_["pair_upper"]), MUL)
                    tt(blk(Y[:, e, :]), blk(Y[:, e, :]), over(M["ident"]), ADD, "inverse_ready")
                for l in range(1, 6):
                    for e in range(2):
                        dve.wait_ge(S("lx_done"), 10 * hp + 2 * (l - 1) + e + 1)
                        tt(blk(Z[:, e, :]), blk(PS[:, 6 + e, :]), over(K_[f"lvl{l}"]), MUL, "lx_masked")
                    for e in range(2):
                        dve.wait_ge(S("xlx_done"), 10 * hp + 2 * (l - 1) + e + 1)
                        if l < 5:
                            tt(X[:, e, :], X[:, e, :], PS[:, 2 + e, :], ADD)
                        tt(Y[:, e, :], Y[:, e, :], PS[:, 4 + e, :], ADD, "inverse_ready")
                for n, (dst, mask) in enumerate((((Lt[:, 0, :], Lt[:, 1, :]), "before"),
                                                 ((X[:, 0, :], X[:, 1, :]), "upto"), ((FA[:], FB[:]), "upto"))):
                    for e in range(2):
                        dve.wait_ge(S("pairs_done"), 6 * hp + 2 * n + e + 1)
                        tt(blk(dst[e]), blk(PS[:, 2 + 2 * n + e, :]), over(K_[mask]), MUL, "pairs_masked")
                dve.wait_ge(S("qy_done"), hp + 1)
                tt(FR[:], FR[:], PS[:, 6, :], ADD, "q_ready")
                dve.wait_ge(S("chunks_done"), hp + 1)
                for lo, src in ((2, blk(PS[:, 2, :])[:, 1:4, :]), (1, blk(PS[:, 3, :])[:, 0:3, :])):
                    tt(G[:, lo:lo + 5:2, :], src, over(M["head_ones"], 3), MUL)
                    tt(G[:, lo:lo + 5:2, :], G[:, lo:lo + 5:2, :], over(M["ident"], 3), ADD)
                for c in range(7):
                    stt(H[:, c, :], PS[:, 4 + c % 2, (c // 2) * P:(c // 2 + 1) * P], PP[:, c, 64:65], M["head_ones"],
                        MUL, MUL, "chunks_ready" if c == 6 else "chain")
                for c in range(1, 7):
                    dve.wait_ge(S("state_done"), 6 * hp + c)
                    stt(St[:, c + 1, :], PS[:, 6 + c % 2, 0:P], PP[:, c, 64:65], H[:, c, :], MUL, ADD, "state_ready")
                gate(4 * hp + 2)
                dve.wait_ge(S("y_done"), hp + 1)
                dve.wait_ge(S("y0_ready"), hp + 1)
                tt(FK[:, 64:T], FK[:, 64:T], PS[:, 2, 64:T], ADD, "y_ready")
                dve.wait_ge(S("mean_done"), hp + 1)
                tt(tmp[0][:], FK[:], PS[:, 3, :], SUB, "y_centered")
                if hp < 3:
                    rkv(hp + 1)
                dve.wait_ge(S("y_root"), hp + 1)
                recip(sq[:], sq[:])
                tt(tmp[0][:], tmp[0][:], sq[:], MUL)
                ts(tmp[0][:], tmp[0][:], col("ln_w", hp), MUL, s2=col("ln_b", hp), op2=ADD)
                tt(tmp[0][:], tmp[0][:], bonus[:], ADD)
                tt(tmp[1][:], tmp[0][:], gt[:], MUL, "y_final")
                dve.wait_ge(S("y_high"), hp + 1)
                tt(YL[:, hp, :], tmp[1][:], YH[:, hp, :].bitcast(F32), SUB, "rwkv_out")
                gate(4 * hp + 3)

            for m in range(2):
                dve.wait_ge(S("p_high"), m + 1)
                tt(PL[:, m, :], pf[:, m, :], PH[:, m, :].bitcast(F32), SUB, "p_low")

            def merge(m, base, x, y, first, second, high, low):
                tt(x, x, first, MUL)
                tt(y, y, second, MUL)
                tt(x, x, y, ADD, "merged")
                dve.wait_ge(S("merged_high"), base + m + 1)
                tt(low[:, m, :], x, high[:, m, :].bitcast(F32), SUB, "merged_low")

            for m in range(KT):
                b, g = 2 + 3 * (m % 2), 2 * (m % 2)
                for j in range(2):
                    dve.wait_ge(S(f"gate_in{g + j}"), 16 * (m // 2 + 1))
                dve.wait_ge(S("units_done"), U_UP + m + 1)
                merge(m, 0, gin[g][:], gin[g + 1][:], PS[:, b, :], PS[:, b + 1, :], MH, ML)
            for m in range(KT):
                add_squares(1, m, sq[:])
            norm_scale(1)

            def update(m, gain):
                stt(t8[:, m, :], t8[:, m, :], col(gain, m), rstd[:], MUL, MUL)
                tt(h[:, m, :], h[:, m, :], t8[:, m, :], ADD, "h_new")

            def update_all(post, n, gain, norm):
                for m in range(KT):
                    update(m, post)
                    if m:
                        split_low(n, m - 1, gain)
                split_low(n, KT - 1, gain)
                if norm is not None:
                    for m in range(KT):
                        add_squares(norm, m, t8[:, m, :])
                    norm_scale(norm)

            def feed_forward(U, O, low, high, dst, hid, norm, add_first):
                lows = low[:].rearrange("p (g j) t -> p g j t", j=4)
                highs = high[:].rearrange("p (g j) t -> p g j t", j=4)
                outs = dst[:].rearrange("p (g j) t -> p g j t", j=2)
                for half in range(2):
                    u, o = U + 32 * half, O + 24 * half
                    with lane.loop(4, {"out_evicted0": 2, "out_evicted1": 2, "hidden_low": 4}) as g:
                        for j in range(4):
                            dve.wait_ge(S("units_done"), g * 4 + (u + j + 1))
                            stt(tmp[j % 2][:], PS[:, (o + j) % 2, :], 0.0, rstd[:], ALU.max, MUL,
                                lane.leaves(o + j))
                            dve.wait_ge(S("hidden_high"), g * 4 + (hid + 16 * half + j + 1))
                            tt(lows[:, g, j, :], tmp[j % 2][:], highs[:, g, j, :].bitcast(F32), SUB, "hidden_low")
                    u, o = u + 16, o + 16
                    if half:
                        lane.do(nc.vector.memset(acc[:], 0.0))
                    with lane.loop(4, {"out_evicted0": 1, "out_evicted1": 1} | ({"squares_summed": 2} if half else {})) as g:
                        for j in range(2):
                            dve.wait_ge(S("units_done"), g * 4 + (u + 2 * j + 2))
                            d = outs[:, g, j, :]
                            if half or add_first:
                                tt(d, d, PS[:, (o + j) % 2, :], ADD, lane.leaves(o + j))
                            else:
                                copy(d, PS[:, (o + j) % 2, :], lane.leaves(o + j))
                            if half:
                                dve.wait_ge(S("squared"), g * 2 + (KT * norm + j + 1))
                                tt(acc[:], acc[:], sq[:], ADD, "squares_summed")
                norm_scale(norm)

            update_all("mix_post", 1, "ffn_pre", 2)
            feed_forward(U_FFN, O_FFN, FL, FH, t8, 0, 3, False)
            update_all("ffn_post", 2, None, None)

            dve.wait_ge(S("block2_in"), 112)
            cosv, sinv = table2[:, 0:T], table2[:, T:2 * T]
            two_pi = 2 * np.pi
            c1 = 6.28125
            c2 = float(np.float32(np.floor((two_pi - c1) * 2 ** 20) / 2 ** 20))
            c3 = float(two_pi - c1 - c2)
            magic = 1.5 * 2 ** 23
            copy(cosv, pos[:])
            ts(cosv, cosv, small[:, 0:1], MUL)
            ts(rt2[:], cosv, float(1 / two_pi), MUL, s2=magic, op2=ADD)
            ts(rt2[:], rt2[:], -magic, ADD)
            for c in (c1, c2, c3):
                stt(cosv, rt2[:], -c, cosv, MUL, ADD)
            ts(sinv, cosv, 3.1415925, ALU.min, s2=-3.1415925, op2=ALU.max, name="angles")
            stt(cosv, sinv, -1.0, sinv, MUL, ALU.max)
            ts(cosv, cosv, -1.0, MUL, s2=float(np.pi / 2), op2=ADD, name="angles")
            for j in range(2):
                lane.do(nc.vector.tensor_tensor_reduce(
                    out=lam4[:, 2 * j, :], in0=lam4[:, 2 * j, :], in1=lam4[:, 2 * j + 1, :], scale=1.0, scalar=0.0,
                    op0=MUL, op1=ADD, accum_out=lamw[:, j:j + 1]), "lam_dots")

            plev = ple[:].rearrange("p (g j) t -> p g j t", j=4)
            t8v = t8[:].rearrange("p (g j) t -> p g j t", j=4)
            lane.do(nc.vector.memset(acc[:], 0.0))
            with lane.loop(2, {"e_new": 4, "squares_summed": 4}) as g:
                for j in range(4):
                    dve.wait_ge(S(f"out_evicted{j % 2}"), g * 2 + ((O_PLE + j) // 2 + 1))
                    tt(t8v[:, g, j, :], tmp[j % 2][:], plev[:, g, j, :], MUL, "e_new")
                    dve.wait_ge(S("squared"), g * 4 + (KT * 4 + j + 1))
                    tt(acc[:], acc[:], sq[:], ADD, "squares_summed")
            norm_scale(4)
            dve.wait_ge(S("lam_exp"), 1)
            tt(lamw[:, 4:5], lamw[:, 2:3], lamw[:, 3:4], SUB)
            ts(lamw[:, 5:6], lamw[:, 4:5], LAM_INIT, ADD, s2=-1.0, op2=MUL)
            ts(lamw[:, 6:7], col("subln"), 1.0 - LAM_INIT, MUL)

            update_all("ple_post", 3, "attn2", 5)

            def finish_head(c, o):
                n = c // 3
                dve.wait_ge(S("head_turned"), c + 1)
                if c % 3 == 2:
                    copy(v2[n % 2][:], blk(PS[:, 2, :]), "head_input")
                else:
                    tt(rt2[:], tmp[o % 2][:], cosv, MUL)
                    tt(tmp[o % 2][:], PS[:, 2, :], sinv, MUL)
                    tt((q2, k2)[c % 3][n % 2][:], rt2[:], tmp[o % 2][:], ADD, "head_input")

            for z in (pz, pa, pb):
                lane.do(nc.vector.memset(z[:, 0:16], 0.0))

            def pool_windows(j):
                cur, w = pz, (2, 4, 8, 16)[j]
                for l in range(j + 1):
                    nxt = (pa, pb)[l % 2]
                    tt(nxt[:, 16:16 + T], cur[:, 16:16 + T], cur[:, 16 - 2 ** l:16 - 2 ** l + T], ADD)
                    cur = nxt
                tt(cur[:, 16:32], cur[:, 16:32], small[:, 4 + 16 * j:20 + 16 * j], MUL)
                ts(cur[:, 32:16 + T], cur[:, 32:16 + T], 1.0 / w, MUL)
                tt(pz[:, 16:16 + T], cur[:, 16:16 + T], pz[:, 16:16 + T], SUB, "pool_diff")

            dve.wait_ge(S("table2"), 2)
            for o in range(3):
                evict(O_HEADS + o, U_HEADS + o, tmp[o % 2][:])
                finish_head(o, O_HEADS + o)
            for i in range(32 + 2):
                n, qt = i // 4, i % 4
                if i < 32:
                    p, w = i % 2, P * (qt + 1)
                    dve.wait_ge(S("scores2"), i + 1)
                    if i >= 2:
                        dve.wait_ge(S("weights_turned"), i - 1)
                    for c in range(2):
                        lane.do(nc.vector.tensor_tensor_reduce(
                            out=e2[p][:, c, 0:w], in0=PS[:, 4 + c, 0:w], in1=causal[:, T - w:T], scale=1.0,
                            scalar=NEG, op0=ADD, op1=ALU.max, accum_out=st2[:, p, c:c + 1]), "masked2")
                    ts(st2[:, p, 2:4], st2[:, p, 0:2], -0.125, MUL, "neg_max2")
                if 1 <= i < 33:
                    (kind, c), o = step_unit(i - 1)
                    if kind == "head":
                        finish_head(c, o)
                    if kind == "pool":
                        dve.wait_ge(S("pool_high"), c + 1)
                        tt(DL[:, c, :], pz[:, 16:16 + T], DH[:, c, :].bitcast(F32), SUB, "pooled_low")
                    p, w = (i - 1) % 2, P * ((i - 1) % 4 + 1)
                    dve.wait_ge(S("exp2"), 2 * i)
                    recip(st2[:, p, 6:8], st2[:, p, 4:6])
                    tt(st2[:, p, 7:8], st2[:, p, 7:8], lamw[:, 5:6], MUL)
                    ts(e2[p][:, 1, 0:w], e2[p][:, 1, 0:w], st2[:, p, 7:8], MUL)
                    stt(e2[p][:, 0, 0:w], e2[p][:, 0, 0:w], st2[:, p, 6:7], e2[p][:, 1, 0:w], MUL, ADD, "weights2")
                if i < 32:
                    (kind, c), o = step_unit(i)
                    if kind == "head":
                        evict(o, U_STEP + i, tmp[o % 2][:])
                    elif kind == "gate":
                        evict(o, U_STEP + i, gates2[:, c, :])
                    elif kind == "pool":
                        evict(o, U_STEP + i, pz[:, 16:16 + T])
                        pool_windows(c)
                if i >= 2 and i % 4 == 1:
                    n = (i - 2) // 4
                    dve.wait_ge(S("a_root"), n + 1)
                    recip(sq[:], sq[:])
                    stt(aT[:, n, :], aT[:, n, :], lamw[:, 6:7], sq[:], MUL, MUL)

            for m in range(KT):
                if 2 * m < N_EARLY:
                    x, y = gates2[:, 2 * m, :], gates2[:, 2 * m + 1, :]
                else:
                    x, y = tmp[0][:], tmp[1][:]
                    for j in range(2):
                        g = 2 * m + j - N_EARLY
                        evict(O_GATE2 + g, U_GATE2 + g, (x, y)[j])
                dve.wait_ge(S("gated"), 2 * m + 2)
                merge(m, KT, x, y, aT[:, m, :], poolT[:, m, :], M2H, M2L)
            for m in range(KT):
                o = O_OUT2 + m
                dve.wait_ge(S("units_done"), U_OUT2 + m + 1)
                tt(h[:, m, :], h[:, m, :], PS[:, o % 2, :], ADD, lane.leaves(o))
                if m:
                    split_low(4, m - 1, "mlp2")
                    add_squares(6, m - 1, aT[:, m - 1, :])
            split_low(4, KT - 1, "mlp2")
            add_squares(6, KT - 1, aT[:, KT - 1, :])
            norm_scale(6)
            feed_forward(U_FFN2, O_FFN2, F2L, F2H, h, 32, 7, True)
            for m in range(KT):
                stt(h[:, m, :], h[:, m, :], col("final", m), rstd[:], MUL, MUL, "final")


def kernel(**inputs):
    import concourse.bacc as bacc
    from concourse.bass_utils import run_bass_kernel_spmd

    x = {k: np.asarray(v) for k, v in inputs.items()}
    w_in, w_in2 = x["w_in"][0], x["w_in_2"][0]

    def unit(w, c, n=P):
        w = w[:, c:c + n]
        if n < P:
            w = np.concatenate([w, np.zeros((D, P - n), w.dtype)], 1)
        return w.reshape(KT, P, P).transpose(1, 0, 2)

    units = [unit(w_in, P * j) for j in range(N_QKV)]
    rw = 9 * 256
    units += [unit(w_in, rw + 1536, 64), unit(w_in, rw + 1600, 96)]
    units += [unit(w_in, rw + 512 * j + P * hp) for hp in range(4) for j in range(3)]
    gate = rw + 1696
    units += [unit(w_in, gate + D * j + P * m) for m in range(KT) for j in range(2)]
    for m in range(KT):
        c = slice(P * m, P * (m + 1))
        units += [unit(np.concatenate([x["w_attn_up"][0][:, c], x["w_rwkv_up"][0][:, c], x["w_ple"][0][:, c]], 0), 0)]

    def feed_forward(w_up, w_down):
        for half in range(2):
            for j in range(16):
                yield unit(w_up, P * (16 * half + j))
            for m in range(KT):
                for w in range(2):
                    yield unit(w_down[2048 * half + 1024 * w:2048 * half + 1024 * (w + 1)], P * m)

    units += [unit(x["w_out"][0], P * m) for m in range(KT)]
    units += list(feed_forward(x["w_ff_in"][0], x["w_ff_out"][0]))
    units += [unit(x["w_ple_gate"][0], P * m) for m in range(KT)]
    gates2 = [unit(w_in2, 3584 + D * j + P * m) for m in range(KT) for j in range(2)]
    beside = {"head": [unit(w_in2, D * j + P * n) for n in range(8) for j in range(3)],
              "pool": [unit(w_in2, 3 * D + P * j) for j in range(4)],
              "pool_weights": [x["w_pool_2"][0].reshape(4, P, 2, P).transpose(1, 0, 2, 3).reshape(P, KT, P)],
              "gate": gates2}
    units += beside["head"][:3]
    for i in range(32):
        kind, c = step_unit(i)[0]
        units.append(beside[kind][c])
    units += gates2[N_EARLY:]
    units += [unit(x["w_out_2"][0], P * m) for m in range(KT)]
    units += list(feed_forward(x["w_up_2"][0], x["w_down_2"][0]))
    assert len(units) == N_UNITS

    mu = x["rwkv_mu"][0]
    mu = np.concatenate([mu[:1600], np.zeros(64, mu.dtype), mu[1600:], np.zeros(32, mu.dtype)])
    cols = {"mix_pre": "mix_pre_norm", "mix_post": "mix_post_norm", "ffn_pre": "ffn_pre_norm",
            "ffn_post": "ffn_post_norm", "ple_post": "ple_post_norm", "attn2": "norm_attn_g_2",
            "mlp2": "norm_mlp_g_2", "final": "final_norm_g_2", "pool_scale": "pool_scale_2", "w0": "rwkv_w0",
            "a0": "rwkv_a0", "k_k": "rwkv_k_k", "k_a": "rwkv_k_a", "r_k": "rwkv_r_k", "ln_w": "rwkv_ln_w",
            "ln_b": "rwkv_ln_b", "subln": "subln_g_2"}
    params = np.concatenate([(mu if n == "mu" else x[cols[n]]).reshape(-1, P).T for n in PARAM_COLS], 1)
    arrays = {
        "w": np.stack(units), "params": params,
        "x": x["x"][0].T.reshape(KT, P, T).transpose(1, 0, 2), "p": x["p"][0, 0].T.reshape(2, P, T).transpose(1, 0, 2),
        "w2": x["rwkv_w2"][0], "a2": x["rwkv_a2"][0], "g2": x["rwkv_g2"][0], "positions": x["positions_2"],
        "lam0": x["lam_q1_2"], "lam1": x["lam_k1_2"], "lam2": x["lam_q2_2"], "lam3": x["lam_k2_2"],
        **shape_constants(),
    }
    arrays = {k: np.ascontiguousarray(v) for k, v in arrays.items()}
    nc = bacc.Bacc("TRN2", target_bir_lowering=False, num_devices=1)
    aps = {k: nc.dram_tensor(f"in_{k}", v.shape, mybir.dt.from_np(v.dtype), kind="ExternalInput").ap()
           for k, v in arrays.items()}
    aps["out"] = nc.dram_tensor("out_0", (P, KT, T), F32, kind="ExternalOutput").ap()
    build(nc, aps)
    result = run_bass_kernel_spmd(nc, [{f"in_{k}": v for k, v in arrays.items()}], core_ids=[0])
    out = result.results[0]["out_0"]
    return out.transpose(1, 0, 2).reshape(D, T).T.reshape(1, T, D)
```

```python
from contextlib import ExitStack, contextmanager

import numpy as np

import concourse.bass as bass
from concourse import mybir

F32 = mybir.dt.float32
F32R = mybir.dt.float32r
I32 = mybir.dt.int32
ALU = mybir.AluOpType
ACT = mybir.ActivationFunctionType

P = 128
T = 512
D = 1024
KT = D // P
NT = T // P
HD = 64
DFF = 4 * D
EPS = 1e-6
GN_EPS = 64e-5
NEG = -1.0e30

N_QKV = 18
N_RWKV = 14
U_QKV = 0
U_LORA = U_QKV + N_QKV
U_RKV = U_LORA + 2
U_GATE = U_LORA + N_RWKV
U_UP = U_GATE + 2 * KT
U_OUT = U_UP + KT
U_FFN = U_OUT + KT
U_PLE = U_FFN + 64
U_HEADS = U_PLE + KT
U_STEP = U_HEADS + 3
U_GATE2 = U_STEP + 32
N_EARLY = 6
U_OUT2 = U_GATE2 + 2 * KT - N_EARLY
U_FFN2 = U_OUT2 + KT
N_UNITS = U_FFN2 + 64
RING = 4

START_CLOCK = 24

MERGE_ORDER = (3, 0, 4, 1, 5, 2, 6, 7)

O_QKV = 0
O_RWKV = O_QKV + N_QKV
O_GATE = O_RWKV + N_RWKV
O_OUT = O_GATE + 2 * KT
O_FFN = O_OUT + KT
O_PLE = O_FFN + 48
O_HEADS = O_PLE + KT
O_GATE2 = O_HEADS + 3 + 31
O_OUT2 = O_GATE2 + 2 * KT - N_EARLY
O_FFN2 = O_OUT2 + KT

POOL_SPLIT_STEPS = (6, 10, 14, 18)
POOLW_STEP = 19


def step_unit(i):
    n, qt = i // 4, i % 4
    if n == 7:
        kind = ("gate", 2 + qt)
    elif qt < 3:
        kind = ("head", 3 * (n + 1) + qt)
    elif n < 4:
        kind = ("pool", n)
    else:
        kind = ("pool_weights", 0) if n == 4 else ("gate", n - 5)
    return kind, O_HEADS + 3 + i - (i > POOLW_STEP)


FILL_AHEAD = 28
FILL = {"turned": 2, "lower": 6, "mv": 1, "wu": 1, "chunks": 6, "states": 6, "mean": 2, "var": 1}


def gates_done(hp, place):
    names = list(FILL)
    before = sum(FILL[n] for n in names[:names.index(place) + 1])
    return min((FILL_AHEAD + sum(FILL.values()) * hp + before) // KT, 2 * KT)


POST_NORMS = (1, 3, 4, 7)
ADDED = (0, 1, 3, 4, 6, 7)
INPUTS = (0, 2, None, 5, 6)

PARAM_COLS = {}


def _columns():
    at = 0
    for name, n in (("mix_pre", 8), ("mix_post", 8), ("ffn_pre", 8), ("ffn_post", 8), ("ple_post", 8),
                    ("attn2", 8), ("mlp2", 8), ("final", 8), ("pool_scale", 8), ("mu", 14), ("w0", 4),
                    ("a0", 4), ("k_k", 4), ("k_a", 4), ("r_k", 4), ("ln_w", 4), ("ln_b", 4), ("subln", 1)):
        PARAM_COLS[name] = at
        at += n
    return at


N_PARAMS = _columns()

MATS = ("ident", "ones", "head_ones", "head_mean")
SCAN_MASKS = ("pair_lower", "pair_upper", "before", "upto", "lvl1", "lvl2", "lvl3", "lvl4", "lvl5")
LAM_INIT = 0.8 - 0.6 * float(np.exp(-0.0))


def shape_constants():
    i = np.arange(P)
    m = {"ident": np.eye(P), "ones": np.ones((P, P))}
    same_head = (i[:, None] // HD == i[None, :] // HD).astype(float)
    m["head_ones"], m["head_mean"] = same_head, same_head / HD
    r1, r2 = np.zeros((P, P)), np.zeros((P, P))
    for b in (0, 64):
        for j in range(32):
            r1[b + j, b + j + 32], r1[b + j + 32, b + j] = -1, 1
        for j in range(8):
            r2[b + j, b + j + 8], r2[b + j + 8, b + j] = -1, 1
    m["rot1"], m["rot2"] = r1.T, r2.T
    row, col = i[:, None], i[None, :]
    m["pair_lower"] = ((row == col + 1) & (col % 2 == 0)).astype(float)
    m["pair_upper"] = m["pair_lower"].T
    chunk = row // 64 == col // 64
    m["before"] = (chunk & (row < col)).astype(float)
    m["upto"] = (chunk & (row <= col)).astype(float)
    for l in range(1, 6):
        b = 2 ** l
        m[f"lvl{l}"] = ((row // (2 * b) == col // (2 * b)) & (row // b % 2 == 1) & (col // b % 2 == 0)).astype(float)
    mats = np.concatenate([m[n] for n in MATS], 1)
    scan_masks = np.concatenate([m[n] for n in SCAN_MASKS], 1)

    q = 4 * i[:, None]
    key = np.arange(T)[None, :]
    by4 = np.where(col <= row, 0.0, NEG)
    by16 = np.where((col <= row) & (col % 4 == row % 4), 0.0, NEG)
    masks = []
    for r in range(4):
        d = q + r - key
        masks += [np.where((d >= 0) & (d <= 128), 0.0, NEG), by4, by16]
    causal = np.where(key <= i[:, None] + 384, 0.0, NEG)
    f = i % HD
    inv1 = (10000.0 ** (-np.arange(0, HD, 2, dtype=np.float32) / np.float32(HD))).astype(np.float32)
    ang = (np.arange(T, dtype=np.float32)[None, :] * inv1[f % 32][:, None]).astype(np.float32).astype(np.float64)
    table1 = np.concatenate([np.cos(ang), np.sin(ang)], 1)
    inv2 = (500000.0 ** (-np.arange(0, 16, 2, dtype=np.float32) / np.float32(16))).astype(np.float32)
    invf2 = np.where(f < 16, inv2[f % 8], 0.0)
    small = np.zeros((P, 68))
    small[:, 0], small[:, 1], small[:, 2] = invf2, EPS, GN_EPS
    for g, w in enumerate((2, 4, 8, 16)):
        small[:, 4 + 16 * g:20 + 16 * g] = 1.0 / np.minimum(np.arange(16) + 1, w)
    c = np.ascontiguousarray
    f32 = np.float32
    return {"mats": c(mats, f32), "scan_masks": c(scan_masks, f32), "masks1": c(np.concatenate(masks, 1), f32),
            "causal": c(causal, f32), "table1": c(table1, f32), "rot1": c(m["rot1"], f32), "rot2": c(m["rot2"], f32), "small": c(small, f32)}


class Lane:

    def __init__(self, eng, sem, name):
        self.eng, self.sem, self.eng_name = eng, sem, name
        self.count, self.turn, self.each = {}, None, {}

    def value(self, name):
        n = self.count[name]
        return n + self.turn * self.each[name] if self.turn is not None else n

    def do(self, instruction, name="chain"):
        name = f"{self.eng_name}_{name}" if name == "chain" else name
        self.count[name] = self.count.get(name, 0) + 1
        instruction.then_inc(self.sem(name), 1)
        self.eng.wait_ge(self.sem(name), self.value(name))

    def ahead(self, instruction, name):
        self.count[name] = self.count.get(name, 0) + 1
        instruction.then_inc(self.sem(name), 1)

    def leaves(self, o):
        name = f"out_evicted{o % 2}"
        self.count[name] = o // 2
        return name

    @contextmanager
    def loop(self, turns, each):
        each = {(f"{self.eng_name}_chain" if k == "chain" else k): v for k, v in each.items()}
        before = dict(self.count)
        with self.eng.Fori(0, turns, 1) as g:
            self.turn, self.each = g, each
            yield g
        self.turn = None
        for k in [k for k in each if not k.startswith("out_evicted")]:
            assert self.count[k] - before.get(k, 0) == each[k], (k, self.count[k], before.get(k), each[k])
            self.count[k] += each[k] * (turns - 1)


def build(nc, a):
    ctx = ExitStack()
    with ctx:
        sems = {}

        def S(name):
            if name not in sems:
                sems[name] = ctx.enter_context(nc.semaphore(name))
            return sems[name]

        def sbuf(stack, name, shape, dt=F32):
            return stack.enter_context(nc.sbuf_tensor(name, shape, dt))

        h = sbuf(ctx, "h", [P, KT, T])
        raw = [sbuf(ctx, f"raw{i}", [P, KT, P]) for i in range(RING)]
        WH = [sbuf(ctx, f"w_high{i}", [P, KT, P], F32R) for i in range(RING)]
        WL = [sbuf(ctx, f"w_low{i}", [P, KT, P], F32R) for i in range(RING)]
        UH = sbuf(ctx, "u_high", [P, KT, T], F32R)
        UL = sbuf(ctx, "u_low", [P, KT, T], F32R)
        par = sbuf(ctx, "params", [P, N_PARAMS])
        mats = sbuf(ctx, "mats", [P, len(MATS) * P])
        small = sbuf(ctx, "small", [P, 68])
        rstd = sbuf(ctx, "rstd", [P, T])
        acc = sbuf(ctx, "acc", [P, T])
        roots = sbuf(ctx, "roots", [P, 2 * NT])
        sq = sbuf(ctx, "sq", [P, T])
        tmp = [sbuf(ctx, f"tmp{i}", [P, T]) for i in range(2)]
        PS = ctx.enter_context(nc.psum_tensor("PS", [P, 8, 512], F32))

        M = {n: mats[:, i * P:(i + 1) * P] for i, n in enumerate(MATS)}

        def col(name, j=0):
            return par[:, PARAM_COLS[name] + j:PARAM_COLS[name] + j + 1]

        def over(m, n=NT):
            return m.unsqueeze(1).to_broadcast([P, n, P])

        def flat(x):
            return x.rearrange("p a b -> p (a b)")

        def blk(x):
            return x.rearrange("p (a b) -> p a b", b=P)

        mix = ExitStack()
        OH = sbuf(mix, "o_high", [P, 2, T], F32R)
        OL = sbuf(mix, "o_low", [P, 2, T], F32R)

        att = ExitStack()
        aq = sbuf(att, "qk1", [P, 12, T])
        av = sbuf(att, "v1", [P, NT, 3, 256])
        table1 = sbuf(att, "table1", [P, 2 * T])
        rot1 = sbuf(att, "rotation1", [P, P])
        masks1 = sbuf(att, "masks1", [P, 4 * 768])
        sp1 = [sbuf(att, f"probs1_{i}", [P, 768]) for i in range(2)]
        pt1 = [sbuf(att, f"probsT1_{i}", [P, 768]) for i in range(2)]
        oA = sbuf(att, "o1", [P, 2, T])
        st = sbuf(att, "stats1", [P, 8])
        rt = sbuf(att, "rope_tmp", [P, T])
        zs = [sbuf(att, f"z_out{i}", [P, T]) for i in range(2)]
        att.close()

        YH = sbuf(mix, "y_high", [P, 4, T], F32R)
        YL = sbuf(mix, "y_low", [P, 4, T], F32R)
        rw = ExitStack()
        smask = sbuf(rw, "scan_masks", [P, len(SCAN_MASKS) * P])
        K_ = {n: smask[:, i * P:(i + 1) * P] for i, n in enumerate(SCAN_MASKS)}
        lora_w = sbuf(rw, "lora_w", [P, 512])
        lora_g = sbuf(rw, "lora_g", [P, 512])
        zp = [sbuf(rw, f"z_padded{i}", [P, T + 1]) for i in range(3)]
        la = sbuf(rw, "lora_in", [P, T])
        lg = sbuf(rw, "lora_gate", [P, T])
        G = sbuf(rw, "transitions", [P, 6, P])
        H = sbuf(rw, "chunk_inputs", [P, 7, P])
        St = sbuf(rw, "states", [P, 6, P])
        vs = sbuf(rw, "v_feature", [P, T])
        gt = sbuf(rw, "gate_feature", [P, T])
        PP = sbuf(rw, "decay_product", [P, 8, 65])
        FR, FA, FB, FK = (sbuf(rw, n, [P, T]) for n in ("r_scaled", "a_scaled", "b_scaled", "k_scaled"))
        bonus = acc
        RHS = sbuf(rw, "a_and_mv", [P, 2, NT, P])
        Bt, Kt, Vt = (sbuf(rw, n, [P, NT, P]) for n in ("b_token", "k_token", "v_token"))
        Lt, X, Y, Z = (sbuf(rw, n, [P, 2, T]) for n in ("lower_T", "inverse", "inverse_T", "product"))
        gs = [sbuf(rw, f"gate_out{i}", [P, T]) for i in range(2)]
        omka = sbuf(rw, "one_minus_ka", [P, 4])
        restart = sbuf(rw, "restart", [P, 8, 64])
        ends = sbuf(rw, "chunk_decay", [P, 8])
        scrap = sbuf(rw, "scrap", [P, 2])
        next_bonus = flat(St[:, 0:4, :])
        next_gate = flat(H[:, 0:4, :])
        rs, ks = Lt[:, 0, :], Lt[:, 1, :]
        wsum, aa = X[:, 0, :], X[:, 1, :]
        kk, ip = Y[:, 0, :], Y[:, 1, :]
        rw.close()

        late = ExitStack()
        ple = late.enter_context(nc.sbuf_tensor("ple", [P, KT, T], F32, side="right"))
        PH = sbuf(mix, "p_high", [P, 2, T], F32R)
        PL = sbuf(mix, "p_low", [P, 2, T], F32R)
        pf = sbuf(mix, "p_in", [P, 2, T])
        mg = ExitStack()
        MH = sbuf(mg, "merged_high", [P, KT, T], F32R)
        ML = sbuf(mg, "merged_low", [P, KT, T], F32R)
        gin = [sbuf(mg, f"gate_in{i}", [P, T]) for i in range(4)]
        mg.close()
        mix.close()

        ff = ExitStack()
        t8 = sbuf(ff, "branch_out", [P, KT, T])
        FH = sbuf(ff, "hidden_high", [P, 16, T], F32R)
        FL = sbuf(ff, "hidden_low", [P, 16, T], F32R)
        ff.close()
        late.close()

        b2 = ExitStack()
        aT = sbuf(b2, "attn_out2", [P, KT, T])
        poolT = sbuf(b2, "pool_out2", [P, KT, T])
        b2w = ExitStack()
        rot2 = sbuf(b2w, "rotation2", [P, P])
        table2 = sbuf(b2w, "table2", [P, 2 * T])
        causal = sbuf(b2w, "causal", [P, T])
        pos = sbuf(b2w, "positions", [P, T], I32)
        rt2 = sbuf(b2w, "rope_tmp2", [P, T])
        lam4 = sbuf(b2w, "lam_vectors", [P, 4, HD])
        lamw = sbuf(b2w, "lam_work", [P, 8])
        q2 = [sbuf(b2w, f"q2_{i}", [P, T]) for i in range(2)]
        k2 = [sbuf(b2w, f"k2_{i}", [P, T]) for i in range(2)]
        v2 = [sbuf(b2w, f"v2_{i}", [P, NT, P]) for i in range(2)]
        e2 = [sbuf(b2w, f"exp2_{i}", [P, 2, T]) for i in range(2)]
        pt2 = [sbuf(b2w, f"weightsT2_{i}", [P, T]) for i in range(2)]
        st2 = sbuf(b2w, "stats2", [P, 2, 8])
        pz, pa, pb = (sbuf(b2w, n, [P, 16 + T]) for n in ("pool_in", "pool_sum_a", "pool_sum_b"))
        b2p = ExitStack()
        DH = sbuf(b2p, "pool_high", [P, 4, T], F32R)
        DL = sbuf(b2p, "pool_low", [P, 4, T], F32R)
        b2p.close()
        gates2 = sbuf(b2w, "early_gates", [P, N_EARLY, T])
        b2w.close()
        M2H = sbuf(b2, "merged2_high", [P, KT, T], F32R)
        M2L = sbuf(b2, "merged2_low", [P, KT, T], F32R)
        b2.close()
        f2 = ExitStack()
        F2H = sbuf(f2, "hidden2_high", [P, 16, T], F32R)
        F2L = sbuf(f2, "hidden2_low", [P, 16, T], F32R)
        f2.close()

        def late_gates(m):
            return (tmp[0][:], tmp[1][:]) if m % 2 else (sq[:], acc[:])

        z_dram = nc.dram_tensor("z_spill", (N_RWKV, P, T), F32, kind="Internal").ap()
        gate_dram = nc.dram_tensor("gate_spill", (2 * KT, P, T), F32, kind="Internal").ap()

        def half_columns(x, l, half):
            return x.rearrange("p (q h b) -> p q h b", h=2, b=2 ** l)[:, :, half, :]

        def evicted(o):
            return S(f"out_evicted{o % 2}"), o // 2 + 1

        block = ctx.enter_context(nc.Block())

        @block.sync
        def _(sp):
            groups = a["w"][0:(N_UNITS // RING) * RING].rearrange("(g s) p k n -> g s p k n", s=RING)
            sp.dma_start(raw[0][:], a["w"][0]).then_inc(S("raw_in0"), 16)
            for m in range(1, KT, 2):
                sp.dma_start(h[:, m, :], a["x"][:, m, :]).then_inc(S(f"x_in{m}"), 16)
            for s in range(1, RING):
                sp.dma_start(raw[s][:], a["w"][s]).then_inc(S(f"raw_in{s}"), 16)
            with sp.Fori(1, N_UNITS // RING, 1) as g:
                for s in range(RING):
                    sp.wait_ge(S("split_done"), g * RING + (s + 1 - RING))
                    sp.dma_start(raw[s][:], groups[g, s]).then_inc(S(f"raw_in{s}"), 16)
            for u in range((N_UNITS // RING) * RING, N_UNITS):
                sp.wait_ge(S("split_done"), u + 1 - RING)
                sp.dma_start(raw[u % RING][:], a["w"][u]).then_inc(S(f"raw_in{u % RING}"), 16)
            sp.wait_ge(S("stored"), 16 * KT)

        @block.gpsimd
        def _(pool):
            lane = Lane(pool, S, "pool")

            def split(s, arrived, free):
                pool.wait_ge(S(f"raw_in{s}"), arrived)
                if free is not None:
                    pool.wait_ge(S("units_done"), free)
                    pool.sem_inc(S("slot_taken"), 1)
                lane.do(nc.gpsimd.tensor_scalar(flat(WH[s][:]), flat(raw[s][:]), 1.0, 0.0, ALU.mult, ALU.add),
                        "split_high")
                nc.gpsimd.tensor_tensor(flat(WL[s][:]), flat(raw[s][:]), flat(WH[s][:]).bitcast(F32),
                                        ALU.subtract).then_inc(S("split_done"), 1)

            def split_units(first, end):
                a, b = -(-first // RING), end // RING
                for u in list(range(first, min(a * RING, end))):
                    lane.count["split_high"] = u
                    split(u % RING, 16 * (u // RING + 1), u + 1 - RING if u >= RING else None)
                lane.count["split_high"] = a * RING
                with pool.Fori(a, b, 1) as g:
                    lane.turn, lane.each = g - a, {"split_high": RING}
                    for s in range(RING):
                        split(s, g * 16 + 16, g * RING + (s + 1 - RING))
                    lane.turn = None
                for u in range(b * RING, end):
                    lane.count["split_high"] = u
                    split(u % RING, 16 * (u // RING + 1), u + 1 - RING)

            for s in range(RING):
                lane.count["split_high"] = s
                split(s, 16, None)
            done = RING
            for n, u in enumerate((U_FFN, U_PLE, U_HEADS)):
                split_units(done, u + RING)
                done = u + RING
                for m in range(KT):
                    pool.wait_ge(S("branch_scaled"), KT * n + m + 1)
                    nc.gpsimd.tensor_tensor(h[:, m, :], h[:, m, :], t8[:, m, :], ALU.add).then_inc(S("h_new"), 1)
            split_units(done, N_UNITS)

        @block.tensor
        def _(pe):
            def mm(out, lhsT, rhs, start=True, stop=True):
                return nc.tensor.matmul(out, lhsT, rhs, start=start, stop=stop)

            def product(out, s, slices, high, low, wait_slice=None, start=True, stop=True, after_slice=None):
                for n, (k, r) in enumerate(slices):
                    if wait_slice is not None:
                        wait_slice(r)
                    first, last = start and n == 0, stop and n == len(slices) - 1
                    mm(out, WH[s][:, k, :], high[:, r, :], first, False)
                    mm(out, WH[s][:, k, :], low[:, r, :], False, False)
                    i = mm(out, WL[s][:, k, :], high[:, r, :], False, last)
                    if after_slice is not None and n < len(slices) - 1:
                        after_slice(r)
                return i

            ALL = [(k, k) for k in range(KT)]

            def unit(u, o, high, low, wait_slice=None, after_slice=None):
                pe.wait_ge(S("split_done"), u + 1)
                if u == U_STEP + POOLW_STEP + 1:
                    pe.wait_ge(S("pool_copied"), KT)
                if o >= 2:
                    pe.wait_ge(*evicted(o - 2))
                product(PS[:, o % 2, :], u % RING, ALL, high, low, wait_slice, after_slice=after_slice)\
                    .then_inc(S("units_done"), 1)

            class Filler:

                def __init__(self, u, o, n):
                    self.u, self.o, self.left, self.k = u, o, n * KT, 0

                def slices(self, n):
                    for _ in range(min(n, self.left)):
                        if self.k == 0:
                            pe.wait_ge(S("split_done"), self.u + 1)
                            pe.wait_ge(*evicted(self.o - 2))
                        x = product(PS[:, self.o % 2, :], self.u % RING, [(self.k, self.k)], UH, UL,
                                    start=self.k == 0, stop=self.k == KT - 1)
                        self.k, self.left = self.k + 1, self.left - 1
                        if self.k == KT:
                            x.then_inc(S("units_done"), 1)
                            self.k, self.u, self.o = 0, self.u + 1, self.o + 1

            def units_loop(u, o, n, high, low):
                with pe.Fori(0, n // 4, 1) as g:
                    for j in range(4):
                        pe.wait_ge(S("split_done"), g * 4 + (u + j + 1))
                        pe.wait_ge(S(f"out_evicted{(o + j) % 2}"), g * 2 + (o + j) // 2)
                        product(PS[:, (o + j) % 2, :], (u + j) % RING, ALL, high, low)\
                            .then_inc(S("units_done"), 1)

            def sum_tokens(squares, first, last):
                for t in range(NT):
                    x = mm(PS[:, 4 + t, 0:1], squares[:, t * P:(t + 1) * P], M["ones"][:, 0:1], first, last)
                return x

            def keep_clock(n):
                for _ in range(n):
                    mm(PS[:, 2, 0:P], M["ones"], M["ones"])

            def spread(n):
                pe.wait_ge(S("diag_ready"), n + 1)
                mm(PS[:, 3, :], M["ones"], acc[:]).then_inc(S("rms_spread"), 1)

            def post_norm(n):
                keep_clock(10)
                pe.wait_ge(S("squares_summed"), KT * (ADDED.index(n) + 1))
                sum_tokens(acc[:], True, True).then_inc(S("norm_summed"), 1)
                keep_clock(6)
                spread(n)
                if n != 7:
                    keep_clock(18)

            def first_units(u, o, n, squares):
                def add_squares(k):
                    pe.wait_ge(S("squared"), KT * n + k + 1)
                    x = sum_tokens(squares[:, k, :], k == 0, k == KT - 1)
                    if k == KT - 1:
                        x.then_inc(S("norm_summed"), 1)

                unit(u, o, UH, UL, lambda k: pe.wait_ge(S("u_low"), KT * INPUTS.index(n) + k + 1),
                     None if n in ADDED else add_squares)
                if n in ADDED:
                    pe.wait_ge(S("squares_summed"), KT * (ADDED.index(n) + 1))
                    sum_tokens(acc[:], True, True).then_inc(S("norm_summed"), 1)
                else:
                    add_squares(KT - 1)
                unit(u + 1, o + 1, UH, UL, None, lambda k: spread(n) if k == 3 else None)

            def input_split(n):
                return lambda k: pe.wait_ge(S("u_low"), KT * n + k + 1)

            def after_qkv(o):
                pe.wait_ge(*evicted(o))
                if o < 12:
                    if o >= 2:
                        pe.wait_ge(S("roped"), o - 1)
                    mm(PS[:, 2 + o % 2, :], rot1[:], tmp[o % 2][:]).then_inc(S("rotated"), 1)
                else:
                    i = o - 12
                    if i >= 2:
                        pe.wait_ge(S("v_token"), i - 1)
                    for t in range(NT):
                        src = tmp[o % 2][:, t * P:(t + 1) * P] if i < 2 else tmp[o % 2][:, t::4]
                        x = nc.tensor.transpose(PS[:, 4 + o % 2, t * P:(t + 1) * P], src, M["ident"])
                    x.then_inc(S("v_turned"), 1)

            pe.wait_ge(S("mats_in"), 16)
            keep_clock(START_CLOCK)
            for o in range(N_QKV):
                if o == 0:
                    first_units(U_QKV, O_QKV, 0, aq)
                elif o > 1:
                    unit(U_QKV + o, O_QKV + o, UH, UL)
                if o:
                    after_qkv(o - 1)
            after_qkv(N_QKV - 1)

            def scores(i):
                r, n = i // 4, i % 4
                half, row = n // 2, 64 * (n % 2)
                if i == 0:
                    pe.wait_ge(S("roped"), 12)
                    pe.wait_ge(S("v_token"), 6)
                if i >= 1:
                    pe.wait_ge(S("masked"), i)
                b = 2
                for g in range(3):
                    q = aq[row:row + 64, 2 * g + half, r::4]
                    k = aq[row:row + 64, 6 + 2 * g + half, :] if g == 0 else aq[row:row + 64, 6 + 2 * g + half, r::4]
                    out = PS[:, b, :] if g == 0 else PS[:, b + 1, (g - 1) * P:g * P]
                    x = mm(out, q, k)
                x.then_inc(S("scores"), 1)

            def turn_probs(i):
                pe.wait_ge(S("probs"), i + 1)
                if i >= 1:
                    pe.wait_ge(S("probs_copied"), i)
                for j in range(6):
                    x = nc.tensor.transpose(PS[:, 4 + j // 4, (j % 4) * P:(j % 4 + 1) * P],
                                            sp1[i % 2][:, j * P:(j + 1) * P], M["ident"])
                x.then_inc(S("probs_turned"), 1)

            def values(i):
                r, n = i // 4, i % 4
                row = 64 * (n % 2)
                pe.wait_ge(S("probs_copied"), i + 1)
                if i >= 2:
                    pe.wait_ge(S("o_copied"), i - 1)
                out = PS[row:row + 64, 6 + i % 2, 0:P]
                for j in range(6):
                    g, t = (0, j) if j < 4 else (j - 3, r)
                    x = mm(out, av[:, t, g, n * 64:(n + 1) * 64], pt1[i % 2][:, j * P:(j + 1) * P],
                           j == 0, j == 5)
                x.then_inc(S("o_done"), 1)

            gates = Filler(U_GATE, O_GATE, 2 * KT)
            for i in range(16 + 2):
                if i < 16:
                    scores(i)
                if i < N_RWKV:
                    unit(U_LORA + i, O_RWKV + i, UH, UL)
                elif i < 16:
                    gates.slices(4)
                if 1 <= i < 17:
                    turn_probs(i - 1)
                if i >= 2:
                    values(i - 2)

            def lora(bank, w, x, rows, hp):
                mm(PS[:, bank, :], w[rows, hp * P:(hp + 1) * P], x[rows, :]).then_inc(S("lora_done"), 1)

            def key_norm(hp):
                pe.wait_ge(S("k_squared"), hp + 1)
                mm(PS[:, 2, :], M["head_ones"], sq[:]).then_inc(S("k_summed"), 1)

            def bonus_and_gate(hp):
                pe.wait_ge(S("rk_ready"), hp + 1)
                mm(PS[:, 6, :], M["head_ones"], tmp[1][:]).then_inc(S("rk_summed"), 1)
                lora(7, lora_g, lg, slice(0, 96), hp)

            gates.slices(10)
            pe.wait_ge(S("lora_in"), 2)
            pe.wait_ge(S("scan_consts_in"), 64)
            pe.wait_ge(S("o_copied"), 16)
            lora(4, lora_w, la, slice(0, 32), 0)
            lora(5, lora_w, la, slice(32, 64), 0)
            key_norm(0)
            gates.slices(5)
            bonus_and_gate(0)
            gates.slices(FILL_AHEAD - 8 - 10 - 5)
            for hp in range(4):
                for n, (src, bank) in enumerate(((FA, 2), (FB, 3), (vs, 5), (FK, 4))):
                    pe.wait_ge(S("scaled"), 4 * hp + (1, 2, 2, 3)[n])
                    if n == 2:
                        pe.wait_ge(S("lora_used"), 3 * hp + 2)
                    if n == 2 and hp:
                        pe.wait_ge(S("y_centered"), hp)
                    if n == 3 and hp:
                        pe.wait_ge(S("y_root"), hp)
                    for t in range(NT):
                        x = nc.tensor.transpose(PS[:, bank, t * P:(t + 1) * P], src[:, t * P:(t + 1) * P], M["ident"])
                    x.then_inc(S("turned"), 1)
                gates.slices(FILL["turned"])

                def tokens(banks, lhsT, rhs, signal):
                    for t in range(NT):
                        b = slice(t * P, (t + 1) * P)
                        for e in range(2):
                            r = slice(64 * e, 64 * e + 64)
                            x = mm(PS[:, banks[e], b], lhsT[r, b], rhs[r, b])
                            if signal and t == NT - 1:
                                x.then_inc(S(signal), 1)

                pe.wait_ge(S("scaled"), 4 * hp + 4)
                pe.wait_ge(S("token_a"), 3 * (hp + 1))
                pe.wait_ge(S("token_d"), 2 * (hp + 1))
                tokens((2, 4), FA, FB, "lower_done")
                tokens((3, 5), FB, FA, "upper_done")
                gates.slices(FILL["lower"])
                pe.wait_ge(S("bonus_ready"), hp + 1)
                pe.wait_ge(S("lora_used"), 3 * hp + 3)
                for l in range(1, 6):
                    for e in range(2):
                        pe.wait_ge(S("inverse_ready"), 12 * hp + 2 * (l - 1) + e + 1)
                        for t in range(NT):
                            b = slice(t * P, (t + 1) * P)
                            x = mm(PS[:, 6 + e, b], Lt[:, e, b], X[:, e, b])
                        x.then_inc(S("lx_done"), 1)
                    for e in range(2):
                        pe.wait_ge(S("lx_masked"), 10 * hp + 2 * (l - 1) + e + 1)
                        for t in range(NT):
                            b = slice(t * P, (t + 1) * P)
                            if l < 5:
                                mm(PS[:, 2 + e, b], Y[:, e, b], Z[:, e, b])
                            x = mm(PS[:, 4 + e, b], Z[:, e, b], Y[:, e, b])
                        x.then_inc(S("xlx_done"), 1)
                pe.wait_ge(S("inverse_ready"), 12 * (hp + 1))
                for n, (l, r) in enumerate(((FK, FA), (FB, FR), (FK, FR))):
                    tokens((2 + 2 * n, 3 + 2 * n), l, r, "pairs_done")
                for e in range(2):
                    pe.wait_ge(S("pairs_masked"), 6 * hp + 1 + e)
                    for t in range(NT):
                        x = mm(PS[:, 2 + e, t * 64:(t + 1) * 64], Lt[:, e, t * P:(t + 1) * P],
                               Vt[:, t, 64 * e:64 * e + 64])
                    x.then_inc(S("mv_done"), 1)
                gates.slices(FILL["mv"])
                for e in range(2):
                    pe.wait_ge(S("mv_copied"), 2 * hp + e + 1)
                    pe.wait_ge(S("pairs_masked"), 6 * hp + 3 + e)
                    for t in range(NT):
                        x = mm(PS[:, 4 + e, t * P:(t + 1) * P], Y[:, e, t * P:(t + 1) * P], RHS[:, e, t, :])
                    x.then_inc(S("wu_done"), 1)
                gates.slices(FILL["wu"])
                if hp < 3:
                    key_norm(hp + 1)
                WU = Z[:].rearrange("p w (t n) -> p w t n", t=NT)
                mrk = (FA, FB)
                pe.wait_ge(S("wu_copied"), 4 * hp + 4)
                pe.wait_ge(S("pairs_masked"), 6 * hp + 6)
                for t in range(NT):
                    b = slice(t * P, (t + 1) * P)
                    for src, right, first, last, bank in ((0, X, True, True, 6), (1, X, True, False, 7),
                                                          (None, mrk, False, True, 7)):
                        for e in range(2):
                            r = slice(64 * e, 64 * e + 64)
                            left = Vt[:, t, r] if src is None else WU[:, src, t, r]
                            x = mm(PS[r, bank, b], left, mrk[e][:, b] if src is None else X[:, e, b], first, last)
                x.then_inc(S("qy_done"), 1)
                def parts(ch):
                    r, t = slice(64 * (ch % 2), 64 * (ch % 2) + 64), ch // 2
                    return r, t, slice(t * P, (t + 1) * P)

                for ch in range(7):
                    r, t, b = parts(ch)
                    mm(PS[:, 4 + ch % 2, b], Bt[r, t, :], WU[r, 1, t, :], True, False)
                    mm(PS[:, 4 + ch % 2, b], Kt[r, t, :], Vt[r, t, :], False, True)
                for ch in (1, 3, 5, 2, 4, 6):
                    if hp < 3 and ch == 2:
                        pe.wait_ge(S("k_root"), hp + 2)
                    r, t, b = parts(ch)
                    x = mm(PS[:, 2 + ch % 2, b], WU[r, 0, t, :], Bt[r, t, :])
                x.then_inc(S("chunks_done"), 1)
                gates.slices(FILL["chunks"])
                pe.wait_ge(S("chunks_ready"), 9 * (hp + 1))
                pe.wait_ge(S("q_ready"), hp + 1)
                pe.wait_ge(S("y0_ready"), hp + 1)
                for ch in range(1, 7):
                    if ch > 1:
                        pe.wait_ge(S("state_ready"), 6 * hp + ch - 1)
                    mm(PS[:, 6 + ch % 2, 0:P], G[:, ch - 1, :], H[:, 0, :] if ch == 1 else St[:, ch - 2, :])\
                        .then_inc(S("state_done"), 1)
                    if hp < 3 and ch == 1:
                        lora(4, lora_w, la, slice(0, 32), hp + 1)
                        lora(5, lora_w, la, slice(32, 64), hp + 1)
                    gates.slices(FILL["states"] // 6)
                pe.wait_ge(S("state_ready"), 6 * hp + 6)
                for ch in range(1, 8):
                    b = slice(64 * ch, 64 * ch + 64)
                    x = mm(PS[:, 2, b], H[:, 0, :] if ch == 1 else St[:, ch - 2, :], FR[:, b])
                x.then_inc(S("y_done"), 1)
                if hp < 3:
                    bonus_and_gate(hp + 1)
                    pe.wait_ge(S("lora_used"), 3 * (hp + 1) + 2)
                pe.wait_ge(S("y_ready"), hp + 1)
                mm(PS[:, 5, :], M["head_mean"], FK[:]).then_inc(S("mean_done"), 1)
                gates.slices(FILL["mean"])
                pe.wait_ge(S("y_squared"), hp + 1)
                mm(PS[:, 4, :], M["head_mean"], sq[:]).then_inc(S("var_done"), 1)
                gates.slices(FILL["var"])

            def attention_and_embedding(m):
                u, b = U_UP + m, 2 + 3 * (m % 2)
                pe.wait_ge(S("split_done"), u + 1)
                product(PS[:, b + 2, :], u % RING, [(6, 0), (7, 1)], PH, PL)
                product(PS[:, b, :], u % RING, [(0, 0), (1, 1)], OH, OL)

            pe.wait_ge(S("p_low"), 2)
            pe.wait_ge(S("y_root"), 4)
            attention_and_embedding(0)
            pe.wait_ge(S("bonus_ready"), 4)
            attention_and_embedding(1)
            pe.wait_ge(S("rwkv_out"), 4)
            for m in range(KT):
                if m >= 2:
                    pe.wait_ge(S("merged"), m - 1)
                    pe.wait_ge(S("ple_copied"), m - 1)
                    attention_and_embedding(m)
                product(PS[:, 3 + 3 * (m % 2), :], (U_UP + m) % RING, [(2 + k, k) for k in range(4)], YH, YL)\
                    .then_inc(S("units_done"), 1)
            for m in range(KT):
                unit(U_OUT + m, O_OUT + m, MH, ML,
                     (lambda k: pe.wait_ge(S("merged_low"), k + 1)) if m == 0 else None)
            post_norm(1)

            def feed_forward(U, O, norm, squares, high, low, hid):
                for half in range(2):
                    u, o = U + 32 * half, O + 24 * half
                    if half == 0:
                        first_units(u, o, norm, squares)
                        for j in range(2, 4):
                            unit(u + j, o + j, UH, UL)
                        units_loop(u + 4, o + 4, 12, UH, UL)
                    else:
                        units_loop(u, o, 16, UH, UL)
                    pe.wait_ge(S("hidden_low"), hid + 16 * half + 8)
                    u, o = u + 16, o + 16
                    with pe.Fori(0, 4, 1) as g:
                        for j in range(2):
                            pe.wait_ge(S(f"out_evicted{(o + j) % 2}"), g + (o + j) // 2)
                            for w in range(2):
                                if j == 0 and w == 1:
                                    pe.wait_ge(S("hidden_low"), hid + 16 * (half + 1))
                                pe.wait_ge(S("split_done"), g * 4 + (u + 2 * j + w + 1))
                                product(PS[:, (o + j) % 2, :], (u + 2 * j + w) % RING,
                                        [(k, 8 * w + k) for k in range(KT)], high, low,
                                        start=w == 0, stop=w == 1).then_inc(S("units_done"), 1)

            feed_forward(U_FFN, O_FFN, 2, t8, FH, FL, 0)
            post_norm(3)
            for m in range(KT):
                unit(U_PLE + m, O_PLE + m, UH, UL, input_split(2) if m == 0 else None)
            post_norm(4)

            def after_heads(c, o):
                pe.wait_ge(*evicted(o))
                if c >= 1:
                    pe.wait_ge(S("head_input"), c)
                src = tmp[o % 2]
                if c % 3 < 2:
                    x = mm(PS[:, 2, :], rot2[:], src[:])
                else:
                    for t in range(NT):
                        x = nc.tensor.transpose(PS[:, 2, t * P:(t + 1) * P], src[:, t * P:(t + 1) * P], M["ident"])
                x.then_inc(S("head_turned"), 1)

            def scores2(i):
                n, qt = i // 4, i % 4
                if qt == 0:
                    pe.wait_ge(S("head_input"), 3 * n + 3)
                if i >= 1:
                    pe.wait_ge(S("masked2"), 2 * i)
                for c in range(2):
                    r = slice(64 * c, 64 * c + 64)
                    x = mm(PS[:, 4 + c, 0:P * (qt + 1)], q2[n % 2][r, qt * P:(qt + 1) * P],
                           k2[n % 2][r, 0:P * (qt + 1)])
                x.then_inc(S("scores2"), 1)

            def turn_weights(i):
                qt = i % 4
                pe.wait_ge(S("weights2"), i + 1)
                if i >= 1:
                    pe.wait_ge(S("weights_copied"), i)
                for j in range(qt + 1):
                    x = nc.tensor.transpose(PS[:, 3, j * P:(j + 1) * P], e2[i % 2][:, 0, j * P:(j + 1) * P], M["ident"])
                x.then_inc(S("weights_turned"), 1)

            def values2(i):
                n, qt = i // 4, i % 4
                pe.wait_ge(S("weights_copied"), i + 1)
                if qt == 0 and n >= 1:
                    pe.wait_ge(S("a_copied"), n)
                for j in range(qt + 1):
                    x = mm(PS[:, 6, qt * P:(qt + 1) * P], v2[n % 2][:, j, :], pt2[i % 2][:, j * P:(j + 1) * P],
                           j == 0, j == qt)
                x.then_inc(S("a_done"), 1)

            def head_sum(n):
                pe.wait_ge(S("a_squared"), n + 1)
                if n:
                    pe.wait_ge(S("a_scaled"), n)
                for t in range(NT):
                    x = mm(PS[:, 7, t:t + 1], sq[:, t * P:(t + 1) * P], M["ones"][:, 0:1])
                x.then_inc(S("a_summed"), 1)

            def head_spread(n):
                pe.wait_ge(S("a_diag"), n + 1)
                mm(PS[:, 7, :], M["ones"], acc[:]).then_inc(S("a_spread"), 1)

            def pool_products():
                u = U_STEP + POOLW_STEP
                pe.wait_ge(S("split_done"), u + 1)
                for m in range(KT):
                    pe.wait_ge(S("pooled_low"), m // 2 + 1)
                    if m == 0:
                        pe.wait_ge(*evicted(step_unit(POOLW_STEP - 1)[1]))
                        pe.wait_ge(*evicted(step_unit(POOLW_STEP - 2)[1]))
                    if m >= 2:
                        pe.wait_ge(S("pool_copied"), m - 1)
                    product(PS[:, m % 2, :], u % RING, [(m, m // 2)], DH, DL)\
                        .then_inc(S("pool_done") if m < KT - 1 else S("units_done"), 1)

            first_units(U_HEADS, O_HEADS, 5, t8)
            after_heads(0, O_HEADS)
            unit(U_HEADS + 2, O_HEADS + 2, UH, UL)
            after_heads(1, O_HEADS + 1)
            unit(U_STEP, step_unit(0)[1], UH, UL)
            after_heads(2, O_HEADS + 2)
            for i in range(32 + 2):
                n, qt = i // 4, i % 4
                if i < 32:
                    scores2(i)
                if 1 <= i < 33:
                    (kind, c), o = step_unit(i - 1)
                    if kind == "head":
                        after_heads(c, o)
                if 1 <= i < 32:
                    (kind, c), o = step_unit(i)
                    if kind == "pool_weights":
                        pool_products()
                    else:
                        unit(U_STEP + i, o, UH, UL)
                elif i >= 32:
                    unit(U_GATE2 + i - 32, O_GATE2 + i - 32, UH, UL)
                if 1 <= i < 33:
                    turn_weights(i - 1)
                if i >= 2:
                    values2(i - 2)
                if i >= 6 and i % 4 == 2:
                    head_sum((i - 6) // 4)
                if i >= 7 and i % 4 == 3:
                    head_spread((i - 7) // 4)
            head_sum(7)
            unit(U_GATE2 + 2, O_GATE2 + 2, UH, UL)
            head_spread(7)

            for g in range(3, 2 * KT - N_EARLY):
                unit(U_GATE2 + g, O_GATE2 + g, UH, UL)
            for m in range(KT):
                unit(U_OUT2 + m, O_OUT2 + m, M2H, M2L,
                     (lambda k: pe.wait_ge(S("merged_low"), KT + MERGE_ORDER.index(k) + 1)) if m == 0 else None)
            feed_forward(U_FFN2, O_FFN2, 6, aT, F2H, F2L, 32)
            post_norm(7)

        @block.scalar
        def _(act):
            lane = Lane(act, S, "act")

            def f(out, in_, func, name="chain", **more):
                lane.do(nc.scalar.activation(out, in_, func, **more), name)

            def ahead(out, in_, func, name, **more):
                lane.ahead(nc.scalar.activation(out, in_, func, **more), name)

            act.dma_start(par[:], a["params"]).then_inc(S("params_in"), 16)
            act.dma_start(h[:, 0, :], a["x"][:, 0, :]).then_inc(S("x_in0"), 16)
            act.dma_start(mats[:], a["mats"]).then_inc(S("mats_in"), 16)
            for m in range(2, KT, 2):
                act.dma_start(h[:, m, :], a["x"][:, m, :]).then_inc(S(f"x_in{m}"), 16)
            act.dma_start(small[:], a["small"]).then_inc(S("small_in"), 16)
            act.dma_start(table1[:], a["table1"]).then_inc(S("table1_in"), 16)
            act.dma_start(rot1[:], a["rot1"]).then_inc(S("table1_in"), 16)
            act.dma_start(masks1[:], a["masks1"]).then_inc(S("masks1_in"), 16)

            def split_high(n, m, gain, norm, squares=None):
                if gain:
                    ahead(UH[:, m, :], h[:, m, :], ACT.Identity, "u_high", scale=col(gain, m))
                else:
                    ahead(UH[:, m, :], h[:, m, :], ACT.Copy, "u_high")
                if norm is not None:
                    ahead(squares[:, m, :], h[:, m, :], ACT.Square, "squared")

            def square(src, norm, m):
                added = KT * ADDED.index(norm) + m
                if added:
                    act.wait_ge(S("squares_summed"), added)
                f(sq[:], src, ACT.Square, "squared")

            def root(n):
                if n == 0:
                    act.wait_ge(S("small_in"), 16)
                f(roots[:, 0:NT], small[:, 4:4 + NT], ACT.Sqrt)
                act.wait_ge(S("norm_summed"), n + 1)
                f(roots[:, 0:NT], PS[:, 4:8, 0], ACT.Sqrt, "rooted", scale=1.0 / D, bias=small[:, 1:2])
                if n not in POST_NORMS:
                    act.wait_ge(S("rms_spread"), n + 1)
                    f(rstd[:], PS[:, 3, :], ACT.Copy, "rstd_ready")

            act.wait_ge(S("params_in"), 16)
            for m in range(KT):
                act.wait_ge(S(f"x_in{m}"), 16)
                split_high(0, m, "mix_pre", 0, aq)
            root(0)

            for i in range(16 + 2):
                if i < 16:
                    p = 4 * (i % 2)
                    act.wait_ge(S("neg_max"), i + 1)
                    f(sp1[i % 2][:], sp1[i % 2][:], ACT.Exp, "exp1", scale=0.125, bias=st[:, p + 1:p + 2],
                      accum_out=st[:, p + 2:p + 3])
                if 1 <= i < 17:
                    act.wait_ge(S("probs_turned"), i)
                    if i >= 3:
                        act.wait_ge(S("o_done"), i - 2)
                    f(pt1[(i - 1) % 2][:], flat(PS[:, 4:6, :])[:, 0:768], ACT.Copy, "probs_copied")
                if i >= 2:
                    r, n = (i - 2) // 4, (i - 2) % 4
                    row = slice(64 * (n % 2), 64 * (n % 2) + 64)
                    act.wait_ge(S("o_done"), i - 1)
                    f(oA[row, n // 2, r::4], PS[row, 6 + i % 2, 0:P], ACT.Copy, "o_copied")
                if 2 <= i < N_RWKV:
                    act.wait_ge(*evicted(O_RWKV + i))
                    act.dma_start(z_dram[i], zs[i % 2][:]).then_inc(S(f"z_stored{i % 2}"), 16)
            for m in range(2):
                f(OH[:, m, :], oA[:, m, :], ACT.Copy, "o_high")
            act.wait_ge(S("o_low"), 2)

            for i in range(2):
                act.wait_ge(S(f"z_stored{i}"), 16 * (N_RWKV // 2 - 1))

            def load_z(j, b):
                act.dma_start(zp[b][:, 1:T + 1], z_dram[j]).then_inc(S(f"z_in{b}"), 16)

            def load_rkv(hp):
                for b in range(3):
                    if hp:
                        act.wait_ge(S("shifted"), 3 * hp + {1: (1, 0, 2)}.get(hp, (2, 1, 0))[b])
                    load_z(2 + 3 * hp + b, b)

            load_rkv(0)
            act.dma_start(lora_w[0:32, :], a["w2"]).then_inc(S("scan_consts_in"), 16)
            act.dma_start(lora_w[32:64, :], a["a2"]).then_inc(S("scan_consts_in"), 16)
            act.dma_start(lora_g[0:96, :], a["g2"]).then_inc(S("scan_consts_in"), 16)
            act.dma_start(smask[:], a["scan_masks"]).then_inc(S("scan_consts_in"), 16)

            stored = [0]

            def store_gates(n):
                for j in range(stored[0], n):
                    act.wait_ge(*evicted(O_GATE + j))
                    act.dma_start(gate_dram[j], gs[j % 2][:]).then_inc(S(f"gate_stored{j % 2}"), 16)
                stored[0] = n

            def key_root(hp):
                act.wait_ge(S("kk_raw"), hp + 1)
                f(sq[:], kk, ACT.Square, "k_squared")
                act.wait_ge(S("k_summed"), hp + 1)
                f(sq[:], PS[:, 2, :], ACT.Sqrt, "k_root")

            def lora_sigmoids(hp):
                act.wait_ge(S("lora_done"), 3 * hp + 1)
                f(wsum, PS[:, 4, :], ACT.Sigmoid, "lora_used", bias=col("w0", hp))
                act.wait_ge(S("lora_done"), 3 * hp + 2)
                f(aa, PS[:, 5, :], ACT.Sigmoid, "lora_used", bias=col("a0", hp))

            def decays(hp):
                act.wait_ge(S("decay_summed"), hp + 1)
                c = float(np.exp(-0.5))
                f(PP[:, :, 1:65], ip.rearrange("p (c t) -> p c t", c=8), ACT.Exp, "decayed", scale=-c)
                f(ip, ip, ACT.Exp, "decayed", scale=c)
                f(scrap[:, 0:1], small[:, 1:2], ACT.Sqrt)

            def split_output(hp):
                act.wait_ge(S("y_final"), hp + 1)
                f(YH[:, hp, :], tmp[1][:], ACT.Copy, "y_high")

            def output_gate(hp):
                act.wait_ge(S("lora_done"), 3 * hp + 3)
                f(next_gate if hp else gt[:], PS[:, 7, :], ACT.Copy, "lora_used")

            act.wait_ge(S("shifted"), 1)
            f(la[0:32, :], la[0:32, :], ACT.Tanh, "lora_in")
            act.wait_ge(S("shifted"), 2)
            f(lg[0:96, :], lg[0:96, :], ACT.Sigmoid, "lora_in")
            WU = Z[:].rearrange("p w (t n) -> p w t n", t=NT)
            lora_sigmoids(0)
            key_root(0)
            decays(0)
            output_gate(0)
            store_gates(FILL_AHEAD // KT)
            for hp in range(4):
                act.wait_ge(S("turned"), 4 * hp + 1)
                for e in range(2):
                    f(RHS[:, e, :, 0:64], blk(PS[:, 2, :])[:, :, 64 * e:64 * e + 64], ACT.Copy, "token_a")
                act.wait_ge(S("turned"), 4 * hp + 2)
                f(Bt[:], blk(PS[:, 3, :]), ACT.Copy, "token_a")
                if hp:
                    output_gate(hp)
                    store_gates(gates_done(hp - 1, "var"))
                if hp < 3:
                    load_rkv(hp + 1)
                if hp:
                    split_output(hp - 1)
                    act.wait_ge(S("bonus_ready"), hp + 1)
                    f(acc[:], next_bonus, ACT.Copy, "carried")
                    f(gt[:], next_gate, ACT.Copy, "carried")
                for e in range(2):
                    act.wait_ge(S("mv_done"), 2 * hp + e + 1)
                    f(RHS[:, e, :, 64:128], PS[:, 2 + e, 0:256].rearrange("p (t n) -> p t n", t=NT), ACT.Copy,
                      "mv_copied")
                for e in range(2):
                    act.wait_ge(S("wu_done"), 2 * hp + e + 1)
                    for w in range(2):
                        f(WU[:, w, :, 64 * e:64 * e + 64], blk(PS[:, 4 + e, :])[:, :, 64 * w:64 * w + 64], ACT.Copy,
                          "wu_copied")
                if hp < 3:
                    key_root(hp + 1)
                act.wait_ge(S("qy_done"), hp + 1)
                f(FK[:], PS[:, 7, :], ACT.Copy, "y0_ready")
                store_gates(gates_done(hp, "wu"))
                store_gates(gates_done(hp, "chunks"))
                if hp < 3:
                    lora_sigmoids(hp + 1)
                    decays(hp + 1)
                if hp == 3:
                    act.wait_ge(S("pairs_masked"), 24)
                    act.dma_start(pf[:], a["p"]).then_inc(S("p_in"), 16)
                    f(scrap[:, 0:1], small[:, 1:2], ACT.Sqrt)
                    act.wait_ge(S("p_in"), 16)
                    for m in range(2):
                        f(PH[:, m, :], pf[:, m, :], ACT.Copy, "p_high")
                act.wait_ge(S("y_centered"), hp + 1)
                f(sq[:], tmp[0][:], ACT.Square, "y_squared")
                act.wait_ge(S("var_done"), hp + 1)
                f(sq[:], PS[:, 4, :], ACT.Sqrt, "y_root", bias=small[:, 2:3])
                store_gates(gates_done(hp, "states"))
            split_output(3)

            def load_gates(m):
                if m >= 2:
                    act.wait_ge(S("merged_low"), m - 1)
                for j in range(2):
                    b = 2 * (m % 2) + j
                    act.dma_start(gin[b][:], gate_dram[2 * m + j]).then_inc(S(f"gate_in{b}"), 16)

            def squash_gates(m):
                for j in range(2):
                    b = 2 * (m % 2) + j
                    act.wait_ge(S(f"gate_in{b}"), 16 * (m // 2 + 1))
                    f(gin[b][:], gin[b][:], ACT.Sigmoid, "gate_ready")

            load_gates(0)
            load_gates(1)
            f(roots[:, 0:1], small[:, 1:2], ACT.Sigmoid)
            store_gates(2 * KT)
            squash_gates(0)
            for i in range(2):
                act.wait_ge(S(f"gate_stored{i}"), 16 * KT)
            for m in range(KT):
                act.wait_ge(S("units_done"), U_UP + m + 1)
                f(ple[:, m, :], PS[:, 4 + 3 * (m % 2), :], ACT.Copy, "ple_copied")
                act.wait_ge(S("merged"), m + 1)
                f(MH[:, m, :], gin[2 * (m % 2)][:], ACT.Copy, "merged_high")
                if m + 1 < KT:
                    squash_gates(m + 1)
                if m + 2 < KT:
                    load_gates(m + 2)
            for m in range(KT):
                act.wait_ge(S("units_done"), U_OUT + m + 1)
                square(PS[:, (O_OUT + m) % 2, :], 1, m)
                f(t8[:, m, :], PS[:, (O_OUT + m) % 2, :], ACT.Copy, lane.leaves(O_OUT + m))
            root(1)

            def feed_forward(U, O, high, hid, dst, norm):
                highs = high[:].rearrange("p (g j) t -> p g j t", j=4)
                outs = dst[:].rearrange("p (g j) t -> p g j t", j=2)
                for half in range(2):
                    o = O + 24 * half
                    with lane.loop(4, {"chain": 4, "hidden_high": 4}) as g:
                        for j in range(4):
                            act.wait_ge(S(f"out_evicted{(o + j) % 2}"), g * 2 + ((o + j) // 2 + 1))
                            f(tmp[j % 2][:], tmp[j % 2][:], ACT.Square)
                            f(highs[:, g, j, :], tmp[j % 2][:], ACT.Copy, "hidden_high")
                o += 16
                with lane.loop(4, {"squared": 2}) as g:
                    for j in range(2):
                        act.wait_ge(S(f"out_evicted{(o + j) % 2}"), g + ((o + j) // 2 + 1))
                        act.wait_ge(S("squares_summed"), g * 2 + (KT * ADDED.index(norm) + j))
                        f(sq[:], outs[:, g, j, :], ACT.Square, "squared")
                root(norm)

            def updated(n, m):
                act.wait_ge(S("h_new"), KT * n + m + 1)

            for m in range(KT):
                updated(0, m)
                split_high(1, m, "ffn_pre", 2, t8)
            root(2)
            feed_forward(U_FFN, O_FFN, FH, 0, t8, 3)

            act.dma_start(pos[:], a["positions"].to_broadcast([P, T])).then_inc(S("block2_in"), 16)
            act.dma_start(rot2[:], a["rot2"]).then_inc(S("block2_in"), 16)
            act.dma_start(causal[:], a["causal"]).then_inc(S("block2_in"), 16)
            for j in range(4):
                act.dma_start(lam4[:, j, :], a[f"lam{j}"].to_broadcast([P, HD])).then_inc(S("block2_in"), 16)
            for m in range(KT):
                updated(1, m)
                split_high(2, m, None, None)
            plev = ple[:].rearrange("p (g j) t -> p g j t", j=4)
            t8v = t8[:].rearrange("p (g j) t -> p g j t", j=4)
            with lane.loop(2, {"out_evicted0": 2, "out_evicted1": 2, "squared": 4}) as g:
                for j in range(4):
                    act.wait_ge(S("units_done"), g * 4 + (U_PLE + j + 1))
                    f(tmp[j % 2][:], PS[:, j % 2, :], ACT.Sigmoid, lane.leaves(O_PLE + j))
                    act.wait_ge(S("e_new"), g * 4 + (j + 1))
                    act.wait_ge(S("squares_summed"), g * 4 + (KT * ADDED.index(4) + j))
                    f(sq[:], t8v[:, g, j, :], ACT.Square, "squared")
            root(4)

            for m in range(KT):
                updated(2, m)
                split_high(3, m, "attn2", 5, t8)
            root(5)
            act.wait_ge(S("angles"), 2)
            f(table2[:, T:2 * T], table2[:, T:2 * T], ACT.Sin, "table2")
            f(table2[:, 0:T], table2[:, 0:T], ACT.Sin, "table2")
            act.wait_ge(S("lam_dots"), 2)
            f(lamw[:, 2:4], lamw[:, 0:2], ACT.Exp, "lam_exp")

            def head_root(n):
                act.wait_ge(S("a_summed"), n + 1)
                f(roots[:, 0:NT], PS[:, 7, 0:NT], ACT.Sqrt, "a_root", scale=1.0 / P, bias=small[:, 1:2])

            for i in range(32 + 2):
                if i in POOL_SPLIT_STEPS:
                    j = POOL_SPLIT_STEPS.index(i)
                    act.wait_ge(S("pool_diff"), j + 1)
                    f(DH[:, j, :], pz[:, 16:16 + T], ACT.Copy, "pool_high")
                if i < 32:
                    p, n = i % 2, P * (i % 4 + 1)
                    act.wait_ge(S("neg_max2"), i + 1)
                    for c in range(2):
                        f(e2[p][:, c, 0:n], e2[p][:, c, 0:n], ACT.Exp, "exp2", scale=0.125,
                          bias=st2[:, p, 2 + c:3 + c], accum_out=st2[:, p, 4 + c:5 + c])
                if i == POOLW_STEP:
                    for m in range(KT):
                        if m < KT - 1:
                            act.wait_ge(S("pool_done"), m + 1)
                        else:
                            act.wait_ge(S("units_done"), U_STEP + POOLW_STEP + 1)
                        f(poolT[:, m, :], PS[:, m % 2, :], ACT.Identity, "pool_copied", scale=col("pool_scale", m))
                if 1 <= i < 33 and step_unit(i - 1)[0][0] == "gate":
                    (_, g), o = step_unit(i - 1)
                    act.wait_ge(*evicted(o))
                    f(gates2[:, g, :], gates2[:, g, :], ACT.Sigmoid, "gated")
                if 1 <= i < 33:
                    n = P * ((i - 1) % 4 + 1)
                    act.wait_ge(S("weights_turned"), i)
                    if i >= 3:
                        act.wait_ge(S("a_done"), i - 2)
                    f(pt2[(i - 1) % 2][:, 0:n], PS[:, 3, 0:n], ACT.Copy, "weights_copied")
                if i >= 2 and i % 4 == 1:
                    n = (i - 2) // 4
                    act.wait_ge(S("a_done"), 4 * n + 4)
                    f(aT[:, n, :], PS[:, 6, :], ACT.Copy, "a_copied")
                    f(sq[:], aT[:, n, :], ACT.Square, "a_squared")
                if i >= 6 and i % 4 == 2:
                    head_root((i - 6) // 4)
                    f(lamw[:, 7:8], small[:, 0:1], ACT.Exp)
            head_root(7)
            def squash_late_gates(m):
                for j in range(2):
                    act.wait_ge(*evicted(O_GATE2 + 2 * m + j - N_EARLY))
                    f(late_gates(m)[j], late_gates(m)[j], ACT.Sigmoid, "gated")

            squash_late_gates(3)
            for n, m in enumerate(MERGE_ORDER):
                if n % 2 == 0:
                    squash_late_gates(4 + n // 2)
                act.wait_ge(S("merged"), KT + n + 1)
                f(M2H[:, m, :], gates2[:, 2 * m, :] if 2 * m < N_EARLY else late_gates(m)[0], ACT.Copy, "merged_high")
            for m in range(KT):
                act.wait_ge(*evicted(O_OUT2 + m))
                split_high(4, m, "mlp2", 6, aT)
            root(6)
            feed_forward(U_FFN2, O_FFN2, F2H, 32, h, 7)
            for m in range(KT):
                act.wait_ge(S("final"), m + 1)
                act.dma_start(a["out"][:, m, :], h[:, m, :]).then_inc(S("stored"), 16)

        @block.vector
        def _(dve):
            lane = Lane(dve, S, "dve")

            def tt(out, x, y, op, name="chain"):
                lane.do(nc.vector.tensor_tensor(out, x, y, op), name)

            def ts(out, x, s1, op1, name="chain", s2=None, op2=ALU.bypass):
                if s2 is None:
                    lane.do(nc.vector.tensor_scalar(out, x, s1, None, op1), name)
                else:
                    lane.do(nc.vector.tensor_scalar(out, x, s1, s2, op1, op2), name)

            def stt(out, x, s, y, op1, op2, name="chain"):
                lane.do(nc.vector.scalar_tensor_tensor(out=out, in0=x, scalar=s, in1=y, op0=op1, op1=op2), name)

            def copy(out, x, name="chain"):
                lane.do(nc.vector.tensor_copy(out, x), name)

            def recip(out, x):
                lane.do(nc.vector.reciprocal(out, x))

            MUL, ADD, SUB = ALU.mult, ALU.add, ALU.subtract

            def split_low(n, m, gain):
                dve.wait_ge(S("u_high"), KT * n + m + 1)
                if gain:
                    lane.ahead(nc.vector.scalar_tensor_tensor(
                        out=UL[:, m, :], in0=h[:, m, :], scalar=col(gain, m), in1=UH[:, m, :].bitcast(F32),
                        op0=MUL, op1=SUB), "u_low")
                else:
                    lane.ahead(nc.vector.tensor_tensor(UL[:, m, :], h[:, m, :], UH[:, m, :].bitcast(F32), SUB),
                               "u_low")

            def add_squares(norm, m, src):
                dve.wait_ge(S("squared"), KT * norm + m + 1)
                if m == 0:
                    copy(acc[:], src, "squares_summed")
                else:
                    tt(acc[:], acc[:], src, ADD, "squares_summed")

            def norm_scale(n):
                dve.wait_ge(S("rooted"), n + 1)
                recip(roots[:, NT:2 * NT], roots[:, 0:NT])
                tt(blk(acc[:]), over(M["ident"]), roots[:, NT:2 * NT].unsqueeze(2).to_broadcast([P, NT, P]), MUL,
                   "diag_ready")
                if n in POST_NORMS:
                    dve.wait_ge(S("rms_spread"), n + 1)
                else:
                    dve.wait_ge(S("rstd_ready"), {0: 1, 2: 2, 5: 3, 6: 4}[n])

            def evict(o, u, dst):
                dve.wait_ge(S("units_done"), u + 1)
                tt(dst, PS[:, o % 2, :], rstd[:], MUL, lane.leaves(o))

            for m in range(KT):
                split_low(0, m, "mix_pre")
                add_squares(0, m, aq[:, m, :])
            norm_scale(0)

            def finish_qkv(o):
                if o < 12:
                    tt(rt[:], tmp[o % 2][:], table1[:, 0:T], MUL)
                    dve.wait_ge(S("rotated"), o + 1)
                    tt(tmp[o % 2][:], PS[:, 2 + o % 2, :], table1[:, T:2 * T], MUL)
                    tt(aq[:, o, :], rt[:], tmp[o % 2][:], ADD, "roped")
                else:
                    i = o - 12
                    dve.wait_ge(S("v_turned"), i + 1)
                    copy(av[:, :, i // 2, (i % 2) * P:(i % 2 + 1) * P], blk(PS[:, 4 + o % 2, :]), "v_token")

            dve.wait_ge(S("table1_in"), 32)
            for o in range(N_QKV):
                evict(O_QKV + o, U_QKV + o, tmp[o % 2][:])
                if o:
                    finish_qkv(o - 1)
            finish_qkv(N_QKV - 1)

            dve.wait_ge(S("masks1_in"), 16)
            for i in range(16 + 1):
                if i < 16:
                    r, p = i // 4, 4 * (i % 2)
                    dve.wait_ge(S("scores"), i + 1)
                    if i >= 2:
                        dve.wait_ge(S("probs_turned"), i - 1)
                    b = 2
                    lane.do(nc.vector.tensor_tensor_reduce(
                        out=sp1[i % 2][:], in0=flat(PS[:, b:b + 2, :])[:, 0:768],
                        in1=masks1[:, r * 768:(r + 1) * 768], scale=1.0, scalar=NEG, op0=ADD, op1=ALU.max,
                        accum_out=st[:, p:p + 1]), "masked")
                    ts(st[:, p + 1:p + 2], st[:, p:p + 1], -0.125, MUL, "neg_max")
                if i >= 1:
                    p = 4 * ((i - 1) % 2)
                    dve.wait_ge(S("exp1"), i)
                    recip(st[:, p + 3:p + 4], st[:, p + 2:p + 3])
                    ts(sp1[(i - 1) % 2][:], sp1[(i - 1) % 2][:], st[:, p + 3:p + 4], MUL, "probs")
                if i < N_RWKV:
                    if i >= 4:
                        dve.wait_ge(S(f"z_stored{i % 2}"), 16 * (i // 2 - 1))
                    evict(O_RWKV + i, U_LORA + i, (sq, acc)[i][:] if i < 2 else zs[i % 2][:])
            for m in range(2):
                dve.wait_ge(S("o_high"), m + 1)
                tt(OL[:, m, :], oA[:, m, :], OH[:, m, :].bitcast(F32), SUB, "o_low")

            for z in zp:
                lane.do(nc.vector.memset(z[:, 0:1], 0.0))
            lane.do(nc.vector.memset(PP[:, :, 0:1], 1.0))
            lane.do(nc.vector.memset(restart[:], 1.0))
            lane.do(nc.vector.memset(restart[:, :, 0:1], 0.0))
            ts(omka[:], par[:, PARAM_COLS["k_a"]:PARAM_COLS["k_a"] + 4], -1.0, MUL, s2=1.0, op2=ADD)

            def shift(b, j, out, n):
                dve.wait_ge(S(f"z_in{b}"), 16 * n)
                tt(tmp[0][:], zp[b][:, 0:T], zp[b][:, 1:T + 1], SUB)
                stt(out, tmp[0][:], col("mu", j), zp[b][:, 1:T + 1], MUL, ADD, "shifted")

            taken = [0]

            def take_gates(n):
                for j in range(taken[0], n):
                    if j >= 2:
                        dve.wait_ge(S(f"gate_stored{j % 2}"), 16 * (j // 2))
                    evict(O_GATE + j, U_GATE + j, gs[j % 2][:])
                taken[0] = n

            take_gates(1)
            for z, j, out in ((sq, 12, la), (acc, 13, lg)):
                ts(tmp[0][:, 0:1], z[:, 0:1], -1.0, MUL)
                tt(tmp[0][:, 1:T], z[:, 0:T - 1], z[:, 1:T], SUB)
                stt(out[:], tmp[0][:], col("mu", j), z[:], MUL, ADD, "shifted")

            def ch(x):
                return x.rearrange("p (c t) -> p c t", c=8)

            def rkv(hp):
                shift(1, 4 + hp, ks, hp + 1)
                if hp:
                    dve.wait_ge(S("wu_done"), 2 * hp)
                ts(kk, ks, col("k_k", hp), MUL, "kk_raw")
                shift(0, hp, rs, hp + 1)

            def sum_decay(hp):
                dve.wait_ge(S("lora_used"), 3 * hp + 1)
                lane.do(nc.vector.tensor_tensor_scan(
                    ip, flat(restart[:]), wsum, 0.0, MUL, ADD), "decay_summed")

            def adjust_k(hp):
                dve.wait_ge(S("lora_used"), 3 * hp + 2)
                ts(tmp[0][:], aa, col("k_a", hp), MUL, s2=omka[:, hp:hp + 1], op2=ADD)
                tt(ks, ks, tmp[0][:], MUL)

            def weigh_rk(hp):
                stt(tmp[1][:], rs, col("r_k", hp), ks, MUL, MUL, "rk_ready")

            def normalize_k(hp):
                dve.wait_ge(S("k_root"), hp + 1)
                ts(sq[:], sq[:], 1e-12, ALU.max)
                recip(sq[:], sq[:])
                tt(kk, kk, sq[:], MUL)

            def scale_a(hp):
                dve.wait_ge(S("decayed"), 2 * hp + 2)
                stt(ch(FA[:]), ch(kk), -1.0, PP[:, :, 0:64], MUL, MUL, "scaled")

            def scale_b():
                tt(aa, kk, aa, MUL)
                tt(FB[:], aa, ip, MUL, "scaled")

            def scale_r():
                tt(ch(FR[:]), ch(rs), PP[:, :, 1:65], MUL, "scaled")
                copy(ends[:], PP[:, :, 64])

            def scale_k():
                tt(FK[:], ks, ip, MUL, "scaled")

            def bonuses(hp):
                dve.wait_ge(S("rk_summed"), hp + 1)
                tt(next_bonus if hp else bonus[:], PS[:, 6, :], vs[:], MUL, "bonus_ready")

            def finish_part(hp, part):
                if part < 4:
                    if part == 0:
                        dve.wait_ge(S("y_root"), hp + 1)
                    recip(sq[:, part * P:(part + 1) * P], sq[:, part * P:(part + 1) * P])
                elif part == 4:
                    tt(tmp[0][:], tmp[0][:], sq[:], MUL)
                elif part == 5:
                    ts(tmp[0][:], tmp[0][:], col("ln_w", hp), MUL, s2=col("ln_b", hp), op2=ADD)
                elif part == 6:
                    if hp:
                        dve.wait_ge(S("carried"), 2 * hp)
                    tt(tmp[0][:], tmp[0][:], bonus[:], ADD)
                elif part == 7:
                    tt(tmp[1][:], tmp[0][:], gt[:], MUL, "y_final")
                elif part == 8:
                    dve.wait_ge(S("y_high"), hp + 1)
                    tt(YL[:, hp, :], tmp[1][:], YH[:, hp, :].bitcast(F32), SUB, "rwkv_out")

            rkv(0)
            shift(2, 8, vs[:], 1)
            take_gates(2)
            sum_decay(0)
            adjust_k(0)
            weigh_rk(0)
            normalize_k(0)
            scale_a(0)
            scale_b()
            scale_k()
            scale_r()
            bonuses(0)
            take_gates(FILL_AHEAD // KT)
            for hp in range(4):
                dve.wait_ge(S("turned"), 4 * hp + 3)
                copy(Vt[:], blk(PS[:, 5, :]), "token_d")
                dve.wait_ge(S("turned"), 4 * hp + 4)
                copy(Kt[:], blk(PS[:, 4, :]), "token_d")
                if hp:
                    bonuses(hp)
                    take_gates(gates_done(hp - 1, "var"))
                for e in range(2):
                    dve.wait_ge(S("lower_done"), 2 * hp + e + 1)
                    lane.ahead(nc.vector.tensor_tensor(
                        blk(X[:, e, :]), blk(PS[:, 2 + 2 * e, :]), over(K_["pair_lower"]), MUL), "lower_masked")
                for e in range(2):
                    x, y, lt = blk(X[:, e, :]), blk(Y[:, e, :]), blk(Lt[:, e, :])
                    dve.wait_ge(S("lower_masked"), 2 * hp + e + 1)
                    lane.ahead(nc.vector.tensor_tensor(x, x, over(M["ident"]), ADD), "x_started")
                    dve.wait_ge(S("upper_done"), 2 * hp + e + 1)
                    tt(lt, blk(PS[:, 3 + 2 * e, :]), over(K_["before"]), MUL)
                    tt(y, lt, over(K_["pair_upper"]), MUL)
                    lane.ahead(nc.vector.tensor_tensor(y, y, over(M["ident"]), ADD), "inverse_ready")
                for l in range(1, 6):
                    for e in range(2):
                        dve.wait_ge(S("lx_done"), 10 * hp + 2 * (l - 1) + e + 1)
                        lane.ahead(nc.vector.tensor_tensor(
                            blk(Z[:, e, :]), blk(PS[:, 6 + e, :]), over(K_[f"lvl{l}"]), MUL), "lx_masked")
                    for e in range(2):
                        if hp:
                            finish_part(hp - 1, 2 * (l - 1) + e)
                        dve.wait_ge(S("xlx_done"), 10 * hp + 2 * (l - 1) + e + 1)
                        if l < 5:
                            x = half_columns(X[:, e, :], l, 0)
                            lane.ahead(nc.vector.tensor_tensor(x, x, half_columns(PS[:, 2 + e, :], l, 0), ADD),
                                       "x_added")
                        y = half_columns(Y[:, e, :], l, 1)
                        lane.ahead(nc.vector.tensor_tensor(y, y, half_columns(PS[:, 4 + e, :], l, 1), ADD),
                                   "inverse_ready")
                for n, (dst, mask) in enumerate((((Lt[:, 0, :], Lt[:, 1, :]), "before"),
                                                 ((X[:, 0, :], X[:, 1, :]), "upto"), ((FA[:], FB[:]), "upto"))):
                    for e in range(2):
                        dve.wait_ge(S("pairs_done"), 6 * hp + 2 * n + e + 1)
                        tt(blk(dst[e]), blk(PS[:, 2 + 2 * n + e, :]), over(K_[mask]), MUL, "pairs_masked")
                if hp < 3:
                    shift(2, 8 + hp + 1, vs[:], hp + 2)
                    dve.wait_ge(S("mv_done"), 2 * hp + 2)
                    rkv(hp + 1)
                    normalize_k(hp + 1)
                take_gates(gates_done(hp, "wu"))
                dve.wait_ge(S("qy_done"), hp + 1)
                tt(FR[:], FR[:], PS[:, 6, :], ADD, "q_ready")
                if hp:
                    dve.wait_ge(S("carried"), 2 * hp)
                dve.wait_ge(S("chunks_done"), hp + 1)
                for lo, src in ((1, blk(PS[:, 2, :])[:, 1:4, :]), (0, blk(PS[:, 3, :])[:, 0:3, :])):
                    lane.ahead(nc.vector.tensor_tensor(G[:, lo:lo + 5:2, :], src, over(M["head_ones"], 3), MUL),
                               "transition_masked")
                for n, lo in enumerate((1, 0)):
                    dve.wait_ge(S("transition_masked"), 2 * hp + n + 1)
                    g = G[:, lo:lo + 5:2, :]
                    lane.ahead(nc.vector.tensor_tensor(g, g, over(M["ident"], 3), ADD), "chunks_ready")
                for c in range(7):
                    lane.ahead(nc.vector.scalar_tensor_tensor(
                        out=H[:, c, :], in0=PS[:, 4 + c % 2, (c // 2) * P:(c // 2 + 1) * P],
                        scalar=ends[:, c:c + 1], in1=M["head_ones"], op0=MUL, op1=MUL), "chunks_ready")
                dve.wait_ge(S("chunks_ready"), 9 * (hp + 1))
                take_gates(gates_done(hp, "chunks"))
                for c in range(1, 7):
                    dve.wait_ge(S("state_done"), 6 * hp + c)
                    stt(St[:, c - 1, :], PS[:, 6 + c % 2, 0:P], ends[:, c:c + 1], H[:, c, :], MUL, ADD, "state_ready")
                    if hp < 3 and c == 3:
                        sum_decay(hp + 1)
                    elif hp < 3 and c == 4:
                        adjust_k(hp + 1)
                    elif hp < 3 and c == 5:
                        weigh_rk(hp + 1)
                if hp < 3:
                    scale_a(hp + 1)
                dve.wait_ge(S("y_done"), hp + 1)
                dve.wait_ge(S("y0_ready"), hp + 1)
                tt(FK[:, 64:T], FK[:, 64:T], PS[:, 2, 64:T], ADD, "y_ready")
                if hp < 3:
                    scale_b()
                if hp == 3:
                    for m in range(2):
                        dve.wait_ge(S("p_high"), m + 1)
                        tt(PL[:, m, :], pf[:, m, :], PH[:, m, :].bitcast(F32), SUB, "p_low")
                dve.wait_ge(S("mean_done"), hp + 1)
                tt(tmp[0][:], FK[:], PS[:, 5, :], SUB, "y_centered")
                if hp < 3:
                    scale_k()
                    scale_r()
                take_gates(gates_done(hp, "states"))
            for part in range(9):
                finish_part(3, part)
            take_gates(gates_done(3, "var"))

            def merge(m, before, x, y, first, second, high, low):
                tt(x, x, first, MUL)
                tt(y, y, second, MUL)
                tt(x, x, y, ADD, "merged")
                dve.wait_ge(S("merged_high"), before + 1)
                tt(low[:, m, :], x, high[:, m, :].bitcast(F32), SUB, "merged_low")

            for m in range(KT):
                b, g = 2 + 3 * (m % 2), 2 * (m % 2)
                dve.wait_ge(S("gate_ready"), 2 * m + 2)
                dve.wait_ge(S("units_done"), U_UP + m + 1)
                merge(m, m, gin[g][:], gin[g + 1][:], PS[:, b, :], PS[:, b + 1, :], MH, ML)
            for m in range(KT):
                add_squares(1, m, sq[:])
            norm_scale(1)

            def update_all(post, n, gain, norm):
                for m in range(KT + 2):
                    if m < KT:
                        lane.ahead(nc.vector.scalar_tensor_tensor(
                            out=t8[:, m, :], in0=t8[:, m, :], scalar=col(post, m), in1=PS[:, 3, :],
                            op0=MUL, op1=MUL), "branch_scaled")
                    if m >= 2:
                        split_low(n, m - 2, gain)
                if norm is not None:
                    norm_scale(norm)

            def feed_forward(U, O, low, high, dst, hid, norm, add_first):
                lows = low[:].rearrange("p (g j) t -> p g j t", j=4)
                highs = high[:].rearrange("p (g j) t -> p g j t", j=4)
                outs = dst[:].rearrange("p (g j) t -> p g j t", j=2)
                for half in range(2):
                    u, o = U + 32 * half, O + 24 * half
                    with lane.loop(4, {"out_evicted0": 2, "out_evicted1": 2, "hidden_low": 4}) as g:
                        for j in range(4):
                            dve.wait_ge(S("units_done"), g * 4 + (u + j + 1))
                            stt(tmp[j % 2][:], PS[:, (o + j) % 2, :], 0.0, rstd[:], ALU.max, MUL,
                                lane.leaves(o + j))
                            dve.wait_ge(S("hidden_high"), g * 4 + (hid + 16 * half + j + 1))
                            tt(lows[:, g, j, :], tmp[j % 2][:], highs[:, g, j, :].bitcast(F32), SUB, "hidden_low")
                    u, o = u + 16, o + 16
                    if half:
                        lane.do(nc.vector.memset(acc[:], 0.0))
                    with lane.loop(4, {"out_evicted0": 1, "out_evicted1": 1} | ({"squares_summed": 2} if half else {})) as g:
                        for j in range(2):
                            dve.wait_ge(S("units_done"), g * 4 + (u + 2 * j + 2))
                            d = outs[:, g, j, :]
                            if half or add_first:
                                tt(d, d, PS[:, (o + j) % 2, :], ADD, lane.leaves(o + j))
                            else:
                                copy(d, PS[:, (o + j) % 2, :], lane.leaves(o + j))
                            if half:
                                dve.wait_ge(S("squared"), g * 2 + (KT * norm + j + 1))
                                tt(acc[:], acc[:], sq[:], ADD, "squares_summed")
                norm_scale(norm)

            update_all("mix_post", 1, "ffn_pre", 2)
            feed_forward(U_FFN, O_FFN, FL, FH, t8, 0, 3, False)
            update_all("ffn_post", 2, None, None)

            dve.wait_ge(S("block2_in"), 112)
            cosv, sinv = table2[:, 0:T], table2[:, T:2 * T]
            two_pi = 2 * np.pi
            c1 = 6.28125
            c2 = float(np.float32(np.floor((two_pi - c1) * 2 ** 20) / 2 ** 20))
            c3 = float(two_pi - c1 - c2)
            magic = 1.5 * 2 ** 23
            copy(cosv, pos[:])
            ts(cosv, cosv, small[:, 0:1], MUL)
            ts(rt2[:], cosv, float(1 / two_pi), MUL, s2=magic, op2=ADD)
            ts(rt2[:], rt2[:], -magic, ADD)
            for c in (c1, c2, c3):
                stt(cosv, rt2[:], -c, cosv, MUL, ADD)
            ts(sinv, cosv, 3.1415925, ALU.min, s2=-3.1415925, op2=ALU.max, name="angles")
            stt(cosv, sinv, -1.0, sinv, MUL, ALU.max)
            ts(cosv, cosv, -1.0, MUL, s2=float(np.pi / 2), op2=ADD, name="angles")
            for j in range(2):
                lane.do(nc.vector.tensor_tensor_reduce(
                    out=lam4[:, 2 * j, :], in0=lam4[:, 2 * j, :], in1=lam4[:, 2 * j + 1, :], scale=1.0, scalar=0.0,
                    op0=MUL, op1=ADD, accum_out=lamw[:, j:j + 1]), "lam_dots")

            plev = ple[:].rearrange("p (g j) t -> p g j t", j=4)
            t8v = t8[:].rearrange("p (g j) t -> p g j t", j=4)
            lane.do(nc.vector.memset(acc[:], 0.0))
            with lane.loop(2, {"e_new": 4, "squares_summed": 4}) as g:
                for j in range(4):
                    dve.wait_ge(S(f"out_evicted{j % 2}"), g * 2 + ((O_PLE + j) // 2 + 1))
                    tt(t8v[:, g, j, :], tmp[j % 2][:], plev[:, g, j, :], MUL, "e_new")
                    dve.wait_ge(S("squared"), g * 4 + (KT * 4 + j + 1))
                    tt(acc[:], acc[:], sq[:], ADD, "squares_summed")
            norm_scale(4)

            update_all("ple_post", 3, "attn2", 5)

            def head_diag(n):
                dve.wait_ge(S("a_root"), n + 1)
                recip(roots[:, NT:2 * NT], roots[:, 0:NT])
                tt(blk(acc[:]), over(M["ident"]), roots[:, NT:2 * NT].unsqueeze(2).to_broadcast([P, NT, P]), MUL,
                   "a_diag")

            def head_scale(n):
                dve.wait_ge(S("a_spread"), n + 1)
                stt(aT[:, n, :], aT[:, n, :], lamw[:, 6:7], PS[:, 7, :], MUL, MUL, "a_scaled")

            def finish_head(c, o):
                n = c // 3
                dve.wait_ge(S("head_turned"), c + 1)
                if c % 3 == 2:
                    copy(v2[n % 2][:], blk(PS[:, 2, :]), "head_input")
                else:
                    tt(rt2[:], tmp[o % 2][:], cosv, MUL)
                    tt(tmp[o % 2][:], PS[:, 2, :], sinv, MUL)
                    tt((q2, k2)[c % 3][n % 2][:], rt2[:], tmp[o % 2][:], ADD, "head_input")

            for z in (pz, pa, pb):
                lane.do(nc.vector.memset(z[:, 0:16], 0.0))

            def pool_windows(j, part):
                out = (pa, pb)[j % 2]
                for l in ((0, 1), (2, 3), ())[part]:
                    if l <= j:
                        cur, nxt = (pz if l == 0 else (pa, pb)[(l - 1) % 2]), (pa, pb)[l % 2]
                        tt(nxt[:, 16:16 + T], cur[:, 16:16 + T], cur[:, 16 - 2 ** l:16 - 2 ** l + T], ADD)
                if part == 2:
                    tt(out[:, 16:32], out[:, 16:32], small[:, 4 + 16 * j:20 + 16 * j], MUL)
                    ts(out[:, 32:16 + T], out[:, 32:16 + T], 1.0 / (2, 4, 8, 16)[j], MUL)
                    tt(pz[:, 16:16 + T], out[:, 16:16 + T], pz[:, 16:16 + T], SUB, "pool_diff")

            dve.wait_ge(S("table2"), 2)
            for o in range(3):
                evict(O_HEADS + o, U_HEADS + o, tmp[o % 2][:])
                finish_head(o, O_HEADS + o)
            dve.wait_ge(S("lam_exp"), 1)
            tt(lamw[:, 4:5], lamw[:, 2:3], lamw[:, 3:4], SUB)
            ts(lamw[:, 5:6], lamw[:, 4:5], LAM_INIT, ADD, s2=-1.0, op2=MUL)
            ts(lamw[:, 6:7], col("subln"), 1.0 - LAM_INIT, MUL)
            for i in range(32 + 2):
                n, qt = i // 4, i % 4
                if i in POOL_SPLIT_STEPS:
                    c = POOL_SPLIT_STEPS.index(i)
                    dve.wait_ge(S("pool_high"), c + 1)
                    tt(DL[:, c, :], pz[:, 16:16 + T], DH[:, c, :].bitcast(F32), SUB, "pooled_low")
                if i < 32:
                    p, w = i % 2, P * (qt + 1)
                    dve.wait_ge(S("scores2"), i + 1)
                    if i >= 2:
                        dve.wait_ge(S("weights_turned"), i - 1)
                    for c in range(2):
                        lane.do(nc.vector.tensor_tensor_reduce(
                            out=e2[p][:, c, 0:w], in0=PS[:, 4 + c, 0:w], in1=causal[:, T - w:T], scale=1.0,
                            scalar=NEG, op0=ADD, op1=ALU.max, accum_out=st2[:, p, c:c + 1]), "masked2")
                    ts(st2[:, p, 2:4], st2[:, p, 0:2], -0.125, MUL, "neg_max2")
                if 1 <= i < 33:
                    (kind, c), o = step_unit(i - 1)
                    if kind == "head":
                        finish_head(c, o)
                    p, w = (i - 1) % 2, P * ((i - 1) % 4 + 1)
                    dve.wait_ge(S("exp2"), 2 * i)
                    recip(st2[:, p, 6:8], st2[:, p, 4:6])
                    tt(st2[:, p, 7:8], st2[:, p, 7:8], lamw[:, 5:6], MUL)
                    ts(e2[p][:, 1, 0:w], e2[p][:, 1, 0:w], st2[:, p, 7:8], MUL)
                    stt(e2[p][:, 0, 0:w], e2[p][:, 0, 0:w], st2[:, p, 6:7], e2[p][:, 1, 0:w], MUL, ADD, "weights2")
                if i < 32:
                    (kind, c), o = step_unit(i)
                    if kind == "head":
                        evict(o, U_STEP + i, tmp[o % 2][:])
                    elif kind == "gate":
                        evict(o, U_STEP + i, gates2[:, c, :])
                    elif kind == "pool":
                        evict(o, U_STEP + i, pz[:, 16:16 + T])
                if 3 <= i < 3 + 16 and (i - 3) % 4 < 3:
                    pool_windows((i - 3) // 4, (i - 3) % 4)
                if i >= 6 and i % 4 == 2:
                    head_diag((i - 6) // 4)
                if i >= 7 and i % 4 == 3:
                    head_scale((i - 7) // 4)
            for g in range(2):
                evict(O_GATE2 + g, U_GATE2 + g, tmp[g][:])
            head_diag(7)
            head_scale(7)

            for n, m in enumerate(MERGE_ORDER):
                if n % 2 == 0:
                    for j in range(2):
                        g = 2 * (4 + n // 2) + j - N_EARLY
                        evict(O_GATE2 + g, U_GATE2 + g, late_gates(4 + n // 2)[j])
                x, y = (gates2[:, 2 * m, :], gates2[:, 2 * m + 1, :]) if 2 * m < N_EARLY else late_gates(m)
                dve.wait_ge(S("gated"), 2 * m + 2)
                merge(m, KT + n, x, y, aT[:, m, :], poolT[:, m, :], M2H, M2L)
            for m in range(KT):
                o = O_OUT2 + m
                dve.wait_ge(S("units_done"), U_OUT2 + m + 1)
                tt(h[:, m, :], h[:, m, :], PS[:, o % 2, :], ADD, lane.leaves(o))
                if m:
                    split_low(4, m - 1, "mlp2")
                    add_squares(6, m - 1, aT[:, m - 1, :])
            split_low(4, KT - 1, "mlp2")
            add_squares(6, KT - 1, aT[:, KT - 1, :])
            norm_scale(6)
            feed_forward(U_FFN2, O_FFN2, F2L, F2H, h, 32, 7, True)
            for m in range(KT):
                lane.ahead(nc.vector.scalar_tensor_tensor(
                    out=h[:, m, :], in0=h[:, m, :], scalar=col("final", m), in1=PS[:, 3, :], op0=MUL, op1=MUL),
                    "final")


def kernel(**inputs):
    import concourse.bacc as bacc
    from concourse.bass_utils import run_bass_kernel_spmd

    x = {k: np.asarray(v) for k, v in inputs.items()}
    w_in, w_in2 = x["w_in"][0], x["w_in_2"][0]

    def unit(w, c, n=P):
        w = w[:, c:c + n]
        if n < P:
            w = np.concatenate([w, np.zeros((D, P - n), w.dtype)], 1)
        return w.reshape(KT, P, P).transpose(1, 0, 2)

    units = [unit(w_in, P * j) for j in range(N_QKV)]
    rw = 9 * 256
    units += [unit(w_in, rw + 1536, 64), unit(w_in, rw + 1600, 96)]
    units += [unit(w_in, rw + 512 * j + P * hp) for hp in range(4) for j in range(3)]
    gate = rw + 1696
    units += [unit(w_in, gate + D * j + P * m) for m in range(KT) for j in range(2)]
    for m in range(KT):
        c = slice(P * m, P * (m + 1))
        units += [unit(np.concatenate([x["w_attn_up"][0][:, c], x["w_rwkv_up"][0][:, c], x["w_ple"][0][:, c]], 0), 0)]

    def feed_forward(w_up, w_down):
        for half in range(2):
            for j in range(16):
                yield unit(w_up, P * (16 * half + j))
            for m in range(KT):
                for w in range(2):
                    yield unit(w_down[2048 * half + 1024 * w:2048 * half + 1024 * (w + 1)], P * m)

    units += [unit(x["w_out"][0], P * m) for m in range(KT)]
    units += list(feed_forward(x["w_ff_in"][0], x["w_ff_out"][0]))
    units += [unit(x["w_ple_gate"][0], P * m) for m in range(KT)]
    gates2 = [unit(w_in2, 3584 + D * j + P * m) for m in range(KT) for j in range(2)]
    beside = {"head": [unit(w_in2, D * j + P * n) for n in range(8) for j in range(3)],
              "pool": [unit(w_in2, 3 * D + P * j) for j in range(4)],
              "pool_weights": [x["w_pool_2"][0].reshape(4, P, 2, P).transpose(1, 0, 2, 3).reshape(P, KT, P)],
              "gate": gates2}
    units += beside["head"][:3]
    for i in range(32):
        kind, c = step_unit(i)[0]
        units.append(beside[kind][c])
    units += gates2[N_EARLY:]
    units += [unit(x["w_out_2"][0], P * m) for m in range(KT)]
    units += list(feed_forward(x["w_up_2"][0], x["w_down_2"][0]))
    assert len(units) == N_UNITS

    mu = x["rwkv_mu"][0]
    mu = np.concatenate([mu[:1600], np.zeros(64, mu.dtype), mu[1600:], np.zeros(32, mu.dtype)])
    cols = {"mix_pre": "mix_pre_norm", "mix_post": "mix_post_norm", "ffn_pre": "ffn_pre_norm",
            "ffn_post": "ffn_post_norm", "ple_post": "ple_post_norm", "attn2": "norm_attn_g_2",
            "mlp2": "norm_mlp_g_2", "final": "final_norm_g_2", "pool_scale": "pool_scale_2", "w0": "rwkv_w0",
            "a0": "rwkv_a0", "k_k": "rwkv_k_k", "k_a": "rwkv_k_a", "r_k": "rwkv_r_k", "ln_w": "rwkv_ln_w",
            "ln_b": "rwkv_ln_b", "subln": "subln_g_2"}
    params = np.concatenate([(mu if n == "mu" else x[cols[n]]).reshape(-1, P).T for n in PARAM_COLS], 1)
    arrays = {
        "w": np.stack(units), "params": params,
        "x": x["x"][0].T.reshape(KT, P, T).transpose(1, 0, 2), "p": x["p"][0, 0].T.reshape(2, P, T).transpose(1, 0, 2),
        "w2": x["rwkv_w2"][0], "a2": x["rwkv_a2"][0], "g2": x["rwkv_g2"][0], "positions": x["positions_2"],
        "lam0": x["lam_q1_2"], "lam1": x["lam_k1_2"], "lam2": x["lam_q2_2"], "lam3": x["lam_k2_2"],
        **shape_constants(),
    }
    arrays = {k: np.ascontiguousarray(v) for k, v in arrays.items()}
    nc = bacc.Bacc("TRN2", target_bir_lowering=False, num_devices=1)
    aps = {k: nc.dram_tensor(f"in_{k}", v.shape, mybir.dt.from_np(v.dtype), kind="ExternalInput").ap()
           for k, v in arrays.items()}
    aps["out"] = nc.dram_tensor("out_0", (P, KT, T), F32, kind="ExternalOutput").ap()
    build(nc, aps)
    result = run_bass_kernel_spmd(nc, [{f"in_{k}": v for k, v in arrays.items()}], core_ids=[0])
    out = result.results[0]["out_0"]
    return out.transpose(1, 0, 2).reshape(D, T).T.reshape(1, T, D)
```
